# Optimizing a Trainium2 kernel written in Bass

```python
import jax, jax.numpy as jnp
from jax import lax
import numpy as np

D_MODEL = 1024
BATCH = 1
SEQ = 1024
DEPTH = 2

GRID_W = 64
CTX_LEN = 256
MIX_W = D_MODEL
N_MIXERS = 4
GROUP_W = MIX_W // N_MIXERS
HEAD_DIM = 64
N_HEADS = GROUP_W // HEAD_DIM
GLA_DK = HEAD_DIM // 2
GLA_QK_W = N_HEADS * GLA_DK
GLA_RANK = 16
GLA_NORMALIZER = 16.0
GLA_CHUNK = 64
MLSTM_CHUNK = 64
CONV_K = 3
SGU_CHUNK = 128
D_FF = 256 * ((8 * D_MODEL // 3 + 255) // 256)
N_EXPERTS = 8
TOP_K = 2
D_FF_EXPERT = 7 * D_MODEL // 2
N_DENSE = (DEPTH + 1) // 2
N_MOE = DEPTH // 2
EPS = 1e-6
IN_SPLITS = (GLA_QK_W, GLA_QK_W, GROUP_W, GROUP_W, 2 * GLA_RANK,
             GROUP_W, GROUP_W, GROUP_W, GROUP_W, 4 * N_HEADS,
             GROUP_W, GROUP_W,
             GROUP_W)
REC_W = 2 * GLA_QK_W + 2 * GROUP_W + 2 * GLA_RANK + 4 * GROUP_W + 4 * N_HEADS
D_IN = REC_W + 3 * GROUP_W
F32 = jnp.float32

kernel_name = 'hybrid_parallel_mixer_dit_block'

def rmsnorm(x, g):
    x32 = x.astype(F32)
    y = x32 * lax.rsqrt(jnp.mean(x32 * x32, axis=-1, keepdims=True) + EPS)
    return (y * g.astype(F32)).astype(x.dtype)

def modulate(xn, shift, scale):
    return xn * (1 + scale) + shift

def heads(x, dh):
    b, t, _ = x.shape
    return x.reshape(b, t, -1, dh).transpose(0, 2, 1, 3)

def merge_heads(x):
    b, h, t, d = x.shape
    return x.transpose(0, 2, 1, 3).reshape(b, t, h * d)

def flip_t(x):
    return jnp.flip(x, axis=2)

def split_cols(p):
    parts, o = [], 0
    for s in IN_SPLITS:
        if o >= p.shape[-1]:
            break
        parts.append(p[..., o:o + s])
        o += s
    return parts

def conv2d_grid(x, w, rows, cols):
    b, t, ch = x.shape
    y = lax.conv_general_dilated(x.reshape(b, rows, cols, ch), w[:, :, None, :].astype(x.dtype),
                                 window_strides=(1, 1), padding='SAME',
                                 dimension_numbers=('NHWC', 'HWIO', 'NHWC'), feature_group_count=ch)
    return y.reshape(b, t, ch)

def gla_scan(q, k, v, log_a, s0, with_output):
    b, h, t, dk = q.shape
    dv = v.shape[-1]
    n = t // GLA_CHUNK
    q, k, log_a = (a.reshape(b, h, n, GLA_CHUNK, dk) for a in (q, k, log_a))
    v = v.reshape(b, h, n, GLA_CHUNK, dv)
    cum = jnp.cumsum(log_a, axis=3)
    cum_last = cum[:, :, :, -1:, :]
    upd = jnp.einsum('bhnld,bhnlv->bhndv', k * jnp.exp(cum_last - cum), v)
    decay = jnp.exp(cum_last[:, :, :, 0, :])

    def step(s, inp):
        d, u = inp
        return d[..., None] * s + u, s

    s_fin, s_prev = lax.scan(step, s0, (jnp.moveaxis(decay, 2, 0), jnp.moveaxis(upd, 2, 0)))
    if not with_output:
        return None, s_fin
    s_prev = jnp.moveaxis(s_prev, 0, 2)
    q_dec = q * jnp.exp(cum)
    mask = jnp.tril(jnp.ones((GLA_CHUNK, GLA_CHUNK), dtype=bool))
    scores = jnp.where(mask, jnp.einsum('bhnld,bhnsd->bhnls', q_dec, k * jnp.exp(-cum)), 0.0)
    o = jnp.einsum('bhnls,bhnsv->bhnlv', scores, v) + jnp.einsum('bhnld,bhndv->bhnlv', q_dec, s_prev)
    return o.reshape(b, h, t, dv), s_fin

def mlstm_scan(q, k, v, ig, lf, state, with_output):
    b, h, t, dk = q.shape
    dv = v.shape[-1]
    n = t // MLSTM_CHUNK
    L = MLSTM_CHUNK
    q, k = (a.reshape(b, h, n, L, dk) for a in (q, k))
    v = v.reshape(b, h, n, L, dv)
    ig, lf = (a.reshape(b, h, n, L) for a in (ig, lf))
    cum = jnp.cumsum(lf, axis=3)
    cum_last = cum[..., -1]
    w_end = cum_last[..., None] - cum + ig
    m_chunk = jnp.max(w_end, axis=-1)
    w_k = jnp.exp(w_end - m_chunk[..., None])
    upd_c = jnp.einsum('bhnl,bhnld,bhnlv->bhndv', w_k, k, v)
    upd_n = jnp.einsum('bhnl,bhnld->bhnd', w_k, k)

    def step(carry, inp):
        c_st, n_st, m_st = carry
        fl, mc, uc, un = inp
        m_new = jnp.maximum(fl + m_st, mc)
        a = jnp.exp(fl + m_st - m_new)
        g = jnp.exp(mc - m_new)
        c_new = a[..., None, None] * c_st + g[..., None, None] * uc
        n_new = a[..., None] * n_st + g[..., None] * un
        return (c_new, n_new, m_new), (c_st, n_st, m_st)

    xs = tuple(jnp.moveaxis(a, 2, 0) for a in (cum_last, m_chunk, upd_c, upd_n))
    fin, prev = lax.scan(step, state, xs)
    if not with_output:
        return None, fin
    c_prev, n_prev, m_prev = (jnp.moveaxis(a, 0, 2) for a in prev)
    mask = jnp.tril(jnp.ones((L, L), dtype=bool))
    d_log = jnp.where(mask, cum[..., :, None] - cum[..., None, :] + ig[..., None, :], -jnp.inf)
    inter_log = cum + m_prev[..., None]
    m_row = jnp.maximum(inter_log, jnp.max(d_log, axis=-1))
    s = jnp.exp(d_log - m_row[..., None]) * jnp.einsum('bhnld,bhnsd->bhnls', q, k)
    w_int = jnp.exp(inter_log - m_row)
    num = jnp.einsum('bhnls,bhnsv->bhnlv', s, v) + w_int[..., None] * jnp.einsum('bhnld,bhndv->bhnlv', q, c_prev)
    den = jnp.sum(s, axis=-1) + w_int * jnp.einsum('bhnld,bhnd->bhnl', q, n_prev)
    out = num / jnp.maximum(jnp.abs(den), jnp.exp(-m_row))[..., None]
    return out.reshape(b, h, t, dv), fin

def gla_inputs(parts, w_lr, b_lr):
    b, t, _ = parts[0].shape
    q = heads(parts[0], GLA_DK) * GLA_DK ** -0.5
    k = heads(parts[1], GLA_DK)
    v = heads(parts[2], HEAD_DIM)
    lr = parts[4].reshape(b, t, 2, GLA_RANK)
    la = jax.nn.log_sigmoid(jnp.einsum('btjr,jrd->jbtd', lr, w_lr) + b_lr[:, None, None, :]) / GLA_NORMALIZER
    return q, k, v, heads(la[0], GLA_DK), heads(la[1], GLA_DK)

def gla_output(o, g, norm_g):
    o = o * lax.rsqrt(jnp.mean(o * o, axis=-1, keepdims=True) + EPS)
    return merge_heads(o) * norm_g * jax.nn.silu(g)

def gla_mixer(parts, parts_c, w_lr, b_lr, norm_g, ctx_out):
    q, k, v, la_f, la_b = gla_inputs(parts, w_lr, b_lr)
    qc, kc, vc, lac_f, lac_b = gla_inputs(parts_c, w_lr, b_lr)
    s0 = jnp.zeros(qc.shape[:2] + (GLA_DK, HEAD_DIM), F32)
    oc_f, s_f = gla_scan(qc, kc, vc, lac_f, s0, ctx_out)
    oc_b, s_b = gla_scan(flip_t(qc), flip_t(kc), flip_t(vc), flip_t(lac_b), s0, ctx_out)
    o_f, _ = gla_scan(q, k, v, la_f, s_f, True)
    o_b, _ = gla_scan(flip_t(q), flip_t(k), flip_t(v), flip_t(la_b), s_b, True)
    out = gla_output(o_f + flip_t(o_b), parts[3], norm_g)
    out_c = gla_output(oc_f + flip_t(oc_b), parts_c[3], norm_g) if ctx_out else None
    return out, out_c

def mlstm_inputs(parts, conv_w, gate_b, rows, cols):
    b, t, _ = parts[5].shape
    qk = jax.nn.silu(conv2d_grid(jnp.concatenate([parts[5], parts[6]], axis=-1), conv_w, rows, cols))
    q = heads(qk[..., :GROUP_W], HEAD_DIM)
    k = heads(qk[..., GROUP_W:], HEAD_DIM) * HEAD_DIM ** -0.5
    v = heads(parts[7], HEAD_DIM)
    gates = (parts[9].reshape(b, t, 2, 2, N_HEADS) + gate_b).transpose(2, 3, 0, 4, 1)
    return (q, k, v, gates[0, 0], jax.nn.log_sigmoid(gates[0, 1]),
            gates[1, 0], jax.nn.log_sigmoid(gates[1, 1]))

def mlstm_mixer(parts, parts_c, conv_w, gate_b, rows, ctx_out):
    q, k, v, i_f, f_f, i_b, f_b = mlstm_inputs(parts, conv_w, gate_b, rows, GRID_W)
    qc, kc, vc, ic_f, fc_f, ic_b, fc_b = mlstm_inputs(parts_c, conv_w, gate_b, 1, parts_c[5].shape[1])
    nb, nh = qc.shape[:2]
    st0 = (jnp.zeros((nb, nh, HEAD_DIM, HEAD_DIM), F32), jnp.zeros((nb, nh, HEAD_DIM), F32),
           jnp.zeros((nb, nh), F32))
    hc_f, st_f = mlstm_scan(qc, kc, vc, ic_f, fc_f, st0, ctx_out)
    hc_b, st_b = mlstm_scan(flip_t(qc), flip_t(kc), flip_t(vc), flip_t(ic_b), flip_t(fc_b), st0, ctx_out)
    h_f, _ = mlstm_scan(q, k, v, i_f, f_f, st_f, True)
    h_b, _ = mlstm_scan(flip_t(q), flip_t(k), flip_t(v), flip_t(i_b), flip_t(f_b), st_b, True)
    out = jax.nn.sigmoid(parts[8]) * merge_heads(h_f + flip_t(h_b))
    out_c = jax.nn.sigmoid(parts_c[8]) * merge_heads(hc_f + flip_t(hc_b)) if ctx_out else None
    return out, out_c

def sgu(u, v, w_s, b_s):
    b, t, _ = v.shape
    mu = jnp.mean(v, axis=-1, keepdims=True)
    vn = (v - mu) * lax.rsqrt(jnp.mean((v - mu) ** 2, axis=-1, keepdims=True) + EPS)
    vg = vn.reshape(b, t // SGU_CHUNK, SGU_CHUNK, N_HEADS, HEAD_DIM)
    mixed = jnp.einsum('gls,bnsgc->bnlgc', w_s, vg) + b_s.T[:, :, None]
    return u * mixed.reshape(b, t, GROUP_W)

def fourier_mix(u):
    b, t, _ = u.shape
    ug = u.astype(F32).reshape(b, t, N_HEADS, HEAD_DIM)
    return jnp.fft.fft2(ug, axes=(1, 3), norm='ortho').real.reshape(b, t, GROUP_W)

def token_mixers(h, hc, w_in, gla_w_lr, gla_b_lr, gla_norm_g, mlstm_conv, mlstm_gate_b, sgu_w, sgu_b, ctx_out):
    rows = h.shape[1] // GRID_W
    parts = split_cols((h @ w_in).astype(F32))
    parts_c = split_cols((hc @ (w_in if ctx_out else w_in[:, :REC_W])).astype(F32))
    gla, gla_c = gla_mixer(parts, parts_c, gla_w_lr, gla_b_lr, gla_norm_g, ctx_out)
    ml, ml_c = mlstm_mixer(parts, parts_c, mlstm_conv, mlstm_gate_b, rows, ctx_out)
    sg = sgu(parts[10], parts[11], sgu_w, sgu_b)
    fo = fourier_mix(parts[12])
    mix = jnp.concatenate([gla, ml, sg, fo], axis=-1).astype(h.dtype)
    if not ctx_out:
        return mix, None
    sg_c = sgu(parts_c[10], parts_c[11], sgu_w, sgu_b)
    fo_c = fourier_mix(parts_c[12])
    mix_c = jnp.concatenate([gla_c, ml_c, sg_c, fo_c], axis=-1).astype(hc.dtype)
    return mix, mix_c

def swiglu(h, w_g, w_u, w_d):
    return (jax.nn.silu(h @ w_g) * (h @ w_u)) @ w_d

def moe_ffn(h, w_router, w_g, w_u, w_d):
    b, t, d = h.shape
    hf = h.reshape(-1, d)
    logits = (hf @ w_router).astype(F32)
    top_v, top_i = lax.top_k(logits, TOP_K)
    gates = jax.nn.softmax(top_v, axis=-1)
    flat_e = top_i.reshape(-1)
    order = jnp.argsort(flat_e)
    tok = order // TOP_K
    xs = hf[tok]
    sizes = jnp.bincount(flat_e, length=N_EXPERTS).astype(jnp.int32)
    g = lax.ragged_dot(xs, w_g, sizes)
    u = lax.ragged_dot(xs, w_u, sizes)
    y = lax.ragged_dot(jax.nn.silu(g) * u, w_d, sizes)
    y = y * gates.reshape(-1)[order][:, None].astype(y.dtype)
    return jnp.zeros_like(hf).at[tok].add(y).reshape(b, t, d)

def setup_inputs(seed: int = 0) -> dict:
    key = jax.random.key(seed)
    ks = jax.random.split(key, 25)
    nrm = jax.random.normal
    s = D_MODEL ** -0.5
    fbias = jnp.zeros((DEPTH, 2, 2, N_HEADS), F32).at[:, :, 1, :].set(jnp.linspace(3.0, 6.0, N_HEADS))
    return {
        'x': nrm(ks[0], (BATCH, SEQ, D_MODEL), F32),
        'c': nrm(ks[1], (BATCH, D_MODEL), F32),
        'ctx': nrm(ks[2], (BATCH, CTX_LEN, D_MODEL), F32),
        'c_ctx': nrm(ks[3], (D_MODEL,), F32),
        'w_ada': nrm(ks[4], (DEPTH, D_MODEL, 6 * D_MODEL), F32) * s,
        'b_ada': 0.02 * nrm(ks[5], (DEPTH, 6 * D_MODEL), F32),
        'norm_mix_g': 1.0 + 0.1 * nrm(ks[6], (DEPTH, D_MODEL), F32),
        'norm_ffn_g': 1.0 + 0.1 * nrm(ks[7], (DEPTH, D_MODEL), F32),
        'w_in': nrm(ks[8], (DEPTH, D_MODEL, D_IN), F32) * s,
        'w_out': nrm(ks[9], (DEPTH, MIX_W, D_MODEL), F32) * MIX_W ** -0.5,
        'gla_w_lr': nrm(ks[10], (DEPTH, 2, GLA_RANK, GLA_QK_W), F32) * GLA_RANK ** -0.5,
        'gla_b_lr': 0.1 * nrm(ks[11], (DEPTH, 2, GLA_QK_W), F32),
        'gla_norm_g': 1.0 + 0.1 * nrm(ks[12], (DEPTH, GROUP_W), F32),
        'mlstm_conv': nrm(ks[13], (DEPTH, CONV_K, CONV_K, 2 * GROUP_W), F32) / CONV_K,
        'mlstm_gate_b': fbias + 0.1 * nrm(ks[14], (DEPTH, 2, 2, N_HEADS), F32),
        'sgu_w': nrm(ks[15], (DEPTH, N_HEADS, SGU_CHUNK, SGU_CHUNK), F32) * SGU_CHUNK ** -0.5,
        'sgu_b': 1.0 + 0.1 * nrm(ks[16], (DEPTH, N_HEADS, SGU_CHUNK), F32),
        'ffn_w_gate': nrm(ks[17], (N_DENSE, D_MODEL, D_FF), F32) * s,
        'ffn_w_up': nrm(ks[18], (N_DENSE, D_MODEL, D_FF), F32) * s,
        'ffn_w_down': nrm(ks[19], (N_DENSE, D_FF, D_MODEL), F32) * D_FF ** -0.5,
        'moe_router': nrm(ks[20], (N_MOE, D_MODEL, N_EXPERTS), F32) * s,
        'moe_w_gate': nrm(ks[21], (N_MOE, N_EXPERTS, D_MODEL, D_FF_EXPERT), F32) * s,
        'moe_w_up': nrm(ks[22], (N_MOE, N_EXPERTS, D_MODEL, D_FF_EXPERT), F32) * s,
        'moe_w_down': nrm(ks[23], (N_MOE, N_EXPERTS, D_FF_EXPERT, D_MODEL), F32) * D_FF_EXPERT ** -0.5,
        'final_norm_g': 1.0 + 0.1 * nrm(ks[24], (D_MODEL,), F32),
    }

def reference(x, c, ctx, c_ctx, w_ada, b_ada, norm_mix_g, norm_ffn_g, w_in, w_out, gla_w_lr, gla_b_lr,
              gla_norm_g, mlstm_conv, mlstm_gate_b, sgu_w, sgu_b, ffn_w_gate, ffn_w_up, ffn_w_down,
              moe_router, moe_w_gate, moe_w_up, moe_w_down, final_norm_g):
    xc = ctx
    for l in range(DEPTH):
        ctx_out = l < DEPTH - 1
        mod = jnp.split(jax.nn.silu(c) @ w_ada[l] + b_ada[l], 6, axis=-1)
        mod_c = jnp.split(jax.nn.silu(c_ctx) @ w_ada[l] + b_ada[l], 6, axis=-1)
        sh1, sc1, g1, sh2, sc2, g2 = (m[:, None, :] for m in mod)
        csh1, csc1, cg1, csh2, csc2, cg2 = mod_c
        h = modulate(rmsnorm(x, norm_mix_g[l]), sh1, sc1)
        hc = modulate(rmsnorm(xc, norm_mix_g[l]), csh1, csc1)
        mix, mix_c = token_mixers(h, hc, w_in[l], gla_w_lr[l], gla_b_lr[l], gla_norm_g[l], mlstm_conv[l],
                                  mlstm_gate_b[l], sgu_w[l], sgu_b[l], ctx_out)
        x = x + g1 * (mix @ w_out[l])
        if ctx_out:
            xc = xc + cg1 * (mix_c @ w_out[l])
        h = modulate(rmsnorm(x, norm_ffn_g[l]), sh2, sc2)
        i = l // 2
        if l % 2 == 0:
            x = x + g2 * swiglu(h, ffn_w_gate[i], ffn_w_up[i], ffn_w_down[i])
            if ctx_out:
                hc = modulate(rmsnorm(xc, norm_ffn_g[l]), csh2, csc2)
                xc = xc + cg2 * swiglu(hc, ffn_w_gate[i], ffn_w_up[i], ffn_w_down[i])
        else:
            x = x + g2 * moe_ffn(h, moe_router[i], moe_w_gate[i], moe_w_up[i], moe_w_down[i])
            if ctx_out:
                hc = modulate(rmsnorm(xc, norm_ffn_g[l]), csh2, csc2)
                xc = xc + cg2 * moe_ffn(hc, moe_router[i], moe_w_gate[i], moe_w_up[i], moe_w_down[i])
    return rmsnorm(x, final_norm_g)


_drawn_inputs = setup_inputs


def setup_inputs(seed=0):
    import zlib

    import numpy as np

    out = dict(_drawn_inputs(seed))
    spreads = {}
    factors = {}
    for name, (base, spread) in spreads.items():
        noise = np.random.default_rng([zlib.crc32(name.encode()), seed]).standard_normal(out[name].shape)
        drawn = base * np.exp(spread * noise) if base else spread * noise
        out[name] = __import__('jax').numpy.asarray(drawn.astype(out[name].dtype))
    for name, factor in factors.items():
        out[name] = (out[name] * factor).astype(out[name].dtype)
    return out
```

```python
from contextlib import ExitStack

import concourse.bass as bass
import numpy as np
from concourse import mybir

F32 = mybir.dt.float32
I32 = mybir.dt.int32
U32 = mybir.dt.uint32
ACT = mybir.ActivationFunctionType
ALU = mybir.AluOpType
AX = mybir.AxisListType

P = 128
D = 1024
KD = D // P
CTX, SEQ = 256, 1024
T = CTX + SEQ
NT = T // P
NCT = CTX // P
GRID_W = 64
ROWS = SEQ // GRID_W
GROUPS = [(0, CTX), (CTX, 512), (CTX + 512, 512)]
NH, HD = 4, 64
GW = NH * HD
DFF = 2816
DFE = 3584
NE = 8
EPS = 1e-6
BIG = 1e30
NBLK = (2 * SEQ + NE * (P - 1)) // P
NSLOT = NBLK * P
FG = 512
NFG = DFE // FG

CST = {}


def _layout():
    at = 0
    for name, n in [("ident", P), ("ones", P), ("negF", 4 * P), ("negB", 4 * P), ("keepF", P), ("keepB", P),
                    ("sel8", 8 * P), ("selpair", 4 * P), ("blockg", 2 * P), ("blockm", 130), ("tri", P),
                    ("pref", NE), ("koff", NE), ("blk", NBLK), ("one", 1), ("eps", 1), ("chan", 2 * P), ("row4", 4), ("row2", 2)]:
        CST[name] = (at, n)
        at += n
    return at


NCST = _layout()


def constants():
    c = np.zeros((P, NCST), np.float32)

    def put(name, a):
        o, n = CST[name]
        c[:a.shape[0], o:o + n] = a.reshape(a.shape[0], n)

    s, l = np.arange(P)[:, None], np.arange(P)[None, :]
    put("ident", np.eye(P))
    put("ones", np.ones((P, P)))
    put("negF", np.tile(np.where(s > l, BIG, 0.0), (1, 4)))
    put("negB", np.tile(np.where(s < l, BIG, 0.0), (1, 4)))
    put("keepF", (s <= l) * 1.0)
    put("keepB", (s >= l) * 1.0)
    sel = np.zeros((8, 8, P))
    for r in range(8):
        sel[r, r] = 1
    put("sel8", sel)
    selp = np.zeros((8, 4, P))
    for j in range(4):
        for p in range(P):
            selp[4 * (j // 2) + 2 * (j % 2) + p // HD, j, p] = 1
    put("selpair", selp)
    put("blockg", (np.arange(P)[:, None] // 32 == np.arange(2 * P)[None, :] // HD) * 1.0)
    put("blockm", (np.arange(P)[:, None] // HD == np.arange(130)[None, :] // 65) * 1.0)
    put("tri", (s < l) * 1.0)
    put("pref", np.tile(np.arange(NE, 0, -1.0), (P, 1)))
    put("koff", np.tile(P * np.arange(NE * 1.0), (P, 1)))
    put("blk", np.tile(np.arange(NBLK * 1.0), (P, 1)))
    put("row4", (np.arange(P)[:, None] // 32 == np.arange(4)[None, :]) * 1.0)
    put("row2", (np.arange(P)[:, None] // HD == np.arange(2)[None, :]) * 1.0)
    put("one", np.ones((P, 1)))
    put("eps", np.full((P, 1), EPS))
    ang = 2 * np.pi * (np.outer(np.arange(HD), np.arange(HD)) % HD) / HD
    ch = np.zeros((P, 2, P))
    for h in range(2):
        i = slice(h * HD, (h + 1) * HD)
        ch[i, 0, i] = np.cos(ang)
        ch[i, 1, i] = -np.sin(ang)
    put("chan", ch)
    return c


def dft(n):
    ang = 2 * np.pi * (np.outer(np.arange(n), np.arange(n)) % n) / n
    m = np.stack([np.cos(ang), np.sin(ang)], 1) / np.sqrt(n * HD)
    return np.ascontiguousarray(m.reshape(n // P, P, 2, n).transpose(1, 0, 2, 3)).astype(np.float32)


class Phase:

    def __init__(self, nc, name):
        self.nc, self.name, self.sems = nc, name, []

    def __enter__(self):
        self.stack = ExitStack()
        return self

    def sb(self, name, shape, dt=F32):
        return self.stack.enter_context(self.nc.sbuf_tensor(f"{self.name}_{name}", shape, dt))

    def sem(self, name):
        s = self.stack.enter_context(self.nc.semaphore(f"{self.name}_{name}"))
        self.sems.append(s)
        return s

    def __exit__(self, kind, value, trace):
        if kind is None:
            for s in self.sems:
                self.nc.gpsimd.sem_clear(s)
            self.nc.all_engine_barrier()
        self.stack.close()
        return False


class Chain:

    def __init__(self, eng, sem):
        self.eng, self.sem, self.n = eng, sem, 0

    def __call__(self, ins):
        self.n += 1
        ins.then_inc(self.sem, 1)
        self.eng.wait_ge(self.sem, self.n)


def cols(ap1d):
    return ap1d.rearrange("(k p) -> p k", p=P)


def bc(ap, n):
    return ap.unsqueeze(2).to_broadcast([ap.shape[0], ap.shape[1], n])


def phase_modulation(nc, io, S):
    with Phase(nc, "ada") as ph:
        wring = ph.sb("w", [P, 2, KD, 512])
        cond = ph.sb("cond", [P, 2, KD])
        act = ph.sb("act", [P, KD, 2])
        bias = ph.sb("bias", [P, 2, 48])
        ng = ph.sb("ng", [P, 2, 2, KD])
        small = ph.sem("small_loaded")
        wl = [ph.sem(f"w_loaded{s}") for s in range(2)]
        silu_ready, mm_done, evac, mod_done = (ph.sem(n) for n in ("silu_ready", "mm_done", "evacuated", "mod_done"))
        wfree = ph.sem("w_slot_free")
        mod, gmod, ps = S["mod"], S["gmod"], S["ps"]
        with nc.Block() as block:

            @block.sync
            def _(sp):
                with nc.allow_non_contiguous_dma(reason="vectors as columns"):
                    sp.dma_start(S["cst"][:, :], io["cst"]).then_inc(small, 16)
                    sp.dma_start(cond[:, 0, :], cols(io["c"].rearrange("a d -> (a d)"))).then_inc(small, 16)
                    sp.dma_start(cond[:, 1, :], cols(io["c_ctx"])).then_inc(small, 16)
                    for l in range(2):
                        sp.dma_start(bias[:, l, :], cols(io["b_ada"][l])).then_inc(small, 16)
                        sp.dma_start(ng[:, l, 0, :], cols(io["norm_mix_g"][l])).then_inc(small, 16)
                        sp.dma_start(ng[:, l, 1, :], cols(io["norm_ffn_g"][l])).then_inc(small, 16)
                for l in range(2):
                    w = io["w_ada"][l].rearrange("(k p) n -> p k n", p=P)
                    with sp.Fori(0, 6) as i:
                        for s in range(2):
                            sp.wait_ge(wfree, i * 2 + (12 * l + s + 1))
                            sp.dma_start(wring[:, s, :, :], w[:, :, bass.ds(i * 1024 + 512 * s, 512)]).then_inc(wl[s], 16)

            @block.scalar
            def _(act_e):
                act_e.wait_ge(small, 16 * 9)
                for j in range(2):
                    a = nc.scalar.activation(act[:, :, j], cond[:, j, :], ACT.Silu)
                a.then_inc(silu_ready, 1)

            @block.tensor
            def _(pe):
                pe.sem_inc(wfree, 2)
                pe.wait_ge(silu_ready, 1)
                for l in range(2):
                    with pe.Fori(0, 6) as i:
                        for s in range(2):
                            pe.wait_ge(wl[s], i * 16 + 16 * (6 * l + 1))
                            pe.wait_ge(evac, i * 2 + (12 * l + s + 1))
                            for m in range(4):
                                for k in range(KD):
                                    mm = nc.tensor.matmul(ps[:, s, 2 * m:2 * m + 2], wring[:, s, k, m * P:(m + 1) * P],
                                                          act[:, k, :], start=(k == 0), stop=(k == KD - 1))
                            mm.then_inc(mm_done, 1)
                            pe.wait_ge(mm_done, i * 2 + (12 * l + s + 1))
                            pe.sem_inc(wfree, 1)

            @block.vector
            def _(dve):
                dve.sem_inc(evac, 2)
                dve.wait_ge(small, 16 * 9)
                for l in range(2):
                    with dve.Fori(0, 6) as i:
                        for s in range(2):
                            dve.wait_ge(mm_done, i * 2 + (12 * l + s + 1))
                            nc.vector.tensor_tensor(
                                mod[:, l, bass.ds(i * 8 + 4 * s, 4), :], ps[:, s, 0:8].rearrange("p (m j) -> p m j", j=2),
                                bc(bias[:, l, bass.ds(i * 8 + 4 * s, 4)], 2), ALU.add).then_inc(evac, 1)
                dve.wait_ge(evac, 26)
                for l in range(2):
                    for w in range(2):
                        for j in range(2):
                            a = nc.vector.scalar_tensor_tensor(
                                out=gmod[:, l, w, j, :], in0=mod[:, l, 24 * w + 8:24 * w + 16, j], scalar=1.0,
                                in1=ng[:, l, w, :], op0=ALU.add, op1=ALU.mult)
                a.then_inc(mod_done, 1)
                dve.wait_ge(mod_done, 1)


def phase_to_features(nc, io, S):
    with Phase(nc, "x0") as ph:
        rows = ph.sb("rows", [P, 2, D])
        turned = ph.sb("turned", [P, 2, KD, P])
        loaded = [ph.sem(f"loaded{s}") for s in range(2)]
        stored = [ph.sem(f"stored{s}") for s in range(2)]
        tr, ev = ph.sem("transposed"), ph.sem("evacuated")
        ps, ident = S["ps"], S["c"]("ident")
        with nc.Block() as block:

            @block.sync
            def _(sp):
                for n in range(NT):
                    src = io["ctx"][0, n * P:(n + 1) * P, :] if n < NCT else io["x"][0, (n - NCT) * P:(n - NCT + 1) * P, :]
                    if n >= 2:
                        sp.wait_ge(tr, n - 1)
                    sp.dma_start(rows[:, n % 2, :], src).then_inc(loaded[n % 2], 16)

            @block.tensor
            def _(pe):
                for n in range(NT):
                    pe.wait_ge(loaded[n % 2], 16 * (n // 2 + 1))
                    if n >= 2:
                        pe.wait_ge(ev, n - 1)
                    for k in range(KD):
                        b = 2 * (n % 2) + k // 4
                        t = nc.tensor.transpose(ps[:, b, (k % 4) * P:(k % 4 + 1) * P], rows[:, n % 2, k * P:(k + 1) * P], ident)
                    t.then_inc(tr, 1)

            @block.vector
            def _(dve):
                for n in range(NT):
                    dve.wait_ge(tr, n + 1)
                    if n >= 2:
                        dve.wait_ge(stored[n % 2], 16 * (n // 2))
                    nc.vector.tensor_copy(turned[:, n % 2, :, :], ps[:, 2 * (n % 2):2 * (n % 2) + 2, :].rearrange(
                        "p b (k t) -> p (b k) t", t=P)).then_inc(ev, 1)

            @block.scalar
            def _(act):
                for n in range(NT):
                    act.wait_ge(ev, n + 1)
                    act.dma_start(S["xT_d"][:, :, n * P:(n + 1) * P], turned[:, n % 2, :, :]).then_inc(stored[n % 2], 16)
                for s in range(2):
                    act.wait_ge(stored[s], 16 * (NT // 2))


def phase_norm(nc, S, name, xT, hT, l, which, groups):
    with Phase(nc, name) as ph:
        sq = ph.sb("sq", [P, 4, 512])
        rstd = ph.sb("rstd", [P, 2, 512])
        xl, sq_ready, sq_used, ss_ready, var_ready, sd_ready, scaled, shifted, rst = (
            ph.sem(n) for n in ("x_loaded", "sq_ready", "sq_used", "ss_ready", "var_ready", "sd_ready", "scaled", "shifted", "rstd_ready"))
        ps, ones = S["ps"], S["c"]("ones")
        gmod, mod = S["gmod"], S["mod"]
        first = groups[0][0]
        with nc.Block() as block:

            @block.sync
            def _(sp):
                for t0, n in groups:
                    sp.dma_start(xT[:, :, t0:t0 + n], S["xT_d"][:, :, t0:t0 + n]).then_inc(xl, 16)

            @block.scalar
            def _(act):
                act.wait_ge(xl, 16 * len(groups))

                def squares(g, t0, n):
                    for k in range(KD):
                        q = g * KD + k
                        if q >= 4:
                            act.wait_ge(sq_used, q - 3)
                        nc.scalar.activation(sq[:, q % 4, :n], xT[:, k, t0:t0 + n], ACT.Square).then_inc(sq_ready, 1)

                def root(g, t0, n):
                    act.wait_ge(var_ready, g + 1)
                    nc.scalar.activation(rstd[:, g % 2, :n], rstd[:, g % 2, :n], ACT.Sqrt).then_inc(sd_ready, 1)

                for g, (t0, n) in enumerate(groups):
                    squares(g, t0, n)
                    root(g, t0, n)

            @block.tensor
            def _(pe):
                for g, (t0, n) in enumerate(groups):
                    for k in range(KD):
                        q = g * KD + k
                        pe.wait_ge(sq_ready, q + 1)
                        mm = nc.tensor.matmul(ps[:, g, :n], ones, sq[:, q % 4, :n], start=(k == 0), stop=(k == KD - 1))
                        mm.then_inc(sq_used, 1)

            @block.vector
            def _(dve):
                for g, (t0, n) in enumerate(groups):
                    dve.wait_ge(sq_used, (g + 1) * KD)
                    if g >= 2:
                        dve.wait_ge(scaled, KD * (g - 1))
                    nc.vector.tensor_scalar(rstd[:, g % 2, :n], ps[:, g, :n], 1.0 / D, EPS, ALU.mult, ALU.add).then_inc(var_ready, 1)
                    dve.wait_ge(sd_ready, g + 1)
                    nc.vector.reciprocal(rstd[:, g % 2, :n], rstd[:, g % 2, :n]).then_inc(rst, 1)
                    dve.wait_ge(rst, g + 1)
                    j = 1 if t0 < CTX else 0
                    for k in range(KD):
                        nc.vector.scalar_tensor_tensor(
                            out=hT[:, k, t0:t0 + n], in0=xT[:, k, t0:t0 + n], scalar=gmod[:, l, which, j, k:k + 1],
                            in1=rstd[:, g % 2, :n], op0=ALU.mult, op1=ALU.mult).then_inc(scaled, 1)

            @block.gpsimd
            def _(pool):
                for g, (t0, n) in enumerate(groups):
                    j = 1 if t0 < CTX else 0
                    for k in range(KD):
                        pool.wait_ge(scaled, g * KD + k + 1)
                        nc.gpsimd.tensor_scalar(hT[:, k, t0:t0 + n], hT[:, k, t0:t0 + n],
                                                mod[:, l, 24 * which + k, j:j + 1], None, ALU.add).then_inc(shifted, 1)
                pool.wait_ge(shifted, KD * len(groups))


def phase_project(nc, io, S, l, hT, FM, TM, ctx_out):
    loads = [((0, 256), [0, 1]), ((800, 512), [2, 3, 4, 5]), ((2352, 256), [6, 7]), (None, [8])]
    tok = [(256, 0), (1312, 512), (1840, 1024)]
    w_in = io["w_in"][l].rearrange("(k p) n -> p k n", p=P)
    units = []
    for i, (_, chunks) in enumerate(loads):
        for j, ch in enumerate(chunks):
            for t0, n in GROUPS:
                if ch in (6, 7) and not ctx_out and t0 < CTX:
                    continue
                units.append((i, "fm", j, ch, t0, n))
    for i, (_, dst) in enumerate(tok):
        for n in range(NT):
            if dst == 1024 and not ctx_out and n < NCT:
                continue
            units.append((len(loads) + i, "tm", 0, dst, n, 0))
    last_of = {}
    for u, un in enumerate(units):
        last_of[un[0]] = u
    NB = 8
    with Phase(nc, f"proj{l}") as ph:
        wring = ph.sb("w", [P, 2, KD, 512])
        wl = [ph.sem(f"w_loaded{s}") for s in range(2)]
        mm_done, ev = ph.sem("mm_done"), [ph.sem("evacuated_act"), ph.sem("evacuated_dve")]
        zeroed = ph.sem("gate_slot_zeroed")
        ps = S["ps"]
        nl = len(loads) + len(tok)
        cnt = {}
        need = []
        for i in range(nl):
            s = i % 2
            cnt[s] = cnt.setdefault(s, 0) + (5 if i == 3 else 1)
            need.append(16 * cnt[s])

        with nc.Block() as block:

            @block.sync
            def _(sp):
                for i in range(nl):
                    s = i % 2
                    if i >= 2:
                        sp.wait_ge(mm_done, last_of[i - 2] + 1)
                    if i == 3:
                        sp.wait_ge(zeroed, 1)
                        with nc.allow_non_contiguous_dma(reason="gate columns"):
                            for dst, src, n in ((0, 1824, 4), (4, 1832, 4), (32, 1828, 4), (36, 1836, 4), (64, 768, 32)):
                                sp.dma_start(wring[:, s, :, dst:dst + n], w_in[:, :, src:src + n]).then_inc(wl[s], 16)
                    else:
                        c0, n = loads[i][0] if i < len(loads) else (tok[i - len(loads)][0], 512)
                        sp.dma_start(wring[:, s, :, 0:n], w_in[:, :, c0:c0 + n]).then_inc(wl[s], 16)

            @block.gpsimd
            def _(pool):
                pool.wait_ge(mm_done, last_of[1] + 1)
                nc.gpsimd.memset(wring[:, 1, :, 0:P], 0.0).then_inc(zeroed, 1)

            @block.tensor
            def _(pe):
                seen = -1
                for u, (i, kind, j, dst, a, n) in enumerate(units):
                    if i != seen:
                        pe.wait_ge(wl[i % 2], need[i])
                        seen = i
                    if u >= NB:
                        v = u - NB
                        pe.wait_ge(ev[v % 2], v // 2 + 1)
                    for k in range(KD):
                        if kind == "fm":
                            mm = nc.tensor.matmul(ps[:, u % NB, :n], wring[:, i % 2, k, j * P:(j + 1) * P], hT[:, k, a:a + n],
                                                  start=(k == 0), stop=(k == KD - 1))
                        else:
                            mm = nc.tensor.matmul(ps[:, u % NB, :], hT[:, k, a * P:(a + 1) * P], wring[:, i % 2, k, :],
                                                  start=(k == 0), stop=(k == KD - 1))
                    mm.then_inc(mm_done, 1)

            def evacuate(eng, copy, par):
                for u, (i, kind, j, dst, a, n) in enumerate(units):
                    if u % 2 != par:
                        continue
                    eng.wait_ge(mm_done, u + 1)
                    out = FM[:, dst, a:a + n] if kind == "fm" else TM[:, a, dst:dst + 512]
                    src = ps[:, u % NB, :n] if kind == "fm" else ps[:, u % NB, :]
                    copy(out, src).then_inc(ev[par], 1)
                eng.wait_ge(ev[par], (len(units) + 1 - par) // 2)

            @block.scalar
            def _(act):
                evacuate(act, nc.scalar.copy, 0)

            @block.vector
            def _(dve):
                evacuate(dve, nc.vector.tensor_copy, 1)


def phase_fourier(nc, io, S, l, FM, ctx_out):
    tiles = list(range(0 if ctx_out else NCT, NT))
    with Phase(nc, f"four{l}") as ph:
        Y = ph.sb("y", [P, NT, 512])
        dring = ph.sb("dft", [P, 3, 2, SEQ])
        dctx = ph.sb("dftc", [P, NCT, 2, CTX])
        Z = ph.sb("z", [P, 2, T])
        dl = [ph.sem(f"dft_loaded{s}") for s in range(3)]
        cl, ymm, yev, dused, zdone, cdone, zev, st = (
            ph.sem(n) for n in ("ctx_dft_loaded", "y_done", "y_ready", "dft_used", "z_done", "ctx_z_done", "z_ready", "stored"))
        ps, chan = S["ps"], S["c"]("chan")
        with nc.Block() as block:

            @block.sync
            def _(sp):
                if ctx_out:
                    sp.dma_start(dctx[:, :, :, :], io["dft_ctx"]).then_inc(cl, 16)
                for i in range(SEQ // P):
                    if i >= 3:
                        sp.wait_ge(dused, i - 2)
                    sp.dma_start(dring[:, i % 3, :, :], io["dft_seq"][:, i, :, :]).then_inc(dl[i % 3], 16)
                sp.wait_ge(zev, 5 if ctx_out else 4)
                a = 0 if ctx_out else CTX
                sp.dma_start(S["mixT_d"][:, 6:8, a:], Z[:, :, a:]).then_inc(st, 16)
                sp.wait_ge(st, 16)

            @block.tensor
            def _(pe):
                for i, n in enumerate(tiles):
                    if i >= 2:
                        pe.wait_ge(yev, i - 1)
                    for c in range(2):
                        mm = nc.tensor.matmul(ps[:, i % 2, c * 256:(c + 1) * 256], FM[:, 6 + c, n * P:(n + 1) * P], chan,
                                              start=True, stop=True)
                    mm.then_inc(ymm, 1)
                pe.wait_ge(yev, len(tiles))
                for i in range(SEQ // P):
                    pe.wait_ge(dl[i % 3], 16 * (i // 3 + 1))
                    for c in range(2):
                        for trig in range(2):
                            for half in range(2):
                                mm = nc.tensor.matmul(
                                    ps[:, 2 + 2 * c + half, :], Y[:, NCT + i, c * 256 + trig * P:c * 256 + (trig + 1) * P],
                                    dring[:, i % 3, trig, half * 512:(half + 1) * 512],
                                    start=(i == 0 and trig == 0), stop=(i == SEQ // P - 1 and trig == 1))
                    mm.then_inc(dused, 1)
                if ctx_out:
                    pe.wait_ge(cl, 16)
                    for c in range(2):
                        for i in range(NCT):
                            for trig in range(2):
                                mm = nc.tensor.matmul(
                                    ps[:, 6 + c, :CTX], Y[:, i, c * 256 + trig * P:c * 256 + (trig + 1) * P],
                                    dctx[:, i, trig, :], start=(i == 0 and trig == 0), stop=(i == NCT - 1 and trig == 1))
                    mm.then_inc(cdone, 1)

            @block.vector
            def _(dve):
                for i, n in enumerate(tiles):
                    dve.wait_ge(ymm, i + 1)
                    nc.vector.tensor_copy(Y[:, n, :], ps[:, i % 2, :]).then_inc(yev, 1)
                dve.wait_ge(dused, SEQ // P)
                for c in range(2):
                    for half in range(2):
                        nc.vector.tensor_copy(Z[:, c, CTX + half * 512:CTX + (half + 1) * 512],
                                              ps[:, 2 + 2 * c + half, :]).then_inc(zev, 1)
                if ctx_out:
                    dve.wait_ge(cdone, 1)
                    nc.vector.tensor_copy(Z[:, :, 0:CTX], ps[:, 6:8, :CTX]).then_inc(zev, 1)


def phase_sgu(nc, io, S, l, TM, ctx_out):
    tiles = list(range(0 if ctx_out else NCT, NT))
    with Phase(nc, f"sgu{l}") as ph:
        ws = ph.sb("ws", [P, NH, P])
        wsT = ph.sb("wsT", [P, NH, P])
        bs = ph.sb("bs", [P, NH])
        stats = ph.sb("stats", [P, NT, 6])
        mv = ph.sb("mv", [P, NT, 2])
        rstd = ph.sb("rstd", [P, NT])
        ld, tr, wev, chain, var, sd, vn, mm_done, done = (
            ph.sem(n) for n in ("loaded", "transposed", "wT_ready", "dve_step", "var_ready", "sd_ready", "vn_ready", "mixed", "gated"))
        ps, ident = S["ps"], S["c"]("ident")
        t0 = tiles[0]
        with nc.Block() as block:

            @block.sync
            def _(sp):
                sp.dma_start(ws[:, :, :], io["sgu_w"][l].rearrange("g a b -> a g b")).then_inc(ld, 16)
                with nc.allow_non_contiguous_dma(reason="bias columns"):
                    sp.dma_start(bs[:, :], io["sgu_b"][l].rearrange("g a -> a g")).then_inc(ld, 16)

            @block.tensor
            def _(pe):
                pe.wait_ge(ld, 32)
                for g in range(NH):
                    t = nc.tensor.transpose(ps[:, 7, g * P:(g + 1) * P], ws[:, g, :], ident)
                t.then_inc(tr, 1)
                pe.wait_ge(wev, 1)
                pe.wait_ge(vn, len(tiles))
                for g in range(NH):
                    v0 = 1280 + g * HD
                    nc.tensor.matmul(ps[:, g, :].rearrange("p (n c) -> p n c", c=HD), wsT[:, g, :], TM[:, NCT:NT, v0:v0 + HD],
                                     start=True, stop=True).then_inc(mm_done, 1)
                if ctx_out:
                    for g in range(NH):
                        v0 = 1280 + g * HD
                        nc.tensor.matmul(ps[:, 4, g * P:(g + 1) * P].rearrange("p (n c) -> p n c", c=HD), wsT[:, g, :],
                                         TM[:, 0:NCT, v0:v0 + HD], start=True, stop=True).then_inc(mm_done, 1)

            @block.scalar
            def _(act):
                act.wait_ge(tr, 1)
                nc.scalar.copy(wsT[:, :, :], ps[:, 7, :].rearrange("p (g t) -> p g t", t=P)).then_inc(wev, 1)
                act.wait_ge(var, 1)
                nc.scalar.activation(rstd[:, t0:], rstd[:, t0:], ACT.Sqrt).then_inc(sd, 1)

            @block.vector
            def _(dve):
                step = Chain(dve, chain)
                for n in tiles:
                    st = nc.vector.bn_stats(stats[:, n, :], TM[:, n, 1280:1536])
                step(st)
                for n in tiles:
                    st = nc.vector.bn_aggr(mv[:, n, :], stats[:, n, :])
                step(st)
                nc.vector.tensor_scalar(rstd[:, t0:], mv[:, t0:, 1], EPS, None, ALU.add).then_inc(var, 1)
                dve.wait_ge(sd, 1)
                step(nc.vector.reciprocal(rstd[:, t0:], rstd[:, t0:]))
                for n in tiles:
                    nc.vector.tensor_scalar(TM[:, n, 1280:1536], TM[:, n, 1280:1536], mv[:, n, 0:1], rstd[:, n:n + 1],
                                            ALU.subtract, ALU.mult).then_inc(vn, 1)
                dve.wait_ge(ld, 32)
                for g in range(NH):
                    dve.wait_ge(mm_done, g + 1)
                    u = TM[:, NCT:NT, 1024 + g * HD:1024 + (g + 1) * HD]
                    nc.vector.scalar_tensor_tensor(out=u, in0=ps[:, g, :].rearrange("p (n c) -> p n c", c=HD),
                                                   scalar=bs[:, g:g + 1], in1=u, op0=ALU.add, op1=ALU.mult).then_inc(done, 1)
                if ctx_out:
                    for g in range(NH):
                        dve.wait_ge(mm_done, 2 * NH)
                        u = TM[:, 0:NCT, 1024 + g * HD:1024 + (g + 1) * HD]
                        nc.vector.scalar_tensor_tensor(out=u, in0=ps[:, 4, g * P:(g + 1) * P].rearrange("p (n c) -> p n c", c=HD),
                                                       scalar=bs[:, g:g + 1], in1=u, op0=ALU.add, op1=ALU.mult).then_inc(done, 1)
                dve.wait_ge(done, 8 if ctx_out else 4)


def order(direction, j):
    if direction == 0:
        return j
    return NCT - 1 - j if j < NCT else NT - 1 - (j - NCT)


def phase_decays(nc, io, S, l, FM, M):
    with Phase(nc, f"dec{l}") as ph:
        wlr = ph.sb("wlr", [P, 2, P])
        blr = ph.sb("blr", [P, 2])
        gb = ph.sb("gb", [P, 1])
        z = ph.sb("z", [P, 2, T])
        e = FM[:, 6:8, :]
        lf = ph.sb("lf", [8, T])
        le = ph.sb("le", [8, T])
        cum8 = ph.sb("cum8", [8, 2, T])
        ones8 = ph.sb("ones8", [8, T])
        stack = ph.sb("stack", [P, T])
        mprev = ph.sb("mprev", [8, 2, NT])
        mlast = ph.sb("mlast", [8, 2, NT])
        dec = ph.sb("dec", [8, 2, NT])
        ld, zer, zmm, ch_d, ch_a, d2a, a2d, st_ready, trd, tev, dmm = (
            ph.sem(n) for n in ("loaded", "zeroed", "z_done", "dve_step", "act_step", "dve_to_act", "act_to_dve", "stack_ready",
                                "stack_transposed", "stack_read", "decay_rows_done"))
        ps, c = S["ps"], S["c"]
        mx, tg, dcol, qd, kd, em = M["mx"], M["tg"], M["dcol"], M["qd"], M["kd"], M["em"]

        def tiles(ap):
            return ap.rearrange("p (n t) -> p n t", t=P)

        with nc.Block() as block:

            @block.sync
            def _(sp):
                sp.wait_ge(zer, 1)
                with nc.allow_non_contiguous_dma(reason="vectors as columns"):
                    for d in range(2):
                        sp.dma_start(wlr[64 + 16 * d:80 + 16 * d, d, :], io["gla_w_lr"][l, d]).then_inc(ld, 16)
                        sp.dma_start(blr[:, d:d + 1], io["gla_b_lr"][l, d].rearrange("(p a) -> p a", a=1)).then_inc(ld, 16)
                        for kind in range(2):
                            sp.dma_start(gb[32 * kind + 4 * d:32 * kind + 4 * d + 4, :],
                                         io["mlstm_gate_b"][l, d, kind].rearrange("(p a) -> p a", a=1)).then_inc(ld, 16)

            @block.gpsimd
            def _(pool):
                nc.gpsimd.memset(wlr[:, :, :], 0.0)
                nc.gpsimd.memset(gb[:, :], 0.0)
                nc.gpsimd.memset(ones8[:, :], 1.0)
                nc.gpsimd.memset(stack[:, :], 0.0).then_inc(zer, 1)

            @block.tensor
            def _(pe):
                pe.wait_ge(ld, 16 * 8)
                for d in range(2):
                    for g, (t0, n) in enumerate(GROUPS):
                        mm = nc.tensor.matmul(ps[:, 3 * d + g, :n], wlr[64:96, d, :], FM[64:96, 8, t0:t0 + n], start=True, stop=True)
                mm.then_inc(zmm, 1)
                for d in range(2):
                    pe.wait_ge(st_ready, d + 1)
                    for n in range(NT):
                        q = d * NT + n
                        if q >= 2:
                            pe.wait_ge(tev, q - 1)
                        nc.tensor.transpose(ps[:, 6 + q % 2, 0:P], stack[:, n * P:(n + 1) * P], c("ident")).then_inc(trd, 1)
                pe.wait_ge(a2d, 6)
                selp = c("selpair").rearrange("p (a t) -> p a t", t=P)
                for j in range(4):
                    mm = nc.tensor.matmul(ps[:, 0, j * NT:(j + 1) * NT], selp[0:8, j, :], dec[:, j // 2, :], start=True, stop=True)
                mm.then_inc(dmm, 1)

            @block.scalar
            def _(act):
                step = Chain(act, ch_a)
                act.wait_ge(d2a, 1)
                step(nc.scalar.activation(e[:, :, :], e[:, :, :], ACT.Exp, scale=-1.0))
                nc.scalar.activation(e[:, :, :], e[:, :, :], ACT.Ln, bias=c("one")).then_inc(a2d, 1)
                act.wait_ge(d2a, 2)
                step(nc.scalar.activation(le[:, :], le[:, :], ACT.Exp, scale=-1.0))
                nc.scalar.activation(le[:, :], le[:, :], ACT.Ln, bias=c("one")[0:8, :]).then_inc(a2d, 1)
                act.wait_ge(d2a, 3)
                nc.scalar.activation(em[:, :, :, :], em[:, :, :, :], ACT.Exp, scale=1.0 / 16).then_inc(a2d, 1)
                for d in range(2):
                    act.wait_ge(d2a, 4 + d)
                    nc.scalar.activation(e[:, 0, :], z[:, d, :], ACT.Exp, scale=1.0 / 16)
                    nc.scalar.activation(e[:, 1, :], z[:, d, :], ACT.Exp, scale=-1.0 / 16).then_inc(a2d, 1)
                for d in range(2):
                    act.wait_ge(d2a, 6 + d)
                    nc.scalar.activation(stack[32:40, :], stack[32:40, :], ACT.Exp)
                    nc.scalar.activation(stack[64:72, :], stack[64:72, :], ACT.Exp, scale=-1.0)
                    nc.scalar.activation(stack[96:104, :], stack[96:104, :], ACT.Exp).then_inc(st_ready, 1)
                nc.scalar.activation(dec[:, :, :], dec[:, :, :], ACT.Exp).then_inc(a2d, 1)

            @block.vector
            def _(dve):
                step = Chain(dve, ch_d)
                dve.wait_ge(ld, 16 * 8)
                dve.wait_ge(zmm, 1)
                for d in range(2):
                    for g, (t0, n) in enumerate(GROUPS):
                        x = nc.vector.tensor_scalar(z[:, d, t0:t0 + n], ps[:, 3 * d + g, :n], blr[:, d:d + 1], None, ALU.add)
                step(x)
                nc.vector.scalar_tensor_tensor(out=e[:, :, :], in0=z[:, :, :], scalar=-1.0, in1=z[:, :, :], op0=ALU.mult, op1=ALU.max).then_inc(d2a, 1)
                nc.vector.tensor_scalar(M["ig"][:, :], FM[0:8, 8, :], gb[0:8, :], None, ALU.add)
                step(nc.vector.tensor_scalar(lf[:, :], FM[32:40, 8, :], gb[32:40, :], None, ALU.add))
                nc.vector.scalar_tensor_tensor(out=le[:, :], in0=lf[:, :], scalar=-1.0, in1=lf[:, :], op0=ALU.mult, op1=ALU.max).then_inc(d2a, 1)
                dve.wait_ge(a2d, 1)
                step(nc.vector.scalar_tensor_tensor(out=z[:, :, :], in0=z[:, :, :], scalar=0.0, in1=e[:, :, :], op0=ALU.min, op1=ALU.subtract))
                for n in range(NT):
                    t = slice(n * P, (n + 1) * P)
                    nc.vector.tensor_tensor_scan(e[:, 0, t], c("ones"), z[:, 0, t], 0.0, ALU.mult, ALU.add)
                    x = nc.vector.tensor_tensor_scan(e[:, 1, t][:, ::-1], c("ones"), z[:, 1, t][:, ::-1], 0.0, ALU.mult, ALU.add)
                step(x)
                for d, (mid, last) in enumerate(((63, 127), (64, 0))):
                    et = tiles(e[:, d, :])
                    nc.vector.tensor_copy(em[:, d, 0, :], et[:, :, mid])
                    nc.vector.tensor_copy(em[:, d, 1, :], et[:, :, last])
                    x = nc.vector.tensor_tensor(em[:, d, 2, :], et[:, :, last], et[:, :, mid], ALU.subtract)
                step(x)
                for d in range(2):
                    x = nc.vector.tensor_tensor(tiles(z[:, d, :]), tiles(e[:, d, :]), bc(em[:, d, 0, :], P), ALU.subtract)
                step(x)
                dve.sem_inc(d2a, 1)
                dve.sem_inc(d2a, 1)
                for d in range(2):
                    dve.wait_ge(a2d, 4 + d)
                    nc.vector.scalar_tensor_tensor(out=qd[:, d, :], in0=FM[:, 0, :], scalar=32.0 ** -0.5, in1=e[:, 0, :], op0=ALU.mult, op1=ALU.mult)
                    step(nc.vector.tensor_tensor(kd[:, d, :], FM[:, 1, :], e[:, 1, :], ALU.mult))
                    if d == 0:
                        dve.sem_inc(d2a, 1)
                step(nc.vector.scalar_tensor_tensor(out=lf[:, :], in0=lf[:, :], scalar=0.0, in1=le[:, :], op0=ALU.min, op1=ALU.subtract))
                step(nc.vector.tensor_tensor_scan(cum8[:, 0, :], ones8[:, :], lf[:, :], 0.0, ALU.mult, ALU.add))
                back = [(0, CTX), (CTX, T)]
                init = 0.0
                for a, b in back:
                    step(nc.vector.tensor_tensor_scan(cum8[:, 1, a:b][:, ::-1], ones8[:, a:b], lf[:, a:b][:, ::-1], init, ALU.mult, ALU.add))
                    init = cum8[:, 1, a:a + 1]
                for d in range(2):
                    if d == 1:
                        dve.wait_ge(trd, NT)
                    step(nc.vector.tensor_tensor(stack[0:8, :], M["ig"][:, :], cum8[:, d, :], ALU.subtract))
                    if d == 0:
                        step(nc.vector.tensor_tensor_scan(mx[:, 0, :], stack[0:8, :], stack[0:8, :], 0.0, ALU.max, ALU.max))
                    else:
                        init = 0.0
                        for a, b in back:
                            r = stack[0:8, a:b][:, ::-1]
                            step(nc.vector.tensor_tensor_scan(mx[:, 1, a:b][:, ::-1], r, r, init, ALU.max, ALU.max))
                            init = mx[:, 1, a:a + 1]
                    m3 = tiles(mx[:, d, :])
                    step(nc.vector.tensor_copy(mlast[:, d, :], m3[:, :, P - 1 if d == 0 else 0]))
                    first = order(d, 0)
                    nc.vector.memset(mprev[:, d, first:first + 1], 0.0)
                    if d == 0:
                        x = nc.vector.tensor_copy(mprev[:, 0, 1:NT], mlast[:, 0, 0:NT - 1])
                    else:
                        nc.vector.tensor_copy(mprev[:, 1, 0:1], mlast[:, 1, 1:2])
                        nc.vector.tensor_copy(mprev[:, 1, NT - 1:NT], mlast[:, 1, 0:1])
                        x = nc.vector.tensor_copy(mprev[:, 1, NCT:NT - 1], mlast[:, 1, NCT + 1:NT])
                    step(x)
                    nc.vector.tensor_tensor(dec[:, d, :], mprev[:, d, :], mlast[:, d, :], ALU.subtract)
                    nc.vector.tensor_tensor(tiles(stack[32:40, :]), bc(mprev[:, d, :], P), m3, ALU.subtract)
                    nc.vector.tensor_tensor(stack[64:72, :], cum8[:, d, :], mx[:, d, :], ALU.add)
                    step(nc.vector.tensor_tensor(tiles(stack[96:104, :]), tiles(stack[0:8, :]), bc(mlast[:, d, :], P), ALU.subtract))
                    dve.sem_inc(d2a, 1)
                    for n in range(NT):
                        q = d * NT + n
                        dve.wait_ge(trd, q + 1)
                        nc.vector.tensor_copy(tg[:, n, d, :, :], ps[:, 6 + q % 2, 0:P].rearrange("p (a r) -> p a r", r=32)[:, :, 0:8]).then_inc(tev, 1)
                dve.wait_ge(dmm, 1)
                step(nc.vector.tensor_copy(dcol[:, :, :], ps[:, 0, 0:4 * NT].rearrange("p (j n) -> p j n", n=NT)))
                dve.wait_ge(tev, 2 * NT)
                dve.wait_ge(a2d, 6)


def phase_conv(nc, io, S, l, FM, TM, M):
    src, dst = [2, 3, 4, 5], [0, 1, 6, 7]
    with Phase(nc, f"conv{l}") as ph:
        w = ph.sb("w", [P, 4, 9])
        ld, ch, cv, done, vx = (ph.sem(n) for n in ("loaded", "dve_step", "convolved", "silu_done", "v_ready"))
        with nc.Block() as block:

            @block.sync
            def _(sp):
                with nc.allow_non_contiguous_dma(reason="taps as columns"):
                    for j in range(4):
                        sp.dma_start(w[:, j, :], io["mlstm_conv"][l].rearrange("a b d -> (a b) d")[:, j * P:(j + 1) * P]
                                     .rearrange("t p -> p t")).then_inc(ld, 16)

            @block.vector
            def _(dve):
                step = Chain(dve, ch)
                dve.wait_ge(ld, 64)
                for j in range(4):
                    x, y = FM[:, src[j], :], FM[:, dst[j], :]
                    x2, y2 = (a[:, CTX:].rearrange("p (r c) -> p r c", c=GRID_W) for a in (x, y))
                    step(nc.vector.tensor_scalar(y, x, w[:, j, 4:5], None, ALU.mult))
                    for dr in (-1, 0, 1):
                        for dc in (-1, 0, 1):
                            if dr == 0 and dc == 0:
                                continue
                            r0, r1 = max(0, -dr), ROWS - max(0, dr)
                            c0, c1 = max(0, -dc), GRID_W - max(0, dc)
                            o = y2[:, r0:r1, c0:c1]
                            tap = w[:, j, 3 * (dr + 1) + dc + 1:3 * (dr + 1) + dc + 2]
                            step(nc.vector.scalar_tensor_tensor(out=o, in0=x2[:, r0 + dr:r1 + dr, c0 + dc:c1 + dc], scalar=tap,
                                                                in1=o, op0=ALU.mult, op1=ALU.add))
                            if dr == 0:
                                a, b = max(0, -dc), CTX - max(0, dc)
                                step(nc.vector.scalar_tensor_tensor(out=y[:, a:b], in0=x[:, a + dc:b + dc], scalar=tap,
                                                                    in1=y[:, a:b], op0=ALU.mult, op1=ALU.add))
                    dve.sem_inc(cv, 1)
                for j in range(2):
                    dve.wait_ge(done, j + 1)
                    step(nc.vector.tensor_scalar(FM[:, dst[j], :], FM[:, dst[j], :], HD ** -0.5, None, ALU.mult))

            @block.scalar
            def _(act):
                for j in range(4):
                    act.wait_ge(cv, j + 1)
                    nc.scalar.activation(FM[:, dst[j], :], FM[:, dst[j], :], ACT.Silu).then_inc(done, 1)
                act.wait_ge(done, 4)

            @block.gpsimd
            def _(pool):
                for n in range(NT):
                    nc.gpsimd.memset(M["vx"][:, n, :, HD:HD + 1], 1.0)
                    x = nc.gpsimd.tensor_copy(M["vx"][:, n, :, 0:HD], TM[:, n, 512:768].rearrange("p (h c) -> p h c", c=HD))
                x.then_inc(vx, 1)
                pool.wait_ge(vx, 1)


def phase_scan(nc, io, S, l, FM, TM, M):
    U = 2 * NT
    with Phase(nc, f"scan{l}") as ph:
        kdt = ph.sb("kdt", [P, 2, P])
        kw = ph.sb("kw", [P, 2, NH, HD])
        sg = ph.sb("sg", [P, 2, NH, P])
        ex = ph.sb("ex", [P, 2, NH, P])
        tmp = ph.sb("tmp", [P, NH, 65])
        num = ph.sb("num", [P, NH, 65])
        den = ph.sb("den", [P, NH])
        dsg = ph.sb("dsg", [P, 2 * P])
        dsm = ph.sb("dsm", [P, 2, 130])
        Sg = ph.sb("Sg", [P, 2, 2 * P])
        Sp = ph.sb("Sp", [P, 2, 2 * P])
        Sm = ph.sb("Sm", [P, 2, 2, 130])
        pe_tr, pe_mb, pe_sg, pe_sm, pe_og, pe_om, pe_u = (ph.sem(n) for n in (
            "transposed", "max_rows_done", "gla_scores_done", "mlstm_scores_done", "gla_out_done", "mlstm_out_done", "updates_done"))
        a_kdt, a_ex = ph.sem("kdt_ready"), ph.sem("ex_ready")
        g_q = ph.sem("masked_q_ready")
        qg = ph.sb("qg", [P, 2, NH, P])
        qm = ph.sb("qm", [P, 2, NH, P])
        v_init, v_kw, v_sg, v_w, v_og, v_om, v_st, ch = (ph.sem(n) for n in (
            "states_zero", "kw_ready", "gla_weights_ready", "mlstm_weights_ready", "gla_out_read", "mlstm_out_read", "states_ready", "dve_step"))
        ps, c = S["ps"], S["c"]
        mx, tg, dcol, qd, kd, em, vx, og, om = (M[k] for k in ("mx", "tg", "dcol", "qd", "kd", "em", "vx", "og", "om"))
        TR, SG, OG, KT, MB, SM, OI, OC = range(8)
        mq, mk = (0, 1), (6, 7)
        sel8 = c("sel8").rearrange("p (a t) -> p a t", t=P)

        def unit(u):
            d = u % 2
            n = order(d, u // 2)
            return d, n, slice(n * P, (n + 1) * P)

        with nc.Block() as block:

            @block.tensor
            def _(pe):
                for u in range(U):
                    d, n, t = unit(u)
                    if u >= 1:
                        pe.wait_ge(a_kdt, u)
                        pe.wait_ge(v_kw, u)
                    nc.tensor.transpose(ps[:, KT, 0:P], kd[:, d, t], c("ident"))
                    for j in range(2):
                        x = nc.tensor.transpose(ps[:, TR, (j + 1) * P:(j + 2) * P], FM[:, mk[j], t], c("ident"))
                    x.then_inc(pe_tr, 1)
                    if u >= 1:
                        pe.wait_ge(a_ex, u)
                    nc.tensor.matmul(ps[:, MB, :], c("ident"), c("negF" if d == 0 else "negB"), start=True, stop=False, skip_group_check=True)
                    for h in range(NH):
                        x = nc.tensor.matmul(ps[:, MB, h * P:(h + 1) * P], sel8[0:8, 4 * d + h, :], mx[:, d, t],
                                             start=False, stop=(h == NH - 1), skip_group_check=True)
                    x.then_inc(pe_mb, 1)
                    if u >= 1:
                        pe.wait_ge(v_w, u)
                    pe.wait_ge(g_q, u + 1)
                    for j in range(2):
                        x = nc.tensor.matmul(ps[:, SM, j * 256:(j + 1) * 256], FM[:, mk[j], t],
                                             qm[:, d, 2 * j:2 * j + 2, :].rearrange("p a b -> p (a b)"), start=True, stop=True)
                    x.then_inc(pe_sm, 1)
                    if u >= 1:
                        pe.wait_ge(v_st, u)
                    else:
                        pe.wait_ge(v_init, 1)
                    nc.tensor.matmul(ps[:, SG, :], kd[:, d, t], qg[:, d, :, :].rearrange("p a b -> p (a b)"),
                                     start=True, stop=True).then_inc(pe_sg, 1)
                    if u >= 1:
                        pe.wait_ge(v_og, u)
                        pe.wait_ge(v_om, u)
                    nc.tensor.matmul(ps[:, OG, 0:256], qd[:, d, t], Sp[:, d, :], start=True, stop=False, skip_group_check=True)
                    for j in range(2):
                        nc.tensor.matmul(ps[:, OC, j * 130:(j + 1) * 130], FM[:, mq[j], t], Sm[:, d, j, :], start=True, stop=True)
                    pe.wait_ge(v_sg, u + 1)
                    for h in range(NH):
                        x = nc.tensor.matmul(ps[:, OG, h * HD:(h + 1) * HD], sg[:, d, h, :], TM[:, n, h * HD:(h + 1) * HD],
                                             start=False, stop=(h == NH - 1), skip_group_check=True)
                    x.then_inc(pe_og, 1)
                    pe.wait_ge(v_w, u + 1)
                    for h in range(NH):
                        x = nc.tensor.matmul(ps[:, OI, h * 65:(h + 1) * 65], ex[:, d, h, :], vx[:, n, h, :], start=True, stop=True)
                    x.then_inc(pe_om, 1)
                    pe.wait_ge(a_kdt, u + 1)
                    pe.wait_ge(v_og, u + 1)
                    nc.tensor.matmul(ps[:, OG, 256:512], kdt[:, d, :], TM[:, n, 0:256], start=True, stop=True)
                    pe.wait_ge(v_kw, u + 1)
                    for j in range(2):
                        x = nc.tensor.matmul(ps[:, SG, j * 130:(j + 1) * 130], kw[:, d, 2 * j:2 * j + 2, :].rearrange("p a b -> p (a b)"),
                                             vx[:, n, 2 * j:2 * j + 2, :].rearrange("p a b -> p (a b)"), start=True, stop=True)
                    x.then_inc(pe_u, 1)

            @block.scalar
            def _(act):
                for u in range(U):
                    d, n, t = unit(u)
                    if u >= 2:
                        act.wait_ge(pe_u, u - 1)
                    act.wait_ge(pe_tr, u + 1)
                    nc.scalar.copy(kdt[:, d, :], ps[:, KT, 0:P]).then_inc(a_kdt, 1)
                    act.wait_ge(pe_mb, u + 1)
                    for h in range(NH):
                        x = nc.scalar.activation(ex[:, d, h, :], ps[:, MB, h * P:(h + 1) * P], ACT.Exp,
                                                 bias=tg[:, n, d, 0, 4 * d + h:4 * d + h + 1], scale=-1.0)
                    x.then_inc(a_ex, 1)

            @block.gpsimd
            def _(pool):
                for u in range(U):
                    d, n, t = unit(u)
                    if u >= 2:
                        pool.wait_ge(pe_sm, u - 1)
                        pool.wait_ge(pe_sg, u - 1)
                    nc.gpsimd.tensor_tensor(qg[:, d, :, :], qd[:, d, t].unsqueeze(1).to_broadcast([P, NH, P]), bc(c("row4"), P), ALU.mult)
                    for j in range(2):
                        x = nc.gpsimd.tensor_tensor(qm[:, d, 2 * j:2 * j + 2, :], FM[:, mq[j], t].unsqueeze(1).to_broadcast([P, 2, P]),
                                                    bc(c("row2"), P), ALU.mult)
                    x.then_inc(g_q, 1)

            @block.vector
            def _(dve):
                step = Chain(dve, ch)
                nc.vector.memset(sg[:, :, :, :], 0.0)
                nc.vector.memset(Sg[:, :, :], 0.0)
                nc.vector.memset(Sp[:, :, :], 0.0)
                nc.vector.memset(Sm[:, :, :, :], 0.0).then_inc(v_init, 1)
                dve.wait_ge(v_init, 1)
                keep = [c("keepF"), c("keepB")]
                written = set()
                for u in range(U):
                    d, n, t = unit(u)
                    h8 = slice(4 * d, 4 * d + 4)
                    if u >= 2:
                        dve.wait_ge(pe_u, u - 1)
                    dve.wait_ge(pe_tr, u + 1)
                    nc.vector.tensor_tensor(kw[:, d, :, :], ps[:, TR, P:3 * P].rearrange("p (h c) -> p h c", c=HD),
                                            bc(tg[:, n, d, 3, h8], HD), ALU.mult).then_inc(v_kw, 1)
                    dve.wait_ge(pe_sg, u + 1)
                    nc.vector.copy_predicated(sg[:, d, :, :], keep[d].bitcast(I32).unsqueeze(1).to_broadcast([P, NH, P]),
                                              ps[:, SG, :].rearrange("p (h t) -> p h t", t=P)).then_inc(v_sg, 1)
                    dve.wait_ge(a_ex, u + 1)
                    dve.wait_ge(pe_sm, u + 1)
                    nc.vector.tensor_tensor(ex[:, d, :, :], ex[:, d, :, :], ps[:, SM, :].rearrange("p (h t) -> p h t", t=P), ALU.mult).then_inc(v_w, 1)
                    dve.wait_ge(pe_og, u + 1)
                    if n in written:
                        nc.vector.tensor_tensor(og[:, n, :], og[:, n, :], ps[:, OG, 0:256], ALU.add).then_inc(v_og, 1)
                    else:
                        nc.vector.tensor_copy(og[:, n, :], ps[:, OG, 0:256]).then_inc(v_og, 1)
                    dve.wait_ge(pe_om, u + 1)
                    step(nc.vector.tensor_tensor(tmp[:, :, :], ps[:, OC, 0:260].rearrange("p (h c) -> p h c", c=65),
                                                 bc(tg[:, n, d, 1, h8], 65), ALU.mult))
                    nc.vector.tensor_tensor(num[:, :, :], tmp[:, :, :], ps[:, OI, 0:260].rearrange("p (h c) -> p h c", c=65),
                                            ALU.add).then_inc(v_om, 1)
                    dve.wait_ge(v_om, u + 1)
                    step(nc.vector.scalar_tensor_tensor(out=den[:, :], in0=num[:, :, 64], scalar=-1.0, in1=num[:, :, 64],
                                                        op0=ALU.mult, op1=ALU.max))
                    step(nc.vector.tensor_tensor(den[:, :], den[:, :], tg[:, n, d, 2, h8], ALU.max))
                    step(nc.vector.reciprocal(den[:, :], den[:, :]))
                    on = om[:, n, :].rearrange("p (h c) -> p h c", c=HD)
                    if n in written:
                        step(nc.vector.tensor_tensor(tmp[:, :, 0:HD], num[:, :, 0:HD], bc(den[:, :], HD), ALU.mult))
                        nc.vector.tensor_tensor(on, on, tmp[:, :, 0:HD], ALU.add)
                    else:
                        nc.vector.tensor_tensor(on, num[:, :, 0:HD], bc(den[:, :], HD), ALU.mult)
                    written.add(n)
                    dve.wait_ge(pe_u, u + 1)
                    nc.vector.scalar_tensor_tensor(out=dsg[:, :], in0=ps[:, OG, 256:512], scalar=em[:, d, 2, n:n + 1], in1=c("blockg"),
                                                   op0=ALU.mult, op1=ALU.mult)
                    nc.vector.tensor_tensor(dsm[:, :, :], ps[:, SG, 0:260].rearrange("p (a b) -> p a b", b=130),
                                            c("blockm").unsqueeze(1).to_broadcast([P, 2, 130]), ALU.mult)
                    step(nc.vector.tensor_tensor(Sm[:, d, :, :], Sm[:, d, :, :], bc(dcol[:, 2 * d:2 * d + 2, n], 130), ALU.mult))
                    step(nc.vector.scalar_tensor_tensor(out=Sg[:, d, :], in0=Sg[:, d, :], scalar=em[:, d, 1, n:n + 1], in1=dsg[:, :],
                                                        op0=ALU.mult, op1=ALU.add))
                    nc.vector.tensor_tensor(Sm[:, d, :, :], Sm[:, d, :, :], dsm[:, :, :], ALU.add)
                    nn = order(d, min(u // 2 + 1, NT - 1))
                    nc.vector.tensor_scalar(Sp[:, d, :], Sg[:, d, :], em[:, d, 0, nn:nn + 1], None, ALU.mult).then_inc(v_st, 1)
                    dve.wait_ge(v_st, u + 1)


def phase_mix_out(nc, io, S, l, TM, M, ctx_out):
    t0 = 0 if ctx_out else NCT
    tiles = list(range(t0, NT))
    with Phase(nc, f"mix{l}") as ph:
        sq = ph.sb("sq", [P, NT, 256])
        ms = ph.sb("ms", [P, NT, NH])
        ng = ph.sb("ng", [P, 256])
        turned = ph.sb("turned", [P, 2, 6, P])
        ld, ch, var, sd, gates, sqd, gd, gm, tr, ev, st = (ph.sem(n) for n in (
            "loaded", "dve_step", "var_ready", "sd_ready", "gates_ready", "squared", "gla_ready", "mlstm_ready", "transposed", "turned_ready", "stored"))
        ps, ident, og, om = S["ps"], S["c"]("ident"), M["og"], M["om"]
        with nc.Block() as block:

            @block.sync
            def _(sp):
                sp.dma_start(ng[:, :], io["gla_norm_g"][l].rearrange("(a n) -> a n", a=1).to_broadcast([P, 256])).then_inc(ld, 16)
                for i, n in enumerate(tiles):
                    sp.wait_ge(ev, i + 1)
                    sp.dma_start(S["mixT_d"][:, 0:6, n * P:(n + 1) * P], turned[:, i % 2, :, :]).then_inc(st, 16)
                    sp.wait_ge(st, 16 * (i + 1))

            @block.scalar
            def _(act):
                nc.scalar.activation(sq[:, t0:, :], og[:, t0:, :], ACT.Square).then_inc(sqd, 1)
                nc.scalar.activation(TM[:, t0:, 768:1024], TM[:, t0:, 768:1024], ACT.Sigmoid).then_inc(gates, 1)
                nc.scalar.activation(TM[:, t0:, 256:512], TM[:, t0:, 256:512], ACT.Silu).then_inc(gates, 1)
                act.wait_ge(var, 1)
                nc.scalar.activation(ms[:, t0:, :], ms[:, t0:, :], ACT.Sqrt).then_inc(sd, 1)

            @block.gpsimd
            def _(pool):
                pool.wait_ge(gates, 1)
                nc.gpsimd.tensor_tensor(om[:, t0:, :], om[:, t0:, :], TM[:, t0:, 768:1024], ALU.mult).then_inc(gm, 1)

            @block.vector
            def _(dve):
                step = Chain(dve, ch)
                dve.wait_ge(sqd, 1)
                step(nc.vector.tensor_reduce(ms[:, t0:, :], sq[:, t0:, :].rearrange("p n (h c) -> p n h c", c=HD), AX.X, ALU.add))
                nc.vector.tensor_scalar(ms[:, t0:, :], ms[:, t0:, :], 1.0 / HD, EPS, ALU.mult, ALU.add).then_inc(var, 1)
                dve.wait_ge(sd, 1)
                step(nc.vector.reciprocal(ms[:, t0:, :], ms[:, t0:, :]))
                dve.wait_ge(ld, 16)
                dve.wait_ge(gates, 2)
                for n in tiles:
                    o = og[:, n, :].rearrange("p (h c) -> p h c", c=HD)
                    step(nc.vector.tensor_tensor(o, o, bc(ms[:, n, :], HD), ALU.mult))
                    step(nc.vector.tensor_tensor(og[:, n, :], og[:, n, :], ng[:, :], ALU.mult))
                    nc.vector.tensor_tensor(og[:, n, :], og[:, n, :], TM[:, n, 256:512], ALU.mult).then_inc(gd, 1)
                for i, n in enumerate(tiles):
                    dve.wait_ge(tr, i + 1)
                    if i >= 2:
                        dve.wait_ge(st, 16 * (i - 1))
                    nc.vector.tensor_copy(turned[:, i % 2, :, :].rearrange("p k t -> p (k t)"),
                                          ps[:, 2 * (i % 2):2 * (i % 2) + 2, :].rearrange("p b t -> p (b t)")[:, 0:6 * P]).then_inc(ev, 1)

            @block.tensor
            def _(pe):
                pe.wait_ge(gm, 1)
                for i, n in enumerate(tiles):
                    pe.wait_ge(gd, i + 1)
                    if i >= 2:
                        pe.wait_ge(ev, i - 1)
                    for k in range(6):
                        src = (og, om)[k // 2][:, n, (k % 2) * P:(k % 2 + 1) * P] if k < 4 else TM[:, n, 1024 + (k - 4) * P:1024 + (k - 3) * P]
                        x = nc.tensor.transpose(ps[:, 2 * (i % 2) + k // 4, (k % 4) * P:(k % 4 + 1) * P], src, ident)
                    x.then_inc(tr, 1)


def phase_out_proj(nc, io, S, l, groups):
    with Phase(nc, f"op{l}") as ph:
        xT = ph.sb("xT", [P, KD, T])
        mT = ph.sb("mT", [P, KD, T])
        w = ph.sb("w", [P, KD, D])
        ld, mm_done, done, st = (ph.sem(n) for n in ("loaded", "mm_done", "added", "stored"))
        ps, mod = S["ps"], S["mod"]
        a = groups[0][0]
        units = [(d, t0, n) for d in range(KD) for t0, n in groups]
        with nc.Block() as block:

            @block.sync
            def _(sp):
                sp.dma_start(w[:, :, :], io["w_out"][l].rearrange("(k p) n -> p k n", p=P)).then_inc(ld, 16)
                sp.dma_start(mT[:, :, a:], S["mixT_d"][:, :, a:]).then_inc(ld, 16)
                sp.dma_start(xT[:, :, a:], S["xT_d"][:, :, a:]).then_inc(ld, 16)
                for d in range(KD):
                    sp.wait_ge(done, (d + 1) * len(groups))
                    sp.dma_start(S["xT_d"][:, d, a:], xT[:, d, a:]).then_inc(st, 16)
                sp.wait_ge(st, 16 * KD)

            @block.tensor
            def _(pe):
                pe.wait_ge(ld, 48)
                for u, (d, t0, n) in enumerate(units):
                    if u >= 8:
                        pe.wait_ge(done, u - 7)
                    for k in range(KD):
                        x = nc.tensor.matmul(ps[:, u % 8, :n], w[:, k, d * P:(d + 1) * P], mT[:, k, t0:t0 + n], start=(k == 0), stop=(k == KD - 1))
                    x.then_inc(mm_done, 1)

            @block.vector
            def _(dve):
                dve.wait_ge(ld, 48)
                for u, (d, t0, n) in enumerate(units):
                    dve.wait_ge(mm_done, u + 1)
                    j = 1 if t0 < CTX else 0
                    nc.vector.scalar_tensor_tensor(out=xT[:, d, t0:t0 + n], in0=ps[:, u % 8, :n], scalar=mod[:, l, 16 + d, j:j + 1],
                                                   in1=xT[:, d, t0:t0 + n], op0=ALU.mult, op1=ALU.add).then_inc(done, 1)


def phase_ffn_up(nc, io, S, hT, aT):
    NC = DFF // P
    with Phase(nc, "up") as ph:
        wg = ph.sb("wg", [P, 2, KD, P])
        wu = ph.sb("wu", [P, 2, KD, P])
        sil = ph.sb("sil", [P, 3, 512])
        wl = [ph.sem(f"w_loaded{s}") for s in range(2)]
        wfree, g_done, u_done, silu_ready, used = (ph.sem(n) for n in ("w_slot_free", "gate_done", "up_done", "silu_ready", "banks_free"))
        ps = S["ps"]
        gsrc, usrc = (io[n][0].rearrange("(k p) n -> p k n", p=P) for n in ("ffn_w_gate", "ffn_w_up"))
        with nc.Block() as block:

            @block.sync
            def _(sp):
                with sp.Fori(0, NC // 2) as i:
                    for s in range(2):
                        sp.wait_ge(wfree, i * 2 + (s + 1))
                        sp.dma_start(wg[:, s, :, :], gsrc[:, :, bass.ds(i * 256 + s * P, P)]).then_inc(wl[s], 16)
                        sp.dma_start(wu[:, s, :, :], usrc[:, :, bass.ds(i * 256 + s * P, P)]).then_inc(wl[s], 16)

            @block.tensor
            def _(pe):
                pe.sem_inc(wfree, 2)
                with pe.Fori(0, NC // 2) as i:
                    for s in range(2):
                        pe.wait_ge(wl[s], i * 32 + 32)
                        for g, (t0, n) in enumerate(GROUPS):
                            pe.wait_ge(used, i * 6 + (3 * s + g + 1))
                            for k in range(KD):
                                x = nc.tensor.matmul(ps[:, 2 * g, :n], wg[:, s, k, :], hT[:, k, t0:t0 + n], start=(k == 0), stop=(k == KD - 1))
                            x.then_inc(g_done, 1)
                            for k in range(KD):
                                x = nc.tensor.matmul(ps[:, 2 * g + 1, :n], wu[:, s, k, :], hT[:, k, t0:t0 + n], start=(k == 0), stop=(k == KD - 1))
                            x.then_inc(u_done, 1)
                        pe.wait_ge(u_done, i * 6 + 3 * (s + 1))
                        pe.sem_inc(wfree, 1)

            @block.scalar
            def _(act):
                with act.Fori(0, NC // 2) as i:
                    for s in range(2):
                        for g, (t0, n) in enumerate(GROUPS):
                            act.wait_ge(g_done, i * 6 + (3 * s + g + 1))
                            act.wait_ge(used, i * 6 + (3 * s + g + 1))
                            nc.scalar.activation(sil[:, g, :n], ps[:, 2 * g, :n], ACT.Silu).then_inc(silu_ready, 1)

            @block.vector
            def _(dve):
                dve.sem_inc(used, 3)
                with dve.Fori(0, NC // 2) as i:
                    for s in range(2):
                        for g, (t0, n) in enumerate(GROUPS):
                            dve.wait_ge(silu_ready, i * 6 + (3 * s + g + 1))
                            dve.wait_ge(u_done, i * 6 + (3 * s + g + 1))
                            nc.vector.tensor_tensor(aT[:, bass.ds(i * (2 * T) + (s * T + t0), n)], sil[:, g, :n], ps[:, 2 * g + 1, :n],
                                                    ALU.mult).then_inc(used, 1)
                dve.wait_ge(used, 3 * NC + 3)


def phase_ffn_down(nc, io, S, aT):
    NC = DFF // P
    with Phase(nc, "down") as ph:
        wd = ph.sb("wd", [P, 2, NC, P])
        xs = ph.sb("xs", [P, 2, T])
        wl = [ph.sem(f"w_loaded{s}") for s in range(2)]
        st = [ph.sem(f"stored{s}") for s in range(2)]
        mm_done, added = ph.sem("mm_done"), ph.sem("added")
        ps, mod = S["ps"], S["mod"]
        src = io["ffn_w_down"][0].rearrange("(f p) n -> p f n", p=P)
        with nc.Block() as block:

            @block.sync
            def _(sp):
                for d in range(KD):
                    s = d % 2
                    if d >= 2:
                        sp.wait_ge(mm_done, 3 * (d - 1))
                        sp.wait_ge(st[s], 16 * (d // 2))
                    sp.dma_start(wd[:, s, :, :], src[:, :, d * P:(d + 1) * P]).then_inc(wl[s], 16)
                    sp.dma_start(xs[:, s, :], S["xT_d"][:, d, :]).then_inc(wl[s], 16)

            @block.tensor
            def _(pe):
                for d in range(KD):
                    s = d % 2
                    pe.wait_ge(wl[s], 32 * (d // 2 + 1))
                    for g, (t0, n) in enumerate(GROUPS):
                        if d >= 2:
                            pe.wait_ge(added, 3 * (d - 2) + g + 1)
                        for f in range(NC):
                            x = nc.tensor.matmul(ps[:, 3 * s + g, :n], wd[:, s, f, :], aT[:, f * T + t0:f * T + t0 + n],
                                                 start=(f == 0), stop=(f == NC - 1))
                        x.then_inc(mm_done, 1)

            @block.vector
            def _(dve):
                for d in range(KD):
                    s = d % 2
                    dve.wait_ge(wl[s], 32 * (d // 2 + 1))
                    for g, (t0, n) in enumerate(GROUPS):
                        dve.wait_ge(mm_done, 3 * d + g + 1)
                        j = 1 if t0 < CTX else 0
                        nc.vector.scalar_tensor_tensor(out=xs[:, s, t0:t0 + n], in0=ps[:, 3 * s + g, :n], scalar=mod[:, 0, 40 + d, j:j + 1],
                                                       in1=xs[:, s, t0:t0 + n], op0=ALU.mult, op1=ALU.add).then_inc(added, 1)

            @block.scalar
            def _(act):
                for d in range(KD):
                    s = d % 2
                    act.wait_ge(added, 3 * (d + 1))
                    act.dma_start(S["xT_d"][:, d, :], xs[:, s, :]).then_inc(st[s], 16)
                for s in range(2):
                    act.wait_ge(st[s], 16 * (KD // 2))


def phase_route(nc, io, S, hT, R):
    NX = SEQ // P
    with Phase(nc, "route") as ph:
        wr = ph.sb("wr", [P, KD, NE])
        L = ph.sb("L", [P, NX, NE])
        sel = ph.sb("sel", [P, 2, NX, NE])
        both = ph.sb("both", [P, NX, NE])
        t = ph.sb("t", [P, NX, NE])
        m = ph.sb("m", [P, 2, NX])
        r = ph.sb("r", [P, NX])
        cnt = ph.sb("cnt", [P, NE])
        ind = ph.sb("ind", [P, NE, NE])
        nb = ph.sb("nb", [P, NE])
        end = ph.sb("end", [P, NE])
        start = ph.sb("start", [P, NE])
        indb = ph.sb("indb", [P, NBLK, NE])
        ebf = ph.sb("ebf", [P, NBLK])
        slotf = ph.sb("slotf", [P, 2, NX])
        ex = ph.sb("ex", [P, NX])
        rows = ph.sb("rows", [P, 2, D])
        zero = ph.sb("zero", [P, D])
        wl, zr, zf, lg, ch, sel_ready, pre, dif, exr, slots, tr, rv, g2s = (ph.sem(n) for n in (
            "router_loaded", "zero_ready", "slots_zeroed", "logits_done", "dve_step", "choice_ready", "ranks_done", "gap_ready", "exp_ready",
            "slots_ready", "rows_transposed", "rows_ready", "g2_stored"))
        sc = [ph.sem(f"scattered{s}") for s in range(2)]
        ps, c = S["ps"], S["c"]
        with nc.Block() as block:

            @block.sync
            def _(sp):
                sp.dma_start(wr[:, :, :], io["moe_router"][0].rearrange("(k p) e -> p k e", p=P)).then_inc(wl, 16)
                sp.wait_ge(zr, 1)
                sp.dma_start(S["xs_d"].rearrange("(b p) d -> p b d", p=P), zero[:, :].unsqueeze(1).to_broadcast([P, NBLK + 1, D])).then_inc(zf, 16)
                with nc.allow_non_contiguous_dma(reason="a column set as a vector"):
                    sp.dma_start(cols(S["g2_d"]), S["mod"][:, 1, 40:48, 0]).then_inc(g2s, 16)
                sp.wait_ge(g2s, 16)

            @block.tensor
            def _(pe):
                pe.wait_ge(wl, 16)
                for n in range(NX):
                    for k in range(KD):
                        x = nc.tensor.matmul(ps[:, 0, n * NE:(n + 1) * NE], hT[:, k, CTX + n * P:CTX + (n + 1) * P], wr[:, k, :],
                                             start=(k == 0), stop=(k == KD - 1))
                x.then_inc(lg, 1)
                pe.wait_ge(sel_ready, 1)
                for n in range(NX):
                    for i in range(n + 1):
                        nc.tensor.matmul(ps[:, 1, n * NE:(n + 1) * NE], c("tri") if i == n else c("ones"), both[:, i, :], start=(i == 0), stop=(i == n))
                for i in range(NX):
                    x = nc.tensor.matmul(ps[:, 2, 0:NE], c("ones"), both[:, i, :], start=(i == 0), stop=(i == NX - 1))
                x.then_inc(pre, 1)
                for n in range(NX):
                    if n >= 2:
                        pe.wait_ge(rv, n - 1)
                    for k in range(KD):
                        b = 4 + 2 * (n % 2) + k // 4
                        x = nc.tensor.transpose(ps[:, b, (k % 4) * P:(k % 4 + 1) * P], hT[:, k, CTX + n * P:CTX + (n + 1) * P], c("ident"))
                    x.then_inc(tr, 1)

            @block.vector
            def _(dve):
                step = Chain(dve, ch)
                pref = c("pref").unsqueeze(1).to_broadcast([P, NX, NE])
                dve.wait_ge(lg, 1)
                step(nc.vector.tensor_copy(L[:, :, :], ps[:, 0, 0:NX * NE].rearrange("p (n e) -> p n e", e=NE)))
                for i in range(2):
                    step(nc.vector.tensor_reduce(m[:, i, :], L[:, :, :], AX.X, ALU.max))
                    step(nc.vector.tensor_tensor(t[:, :, :], L[:, :, :], bc(m[:, i, :], NE), ALU.is_equal))
                    step(nc.vector.tensor_tensor(t[:, :, :], t[:, :, :], pref, ALU.mult))
                    step(nc.vector.tensor_reduce(r[:, :], t[:, :, :], AX.X, ALU.max))
                    step(nc.vector.tensor_tensor(sel[:, i, :, :], pref, bc(r[:, :], NE), ALU.is_equal))
                    if i == 0:
                        step(nc.vector.scalar_tensor_tensor(out=L[:, :, :], in0=sel[:, 0, :, :], scalar=-BIG, in1=L[:, :, :], op0=ALU.mult, op1=ALU.add))
                nc.vector.tensor_tensor(both[:, :, :], sel[:, 0, :, :], sel[:, 1, :, :], ALU.add).then_inc(sel_ready, 1)
                nc.vector.tensor_tensor(ex[:, :], m[:, 1, :], m[:, 0, :], ALU.subtract).then_inc(dif, 1)
                dve.wait_ge(exr, 1)
                step(nc.vector.tensor_scalar(r[:, :], ex[:, :], 1.0, None, ALU.add))
                step(nc.vector.reciprocal(R["gate"][:, 0, :], r[:, :]))
                step(nc.vector.tensor_tensor(R["gate"][:, 1, :], R["gate"][:, 0, :], ex[:, :], ALU.mult))
                dve.wait_ge(pre, 1)
                step(nc.vector.tensor_copy(cnt[:, :], ps[:, 2, 0:NE]))
                step(nc.vector.tensor_tensor(ind[:, :, :], bc(cnt[:, :], NE), c("koff").unsqueeze(1).to_broadcast([P, NE, NE]), ALU.is_gt))
                step(nc.vector.tensor_reduce(nb[:, :], ind[:, :, :], AX.X, ALU.add))
                step(nc.vector.tensor_tensor_scan(end[:, :], c("ones")[:, 0:NE], nb[:, :], 0.0, ALU.mult, ALU.add))
                step(nc.vector.tensor_tensor(start[:, :], end[:, :], nb[:, :], ALU.subtract))
                step(nc.vector.tensor_scalar(start[:, :], start[:, :], float(P), None, ALU.mult))
                step(nc.vector.tensor_tensor(t[:, :, :], ps[:, 1, 0:NX * NE].rearrange("p (n e) -> p n e", e=NE),
                                             start[:, :].unsqueeze(1).to_broadcast([P, NX, NE]), ALU.add))
                for i in range(2):
                    step(nc.vector.tensor_tensor(sel[:, i, :, :], sel[:, i, :, :], t[:, :, :], ALU.mult))
                    step(nc.vector.tensor_reduce(slotf[:, i, :], sel[:, i, :, :], AX.X, ALU.add))
                step(nc.vector.tensor_tensor(indb[:, :, :], bc(c("blk"), NE), end[:, :].unsqueeze(1).to_broadcast([P, NBLK, NE]), ALU.is_ge))
                step(nc.vector.tensor_reduce(ebf[:, :], indb[:, :, :], AX.X, ALU.add))
                step(nc.vector.tensor_scalar(ebf[:, :], ebf[:, :], float(NE - 1), None, ALU.min))
                step(nc.vector.tensor_copy(R["expert"][:, :], ebf[:, :]))
                nc.vector.tensor_copy(R["slot"][:, :, :], slotf[:, :, :]).then_inc(slots, 1)
                for n in range(NX):
                    dve.wait_ge(tr, n + 1)
                    if n >= 2:
                        dve.wait_ge(sc[n % 2], 32 * (n // 2))
                    nc.vector.tensor_copy(rows[:, n % 2, :], ps[:, 4 + 2 * (n % 2):6 + 2 * (n % 2), :].rearrange("p b t -> p (b t)")).then_inc(rv, 1)

            @block.scalar
            def _(act):
                act.wait_ge(dif, 1)
                nc.scalar.activation(ex[:, :], ex[:, :], ACT.Exp).then_inc(exr, 1)

            @block.gpsimd
            def _(pool):
                nc.gpsimd.memset(zero[:, :], 0.0).then_inc(zr, 1)
                pool.wait_ge(zf, 16)
                pool.wait_ge(slots, 1)
                for n in range(NX):
                    pool.wait_ge(rv, n + 1)
                    for i in range(2):
                        nc.gpsimd.indirect_dma_start(
                            out=S["xs_d"][:, :], out_offset=bass.IndirectOffsetOnAxis(ap=R["slot"][:, i, n:n + 1], axis=0),
                            in_=rows[:, n % 2, :], in_offset=None).then_inc(sc[n % 2], 16)
                for s in range(2):
                    pool.wait_ge(sc[s], 32 * (NX // 2))


def phase_experts(nc, io, S, R):
    RING = 7
    seq = [("g", 0), ("u", 0)]
    for j in range(1, NFG):
        seq += [("g", j), ("u", j), ("d", j - 1)]
    seq.append(("d", NFG - 1))
    NW = len(seq)
    pos = {x: i for i, x in enumerate(seq)}
    with Phase(nc, "moe") as ph:
        ring = ph.sb("ring", [P, RING, 4096])
        rows = ph.sb("rows", [P, D])
        xT = ph.sb("xT", [P, KD, P])
        sil = ph.sb("sil", [P, FG])
        prod = ph.sb("prod", [P, FG])
        pT = ph.sb("pT", [P, FG])
        y = ph.sb("y", [P, D])
        wl = [ph.sem(f"w_loaded{s}") for s in range(RING)]
        used, silu, prodr, tr, tev, xl, xtr, xev, ydone, yev, yst, yfree = (ph.sem(n) for n in (
            "products_done", "silu_done", "product_ready", "product_transposed", "turned_ready", "rows_loaded", "rows_transposed", "rows_turned",
            "y_done", "y_read", "y_stored", "y_free"))
        ps, ident = S["ps"], S["c"]("ident")
        G, Uk, TB, Y0, X0 = 0, 1, 2, 3, 5
        gw, uw, dw = io["moe_w_gate"][0], io["moe_w_up"][0], io["moe_w_down"][0]
        xs_b = S["xs_d"].rearrange("(b p) d -> b p d", p=P)
        ys_b = S["ys_d"].rearrange("(b p) d -> b p d", p=P)
        with nc.Block() as block:

            @block.sync
            def _(sp):
                with sp.Fori(0, NBLK) as b:
                    e = sp.value_load(R["expert"][0:1, bass.ds(b, 1)], min_val=0, max_val=NE - 1)
                    for i, (kind, j) in enumerate(seq):
                        s = i % RING
                        sp.wait_ge(used, b * NW + (i + 1))
                        if kind == "d":
                            dst = ring[:, s, :].rearrange("p (f n) -> p f n", n=D)
                            src = dw[bass.ds(e, 1), j * FG:(j + 1) * FG, :].rearrange("a (f p) n -> p (a f) n", p=P)
                        else:
                            dst = ring[:, s, :].rearrange("p (k n) -> p k n", n=FG)
                            src = (gw if kind == "g" else uw)[bass.ds(e, 1), :, j * FG:(j + 1) * FG].rearrange("a (k p) n -> p (a k) n", p=P)
                        sp.dma_start(dst, src).then_inc(wl[s], 16)

            @block.gpsimd
            def _(pool):
                pool.sem_inc(yfree, 1)
                pool.dma_start(rows[:, :], xs_b[0, :, :]).then_inc(xl, 16)
                with pool.Fori(0, NBLK) as b:
                    pool.wait_ge(xtr, b + 1)
                    pool.dma_start(rows[:, :], xs_b[bass.ds(b + 1, 1), :, :].rearrange("a p d -> (a p) d")).then_inc(xl, 16)
                    pool.wait_ge(yev, b + 2)
                    pool.dma_start(ys_b[bass.ds(b, 1), :, :].rearrange("a p d -> (a p) d"), y[:, :]).then_inc(yst, 16)
                    pool.wait_ge(yst, b * 16 + 16)
                    pool.sem_inc(yfree, 1)
                pool.wait_ge(xl, 16 * (NBLK + 1))

            @block.tensor
            def _(pe):
                pe.sem_inc(used, RING)

                def turn_rows():
                    for k in range(KD):
                        x = nc.tensor.transpose(ps[:, X0 + k // 4, (k % 4) * P:(k % 4 + 1) * P], rows[:, k * P:(k + 1) * P], ident)
                    x.then_inc(xtr, 1)

                pe.wait_ge(xl, 16)
                turn_rows()
                with pe.Fori(0, NBLK) as b:

                    def arrived(kind, j):
                        i = pos[kind, j]
                        pe.wait_ge(wl[i % RING], b * (16 * (NW // RING)) + 16 * (i // RING + 1))
                        return ring[:, i % RING, :]

                    def up(kind, j, bank):
                        w = arrived(kind, j).rearrange("p (k n) -> p k n", n=FG)
                        for k in range(KD):
                            x = nc.tensor.matmul(ps[:, bank, :], xT[:, k, :], w[:, k, :], start=(k == 0), stop=(k == KD - 1))
                        x.then_inc(used, 1)

                    def turn_product(j):
                        pe.wait_ge(prodr, b * NFG + (j + 2))
                        pe.wait_ge(tev, b * NFG + (j + 1))
                        for f in range(FG // P):
                            x = nc.tensor.transpose(ps[:, TB, f * P:(f + 1) * P], prod[:, f * P:(f + 1) * P], ident)
                        x.then_inc(tr, 1)

                    def down(j):
                        w = arrived("d", j).rearrange("p (f n) -> p f n", n=D)
                        pe.wait_ge(tev, b * NFG + (j + 2))
                        if j == 0:
                            pe.wait_ge(yev, b + 1)
                        for half in range(2):
                            for f in range(FG // P):
                                x = nc.tensor.matmul(ps[:, Y0 + half, :], pT[:, f * P:(f + 1) * P], w[:, f, half * 512:(half + 1) * 512],
                                                     start=(j == 0 and f == 0), stop=(j == NFG - 1 and f == FG // P - 1))
                        x.then_inc(used, 1)

                    pe.wait_ge(xev, b + 1)
                    for j in range(NFG):
                        pe.wait_ge(silu, b * NFG + (j + 1))
                        up("g", j, G)
                        if j >= 1:
                            turn_product(j - 1)
                        pe.wait_ge(prodr, b * NFG + (j + 1))
                        up("u", j, Uk)
                        if j == NFG - 1:
                            pe.wait_ge(xl, b * 16 + 32)
                            turn_rows()
                        if j >= 1:
                            down(j - 1)
                    turn_product(NFG - 1)
                    down(NFG - 1)
                    pe.wait_ge(used, b * NW + (NW + RING))
                    pe.sem_inc(ydone, 1)

            @block.scalar
            def _(act):
                act.sem_inc(silu, 1)
                act.sem_inc(tev, 1)
                with act.Fori(0, NBLK) as b:

                    def turned(j):
                        act.wait_ge(tr, b * NFG + (j + 1))
                        nc.scalar.copy(pT[:, :], ps[:, TB, :]).then_inc(tev, 1)

                    for j in range(NFG):
                        act.wait_ge(used, b * NW + (pos["g", j] + 1 + RING))
                        act.wait_ge(prodr, b * NFG + (j + 1))
                        nc.scalar.activation(sil[:, :], ps[:, G, :], ACT.Silu).then_inc(silu, 1)
                        if j >= 1:
                            turned(j - 1)
                    turned(NFG - 1)

            @block.vector
            def _(dve):
                dve.sem_inc(prodr, 1)
                dve.sem_inc(yev, 1)

                def turned_rows(done):
                    dve.wait_ge(xtr, done)
                    nc.vector.tensor_copy(xT[:, :, :].rearrange("p k t -> p (k t)"), ps[:, X0:X0 + 2, :].rearrange("p b t -> p (b t)")).then_inc(xev, 1)

                turned_rows(1)
                with dve.Fori(0, NBLK) as b:
                    for j in range(NFG):
                        dve.wait_ge(silu, b * NFG + (j + 2))
                        dve.wait_ge(used, b * NW + (pos["u", j] + 1 + RING))
                        nc.vector.tensor_tensor(prod[:, :], sil[:, :], ps[:, Uk, :], ALU.mult).then_inc(prodr, 1)
                    turned_rows(b + 2)
                    dve.wait_ge(ydone, b + 1)
                    dve.wait_ge(yfree, b + 1)
                    nc.vector.tensor_copy(y[:, :], ps[:, Y0:Y0 + 2, :].rearrange("p b t -> p (b t)")).then_inc(yev, 1)


def phase_final(nc, io, S, R):
    NX = SEQ // P
    with Phase(nc, "fin") as ph:
        xT = ph.sb("xT", [P, KD, SEQ])
        g2 = ph.sb("g2", [P, D])
        fg = ph.sb("fg", [P, D])
        y = ph.sb("y", [P, 2, 2, D])
        x = ph.sb("x", [P, 2, D])
        sq = ph.sb("sq", [P, D])
        ss = ph.sb("ss", [P, NX])
        ld, tr, ch, xr, va, sr, od = (ph.sem(n) for n in ("loaded", "transposed", "dve_step", "x_ready", "var_ready", "sd_ready", "out_ready"))
        gl = [ph.sem(f"gathered{s}") for s in range(2)]
        st = [ph.sem(f"stored{s}") for s in range(2)]
        ps, ident = S["ps"], S["c"]("ident")
        with nc.Block() as block:

            @block.sync
            def _(sp):
                sp.dma_start(xT[:, :, :], S["xT_d"][:, :, CTX:]).then_inc(ld, 16)
                sp.dma_start(g2[:, :], S["g2_d"].rearrange("(a n) -> a n", a=1).to_broadcast([P, D])).then_inc(ld, 16)
                sp.dma_start(fg[:, :], io["final_norm_g"].rearrange("(a n) -> a n", a=1).to_broadcast([P, D])).then_inc(ld, 16)
                for n in range(NX):
                    sp.wait_ge(od, n + 1)
                    sp.dma_start(io["out"][0, n * P:(n + 1) * P, :], x[:, n % 2, :]).then_inc(st[n % 2], 16)
                for s in range(2):
                    sp.wait_ge(st[s], 16 * (NX // 2))

            @block.gpsimd
            def _(pool):
                for n in range(NX):
                    if n >= 2:
                        pool.wait_ge(xr, n - 1)
                    for i in range(2):
                        nc.gpsimd.indirect_dma_start(
                            out=y[:, n % 2, i, :], out_offset=None, in_=S["ys_d"][:, :],
                            in_offset=bass.IndirectOffsetOnAxis(ap=R["slot"][:, i, n:n + 1], axis=0)).then_inc(gl[n % 2], 16)

            @block.tensor
            def _(pe):
                pe.wait_ge(ld, 48)
                for n in range(NX):
                    if n >= 2:
                        pe.wait_ge(xr, n - 1)
                    for k in range(KD):
                        t = nc.tensor.transpose(ps[:, 2 * (n % 2) + k // 4, (k % 4) * P:(k % 4 + 1) * P], xT[:, k, n * P:(n + 1) * P], ident)
                    t.then_inc(tr, 1)

            @block.scalar
            def _(act):
                for n in range(NX):
                    act.wait_ge(xr, n + 1)
                    if n >= 1:
                        act.wait_ge(va, n)
                    nc.scalar.activation(sq[:, :], x[:, n % 2, :], ACT.Square, accum_out=ss[:, n:n + 1]).then_inc(sr, 1)
                    act.wait_ge(va, n + 1)
                    nc.scalar.activation(ss[:, n:n + 1], ss[:, n:n + 1], ACT.Sqrt).then_inc(sr, 1)

            @block.vector
            def _(dve):
                step = Chain(dve, ch)
                dve.wait_ge(ld, 48)
                for n in range(NX):
                    s = n % 2
                    dve.wait_ge(gl[s], 32 * (n // 2 + 1))
                    if n >= 2:
                        dve.wait_ge(st[s], 16 * (n // 2))
                    step(nc.vector.tensor_scalar(y[:, s, 0, :], y[:, s, 0, :], R["gate"][:, 0, n:n + 1], None, ALU.mult))
                    step(nc.vector.scalar_tensor_tensor(out=y[:, s, 0, :], in0=y[:, s, 1, :], scalar=R["gate"][:, 1, n:n + 1],
                                                        in1=y[:, s, 0, :], op0=ALU.mult, op1=ALU.add))
                    step(nc.vector.tensor_tensor(y[:, s, 0, :], y[:, s, 0, :], g2[:, :], ALU.mult))
                    dve.wait_ge(tr, n + 1)
                    nc.vector.tensor_tensor(x[:, s, :], y[:, s, 0, :], ps[:, 2 * s:2 * s + 2, :].rearrange("p b t -> p (b t)"), ALU.add).then_inc(xr, 1)
                    dve.wait_ge(sr, 2 * n + 1)
                    nc.vector.tensor_scalar(ss[:, n:n + 1], ss[:, n:n + 1], 1.0 / D, EPS, ALU.mult, ALU.add).then_inc(va, 1)
                    dve.wait_ge(sr, 2 * n + 2)
                    step(nc.vector.reciprocal(ss[:, n:n + 1], ss[:, n:n + 1]))
                    nc.vector.scalar_tensor_tensor(out=x[:, s, :], in0=x[:, s, :], scalar=ss[:, n:n + 1], in1=fg[:, :],
                                                   op0=ALU.mult, op1=ALU.mult).then_inc(od, 1)


INPUTS = ["x", "c", "ctx", "c_ctx", "w_ada", "b_ada", "norm_mix_g", "norm_ffn_g", "w_in", "w_out", "gla_w_lr", "gla_b_lr",
          "gla_norm_g", "mlstm_conv", "mlstm_gate_b", "sgu_w", "sgu_b", "ffn_w_gate", "ffn_w_up", "ffn_w_down", "moe_router",
          "moe_w_gate", "moe_w_up", "moe_w_down", "final_norm_g", "cst", "dft_seq", "dft_ctx"]


def build(nc, io):
    S = {name: nc.dram_tensor(name, shape, F32, kind="Internal").ap() for name, shape in
         (("xT_d", (P, KD, T)), ("mixT_d", (P, KD, T)), ("xs_d", (NSLOT + P, D)), ("ys_d", (NSLOT, D)), ("g2_d", (D,)))}
    with ExitStack() as top:
        def sb(stack, name, shape, dt=F32):
            return stack.enter_context(nc.sbuf_tensor(name, shape, dt))

        S["ps"] = top.enter_context(nc.psum_tensor("ps", [P, 8, 512], F32))
        S["cst"] = sb(top, "cst", [P, NCST])
        S["c"] = lambda name: S["cst"][:, CST[name][0]:CST[name][0] + CST[name][1]]
        S["mod"] = sb(top, "mod", [P, 2, 48, 2])
        S["gmod"] = sb(top, "gmod", [P, 2, 2, 2, KD])
        R = {"slot": sb(top, "slot", [P, 2, SEQ // P], I32), "gate": sb(top, "gate", [P, 2, SEQ // P]),
             "expert": sb(top, "expert", [P, NBLK], I32)}
        phase_modulation(nc, io, S)
        phase_to_features(nc, io, S)
        for l in range(2):
            ctx_out = l == 0
            groups = GROUPS if ctx_out else GROUPS[1:]
            with ExitStack() as lay:
                FM = sb(lay, f"FM{l}", [P, 9, T])
                TM = sb(lay, f"TM{l}", [P, NT, 1536])
                with ExitStack() as st:
                    hT = sb(st, f"hT{l}", [P, KD, T])
                    xT = TM[:, 0:7, :].rearrange("p a b -> p (a b)")[:, 0:KD * T].rearrange("p (k t) -> p k t", t=T)
                    phase_norm(nc, S, f"nm{l}", xT, hT, l, 0, GROUPS)
                    phase_project(nc, io, S, l, hT, FM, TM, ctx_out)
                phase_fourier(nc, io, S, l, FM, ctx_out)
                phase_sgu(nc, io, S, l, TM, ctx_out)
                M = {}
                M["qd"] = sb(lay, f"qd{l}", [P, 2, T])
                M["kd"] = sb(lay, f"kd{l}", [P, 2, T])
                M["em"] = sb(lay, f"em{l}", [P, 2, 3, NT])
                M["mx"] = sb(lay, f"mx{l}", [8, 2, T])
                M["ig"] = sb(lay, f"ig{l}", [8, T])
                M["tg"] = sb(lay, f"tg{l}", [P, NT, 2, 4, 8])
                M["dcol"] = sb(lay, f"dcol{l}", [P, 4, NT])
                phase_decays(nc, io, S, l, FM, M)
                M["vx"] = sb(lay, f"vx{l}", [P, NT, NH, 65])
                for name, ch in (("og", 2), ("om", 4)):
                    M[name] = FM[:, ch:ch + 2, :].rearrange("p a b -> p (a b)").rearrange("p (n c) -> p n c", c=256)
                phase_conv(nc, io, S, l, FM, TM, M)
                phase_scan(nc, io, S, l, FM, TM, M)
                phase_mix_out(nc, io, S, l, TM, M, ctx_out)
            phase_out_proj(nc, io, S, l, groups)
            with ExitStack() as lay:
                hT = sb(lay, f"hF{l}", [P, KD, T])
                with ExitStack() as st:
                    xT = sb(st, f"xF{l}", [P, KD, T])
                    phase_norm(nc, S, f"nf{l}", xT, hT, l, 1, groups)
                if l == 0:
                    aT = sb(lay, "aT", [P, (DFF // P) * T])
                    phase_ffn_up(nc, io, S, hT, aT)
                    phase_ffn_down(nc, io, S, aT)
                else:
                    phase_route(nc, io, S, hT, R)
        phase_experts(nc, io, S, R)
        phase_final(nc, io, S, R)


def kernel(**inputs):
    import concourse.bacc as bacc
    from concourse.bass_utils import run_bass_kernel_spmd

    nc = bacc.Bacc("TRN2", target_bir_lowering=False, num_devices=1)
    shapes = {"cst": constants(), "dft_seq": dft(SEQ), "dft_ctx": dft(CTX)}
    arrays, io = {}, {}
    for name in INPUTS:
        a = shapes[name] if name in shapes else np.ascontiguousarray(inputs[name])
        arrays["in_" + name] = a
        io[name] = nc.dram_tensor("in_" + name, a.shape, mybir.dt.from_np(a.dtype), kind="ExternalInput").ap()
    io["out"] = nc.dram_tensor("out", (1, SEQ, D), F32, kind="ExternalOutput").ap()
    build(nc, io)
    r = run_bass_kernel_spmd(nc, [arrays], core_ids=[0])
    return r.results[0]["out"]
```

```python
from contextlib import ExitStack

import concourse.bass as bass
import numpy as np
from concourse import mybir

F32 = mybir.dt.float32
F32R = mybir.dt.float32r
I32 = mybir.dt.int32
U32 = mybir.dt.uint32
ACT = mybir.ActivationFunctionType
ALU = mybir.AluOpType
AX = mybir.AxisListType

P = 128
D = 1024
KD = D // P
CTX, SEQ = 256, 1024
T = CTX + SEQ
NT = T // P
NCT = CTX // P
GRID_W = 64
ROWS = SEQ // GRID_W
GROUPS = [(0, CTX), (CTX, 512), (CTX + 512, 512)]
NH, HD = 4, 64
GW = NH * HD
DFF = 2816
DFE = 3584
NE = 8
EPS = 1e-6
BIG = 1e30
UNIT = 2 * P
NUNIT = (2 * SEQ + NE * (UNIT - 1)) // UNIT

CST = {}


def _layout():
    at = 0
    for name, n in [("ident", P), ("ones", P), ("negF", 4 * P), ("negB", 4 * P), ("keepF", P), ("keepB", P),
                    ("sel8", 8 * P), ("selpair", 4 * P), ("blockg", 2 * P), ("blockm", 130), ("tri", P),
                    ("pref", NE), ("koff", NE), ("blk", NUNIT), ("half", NUNIT), ("one", 1), ("eps", 1), ("chan", 2 * P), ("row4", 4), ("row2", 2)]:
        CST[name] = (at, n)
        at += n
    return at


NCST = _layout()


def constants():
    c = np.zeros((P, NCST), np.float32)

    def put(name, a):
        o, n = CST[name]
        c[:a.shape[0], o:o + n] = a.reshape(a.shape[0], n)

    s, l = np.arange(P)[:, None], np.arange(P)[None, :]
    put("ident", np.eye(P))
    put("ones", np.ones((P, P)))
    put("negF", np.tile(np.where(s > l, BIG, 0.0), (1, 4)))
    put("negB", np.tile(np.where(s < l, BIG, 0.0), (1, 4)))
    put("keepF", (s <= l) * 1.0)
    put("keepB", (s >= l) * 1.0)
    sel = np.zeros((8, 8, P))
    for r in range(8):
        sel[r, r] = 1
    put("sel8", sel)
    selp = np.zeros((8, 4, P))
    for j in range(4):
        for p in range(P):
            selp[4 * (j // 2) + 2 * (j % 2) + p // HD, j, p] = 1
    put("selpair", selp)
    put("blockg", (np.arange(P)[:, None] // 32 == np.arange(2 * P)[None, :] // HD) * 1.0)
    put("blockm", (np.arange(P)[:, None] // HD == np.arange(130)[None, :] // 65) * 1.0)
    put("tri", (s < l) * 1.0)
    put("pref", np.tile(np.arange(NE, 0, -1.0), (P, 1)))
    put("koff", np.tile(UNIT * np.arange(NE * 1.0), (P, 1)))
    put("blk", np.tile(np.arange(NUNIT * 1.0), (P, 1)))
    put("half", np.tile(UNIT * np.arange(NUNIT * 1.0) + P, (P, 1)))
    put("row4", (np.arange(P)[:, None] // 32 == np.arange(4)[None, :]) * 1.0)
    put("row2", (np.arange(P)[:, None] // HD == np.arange(2)[None, :]) * 1.0)
    put("one", np.ones((P, 1)))
    put("eps", np.full((P, 1), EPS))
    ang = 2 * np.pi * (np.outer(np.arange(HD), np.arange(HD)) % HD) / HD
    ch = np.zeros((P, 2, P))
    for h in range(2):
        i = slice(h * HD, (h + 1) * HD)
        ch[i, 0, i] = np.cos(ang)
        ch[i, 1, i] = -np.sin(ang)
    put("chan", ch)
    return c


def dft(n):
    ang = 2 * np.pi * (np.outer(np.arange(n), np.arange(n)) % n) / n
    m = np.stack([np.cos(ang), np.sin(ang)], 1) / np.sqrt(n * HD)
    return np.ascontiguousarray(m.reshape(n // P, P, 2, n).transpose(1, 0, 2, 3)).astype(np.float32)


class Phase:

    def __init__(self, nc, name):
        self.nc, self.name, self.sems = nc, name, []

    def __enter__(self):
        self.stack = ExitStack()
        return self

    def sb(self, name, shape, dt=F32):
        return self.stack.enter_context(self.nc.sbuf_tensor(f"{self.name}_{name}", shape, dt))

    def sem(self, name):
        s = self.stack.enter_context(self.nc.semaphore(f"{self.name}_{name}"))
        self.sems.append(s)
        return s

    def __exit__(self, kind, value, trace):
        if kind is None:
            for s in self.sems:
                self.nc.gpsimd.sem_clear(s)
            self.nc.all_engine_barrier()
        self.stack.close()
        return False


class Chain:

    def __init__(self, eng, sem):
        self.eng, self.sem, self.n = eng, sem, 0

    def __call__(self, ins):
        self.n += 1
        ins.then_inc(self.sem, 1)
        self.eng.wait_ge(self.sem, self.n)


def cols(ap1d):
    return ap1d.rearrange("(k p) -> p k", p=P)


def bc(ap, n):
    return ap.unsqueeze(2).to_broadcast([ap.shape[0], ap.shape[1], n])


def phase_modulation(nc, io, S):
    with Phase(nc, "ada") as ph:
        wring = ph.sb("w", [P, 2, KD, 512])
        cond = ph.sb("cond", [P, 2, KD])
        act = ph.sb("act", [P, KD, 2])
        bias = ph.sb("bias", [P, 2, 48])
        ng = ph.sb("ng", [P, 2, 2, KD])
        small = ph.sem("small_loaded")
        wl = [ph.sem(f"w_loaded{s}") for s in range(2)]
        silu_ready, mm_done, evac, mod_done = (ph.sem(n) for n in ("silu_ready", "mm_done", "evacuated", "mod_done"))
        wfree = ph.sem("w_slot_free")
        mod, gmod, ps = S["mod"], S["gmod"], S["ps"]
        with nc.Block() as block:

            @block.sync
            def _(sp):
                with nc.allow_non_contiguous_dma(reason="vectors as columns"):
                    sp.dma_start(S["cst"][:, :], io["cst"]).then_inc(small, 16)
                    sp.dma_start(cond[:, 0, :], cols(io["c"].rearrange("a d -> (a d)"))).then_inc(small, 16)
                    sp.dma_start(cond[:, 1, :], cols(io["c_ctx"])).then_inc(small, 16)
                    for l in range(2):
                        sp.dma_start(bias[:, l, :], cols(io["b_ada"][l])).then_inc(small, 16)
                        sp.dma_start(ng[:, l, 0, :], cols(io["norm_mix_g"][l])).then_inc(small, 16)
                        sp.dma_start(ng[:, l, 1, :], cols(io["norm_ffn_g"][l])).then_inc(small, 16)
                for l in range(2):
                    w = io["w_ada"][l].rearrange("(k p) n -> p k n", p=P)
                    with sp.Fori(0, 6) as i:
                        for s in range(2):
                            sp.wait_ge(wfree, i * 2 + (12 * l + s + 1))
                            sp.dma_start(wring[:, s, :, :], w[:, :, bass.ds(i * 1024 + 512 * s, 512)]).then_inc(wl[s], 16)

            @block.scalar
            def _(act_e):
                act_e.wait_ge(small, 16 * 9)
                for j in range(2):
                    a = nc.scalar.activation(act[:, :, j], cond[:, j, :], ACT.Silu)
                a.then_inc(silu_ready, 1)

            @block.tensor
            def _(pe):
                pe.sem_inc(wfree, 2)
                pe.wait_ge(silu_ready, 1)
                for l in range(2):
                    with pe.Fori(0, 6) as i:
                        for s in range(2):
                            pe.wait_ge(wl[s], i * 16 + 16 * (6 * l + 1))
                            pe.wait_ge(evac, i * 2 + (12 * l + s + 1))
                            for m in range(4):
                                for k in range(KD):
                                    mm = nc.tensor.matmul(ps[:, s, 2 * m:2 * m + 2], wring[:, s, k, m * P:(m + 1) * P],
                                                          act[:, k, :], start=(k == 0), stop=(k == KD - 1))
                            mm.then_inc(mm_done, 1)
                            pe.wait_ge(mm_done, i * 2 + (12 * l + s + 1))
                            pe.sem_inc(wfree, 1)

            @block.vector
            def _(dve):
                dve.sem_inc(evac, 2)
                dve.wait_ge(small, 16 * 9)
                for l in range(2):
                    with dve.Fori(0, 6) as i:
                        for s in range(2):
                            dve.wait_ge(mm_done, i * 2 + (12 * l + s + 1))
                            nc.vector.tensor_tensor(
                                mod[:, l, bass.ds(i * 8 + 4 * s, 4), :], ps[:, s, 0:8].rearrange("p (m j) -> p m j", j=2),
                                bc(bias[:, l, bass.ds(i * 8 + 4 * s, 4)], 2), ALU.add).then_inc(evac, 1)
                dve.wait_ge(evac, 26)
                for l in range(2):
                    for w in range(2):
                        for j in range(2):
                            a = nc.vector.scalar_tensor_tensor(
                                out=gmod[:, l, w, j, :], in0=mod[:, l, 24 * w + 8:24 * w + 16, j], scalar=1.0,
                                in1=ng[:, l, w, :], op0=ALU.add, op1=ALU.mult)
                a.then_inc(mod_done, 1)
                dve.wait_ge(mod_done, 1)


def phase_to_features(nc, io, S):
    with Phase(nc, "x0") as ph:
        rows = ph.sb("rows", [P, 2, D])
        turned = ph.sb("turned", [P, 2, KD, P])
        loaded = [ph.sem(f"loaded{s}") for s in range(2)]
        stored = [ph.sem(f"stored{s}") for s in range(2)]
        tr, ev = ph.sem("transposed"), ph.sem("evacuated")
        ps, ident = S["ps"], S["c"]("ident")
        with nc.Block() as block:

            @block.sync
            def _(sp):
                for n in range(NT):
                    src = io["ctx"][0, n * P:(n + 1) * P, :] if n < NCT else io["x"][0, (n - NCT) * P:(n - NCT + 1) * P, :]
                    if n >= 2:
                        sp.wait_ge(tr, n - 1)
                    sp.dma_start(rows[:, n % 2, :], src).then_inc(loaded[n % 2], 16)

            @block.tensor
            def _(pe):
                for n in range(NT):
                    pe.wait_ge(loaded[n % 2], 16 * (n // 2 + 1))
                    if n >= 2:
                        pe.wait_ge(ev, n - 1)
                    for k in range(KD):
                        b = 2 * (n % 2) + k // 4
                        t = nc.tensor.transpose(ps[:, b, (k % 4) * P:(k % 4 + 1) * P], rows[:, n % 2, k * P:(k + 1) * P], ident)
                    t.then_inc(tr, 1)

            @block.vector
            def _(dve):
                for n in range(NT):
                    dve.wait_ge(tr, n + 1)
                    if n >= 2:
                        dve.wait_ge(stored[n % 2], 16 * (n // 2))
                    nc.vector.tensor_copy(turned[:, n % 2, :, :], ps[:, 2 * (n % 2):2 * (n % 2) + 2, :].rearrange(
                        "p b (k t) -> p (b k) t", t=P)).then_inc(ev, 1)

            @block.scalar
            def _(act):
                for n in range(NT):
                    act.wait_ge(ev, n + 1)
                    act.dma_start(S["xT_d"][:, :, n * P:(n + 1) * P], turned[:, n % 2, :, :]).then_inc(stored[n % 2], 16)
                for s in range(2):
                    act.wait_ge(stored[s], 16 * (NT // 2))


def phase_norm(nc, S, name, xT, hT, l, which, groups):
    with Phase(nc, name) as ph:
        sq = ph.sb("sq", [P, 4, 512])
        rstd = ph.sb("rstd", [P, 2, 512])
        xl, sq_ready, sq_used, ss_ready, var_ready, sd_ready, scaled, shifted, rst = (
            ph.sem(n) for n in ("x_loaded", "sq_ready", "sq_used", "ss_ready", "var_ready", "sd_ready", "scaled", "shifted", "rstd_ready"))
        ps, ones = S["ps"], S["c"]("ones")
        gmod, mod = S["gmod"], S["mod"]
        first = groups[0][0]
        with nc.Block() as block:

            @block.sync
            def _(sp):
                for t0, n in groups:
                    sp.dma_start(xT[:, :, t0:t0 + n], S["xT_d"][:, :, t0:t0 + n]).then_inc(xl, 16)

            @block.scalar
            def _(act):
                act.wait_ge(xl, 16 * len(groups))

                def squares(g, t0, n):
                    for k in range(KD):
                        q = g * KD + k
                        if q >= 4:
                            act.wait_ge(sq_used, q - 3)
                        nc.scalar.activation(sq[:, q % 4, :n], xT[:, k, t0:t0 + n], ACT.Square).then_inc(sq_ready, 1)

                def root(g, t0, n):
                    act.wait_ge(var_ready, g + 1)
                    nc.scalar.activation(rstd[:, g % 2, :n], rstd[:, g % 2, :n], ACT.Sqrt).then_inc(sd_ready, 1)

                for g, (t0, n) in enumerate(groups):
                    squares(g, t0, n)
                    root(g, t0, n)

            @block.tensor
            def _(pe):
                for g, (t0, n) in enumerate(groups):
                    for k in range(KD):
                        q = g * KD + k
                        pe.wait_ge(sq_ready, q + 1)
                        mm = nc.tensor.matmul(ps[:, g, :n], ones, sq[:, q % 4, :n], start=(k == 0), stop=(k == KD - 1))
                        mm.then_inc(sq_used, 1)

            @block.vector
            def _(dve):
                for g, (t0, n) in enumerate(groups):
                    dve.wait_ge(sq_used, (g + 1) * KD)
                    if g >= 2:
                        dve.wait_ge(scaled, KD * (g - 1))
                    nc.vector.tensor_scalar(rstd[:, g % 2, :n], ps[:, g, :n], 1.0 / D, EPS, ALU.mult, ALU.add).then_inc(var_ready, 1)
                    dve.wait_ge(sd_ready, g + 1)
                    nc.vector.reciprocal(rstd[:, g % 2, :n], rstd[:, g % 2, :n]).then_inc(rst, 1)
                    dve.wait_ge(rst, g + 1)
                    j = 1 if t0 < CTX else 0
                    for k in range(KD):
                        nc.vector.scalar_tensor_tensor(
                            out=hT[:, k, t0:t0 + n], in0=xT[:, k, t0:t0 + n], scalar=gmod[:, l, which, j, k:k + 1],
                            in1=rstd[:, g % 2, :n], op0=ALU.mult, op1=ALU.mult).then_inc(scaled, 1)

            @block.gpsimd
            def _(pool):
                for g, (t0, n) in enumerate(groups):
                    j = 1 if t0 < CTX else 0
                    for k in range(KD):
                        pool.wait_ge(scaled, g * KD + k + 1)
                        nc.gpsimd.tensor_scalar(hT[:, k, t0:t0 + n], hT[:, k, t0:t0 + n],
                                                mod[:, l, 24 * which + k, j:j + 1], None, ALU.add).then_inc(shifted, 1)
                pool.wait_ge(shifted, KD * len(groups))


def phase_project(nc, io, S, l, hT, FM, TM, ctx_out):
    loads = [((0, 256), [0, 1]), ((800, 512), [2, 3, 4, 5]), ((2352, 256), [6, 7]), (None, [8])]
    tok = [(256, 0), (1312, 512), (1840, 1024)]
    w_in = io["w_in"][l].rearrange("(k p) n -> p k n", p=P)
    units = []
    for i, (_, chunks) in enumerate(loads):
        for j, ch in enumerate(chunks):
            for t0, n in GROUPS:
                if ch in (6, 7) and not ctx_out and t0 < CTX:
                    continue
                units.append((i, "fm", j, ch, t0, n))
    for i, (_, dst) in enumerate(tok):
        for n in range(NT):
            if dst == 1024 and not ctx_out and n < NCT:
                continue
            units.append((len(loads) + i, "tm", 0, dst, n, 0))
    last_of = {}
    for u, un in enumerate(units):
        last_of[un[0]] = u
    NB = 8
    with Phase(nc, f"proj{l}") as ph:
        wring = ph.sb("w", [P, 2, KD, 512])
        wl = [ph.sem(f"w_loaded{s}") for s in range(2)]
        mm_done, ev = ph.sem("mm_done"), [ph.sem("evacuated_act"), ph.sem("evacuated_dve")]
        zeroed = ph.sem("gate_slot_zeroed")
        ps = S["ps"]
        nl = len(loads) + len(tok)
        cnt = {}
        need = []
        for i in range(nl):
            s = i % 2
            cnt[s] = cnt.setdefault(s, 0) + (5 if i == 3 else 1)
            need.append(16 * cnt[s])

        with nc.Block() as block:

            @block.sync
            def _(sp):
                for i in range(nl):
                    s = i % 2
                    if i >= 2:
                        sp.wait_ge(mm_done, last_of[i - 2] + 1)
                    if i == 3:
                        sp.wait_ge(zeroed, 1)
                        with nc.allow_non_contiguous_dma(reason="gate columns"):
                            for dst, src, n in ((0, 1824, 4), (4, 1832, 4), (32, 1828, 4), (36, 1836, 4), (64, 768, 32)):
                                sp.dma_start(wring[:, s, :, dst:dst + n], w_in[:, :, src:src + n]).then_inc(wl[s], 16)
                    else:
                        c0, n = loads[i][0] if i < len(loads) else (tok[i - len(loads)][0], 512)
                        sp.dma_start(wring[:, s, :, 0:n], w_in[:, :, c0:c0 + n]).then_inc(wl[s], 16)

            @block.gpsimd
            def _(pool):
                pool.wait_ge(mm_done, last_of[1] + 1)
                nc.gpsimd.memset(wring[:, 1, :, 0:P], 0.0).then_inc(zeroed, 1)

            @block.tensor
            def _(pe):
                seen = -1
                for u, (i, kind, j, dst, a, n) in enumerate(units):
                    if i != seen:
                        pe.wait_ge(wl[i % 2], need[i])
                        seen = i
                    if u >= NB:
                        v = u - NB
                        pe.wait_ge(ev[v % 2], v // 2 + 1)
                    for k in range(KD):
                        if kind == "fm":
                            mm = nc.tensor.matmul(ps[:, u % NB, :n], wring[:, i % 2, k, j * P:(j + 1) * P], hT[:, k, a:a + n],
                                                  start=(k == 0), stop=(k == KD - 1))
                        else:
                            mm = nc.tensor.matmul(ps[:, u % NB, :], hT[:, k, a * P:(a + 1) * P], wring[:, i % 2, k, :],
                                                  start=(k == 0), stop=(k == KD - 1))
                    mm.then_inc(mm_done, 1)

            def evacuate(eng, copy, par):
                for u, (i, kind, j, dst, a, n) in enumerate(units):
                    if u % 2 != par:
                        continue
                    eng.wait_ge(mm_done, u + 1)
                    out = FM[:, dst, a:a + n] if kind == "fm" else TM[:, a, dst:dst + 512]
                    src = ps[:, u % NB, :n] if kind == "fm" else ps[:, u % NB, :]
                    copy(out, src).then_inc(ev[par], 1)
                eng.wait_ge(ev[par], (len(units) + 1 - par) // 2)

            @block.scalar
            def _(act):
                evacuate(act, nc.scalar.copy, 0)

            @block.vector
            def _(dve):
                evacuate(dve, nc.vector.tensor_copy, 1)


def phase_fourier(nc, io, S, l, FM, ctx_out):
    tiles = list(range(0 if ctx_out else NCT, NT))
    with Phase(nc, f"four{l}") as ph:
        Y = ph.sb("y", [P, NT, 512])
        dring = ph.sb("dft", [P, 3, 2, SEQ])
        dctx = ph.sb("dftc", [P, NCT, 2, CTX])
        Z = ph.sb("z", [P, 2, T])
        dl = [ph.sem(f"dft_loaded{s}") for s in range(3)]
        cl, ymm, yev, dused, zdone, cdone, zev, st = (
            ph.sem(n) for n in ("ctx_dft_loaded", "y_done", "y_ready", "dft_used", "z_done", "ctx_z_done", "z_ready", "stored"))
        ps, chan = S["ps"], S["c"]("chan")
        with nc.Block() as block:

            @block.sync
            def _(sp):
                if ctx_out:
                    sp.dma_start(dctx[:, :, :, :], io["dft_ctx"]).then_inc(cl, 16)
                for i in range(SEQ // P):
                    if i >= 3:
                        sp.wait_ge(dused, i - 2)
                    sp.dma_start(dring[:, i % 3, :, :], io["dft_seq"][:, i, :, :]).then_inc(dl[i % 3], 16)
                sp.wait_ge(zev, 5 if ctx_out else 4)
                a = 0 if ctx_out else CTX
                sp.dma_start(S["mixT_d"][:, 6:8, a:], Z[:, :, a:]).then_inc(st, 16)
                sp.wait_ge(st, 16)

            @block.tensor
            def _(pe):
                for i, n in enumerate(tiles):
                    if i >= 2:
                        pe.wait_ge(yev, i - 1)
                    for c in range(2):
                        mm = nc.tensor.matmul(ps[:, i % 2, c * 256:(c + 1) * 256], FM[:, 6 + c, n * P:(n + 1) * P], chan,
                                              start=True, stop=True)
                    mm.then_inc(ymm, 1)
                pe.wait_ge(yev, len(tiles))
                for i in range(SEQ // P):
                    pe.wait_ge(dl[i % 3], 16 * (i // 3 + 1))
                    for c in range(2):
                        for trig in range(2):
                            for half in range(2):
                                mm = nc.tensor.matmul(
                                    ps[:, 2 + 2 * c + half, :], Y[:, NCT + i, c * 256 + trig * P:c * 256 + (trig + 1) * P],
                                    dring[:, i % 3, trig, half * 512:(half + 1) * 512],
                                    start=(i == 0 and trig == 0), stop=(i == SEQ // P - 1 and trig == 1))
                    mm.then_inc(dused, 1)
                if ctx_out:
                    pe.wait_ge(cl, 16)
                    for c in range(2):
                        for i in range(NCT):
                            for trig in range(2):
                                mm = nc.tensor.matmul(
                                    ps[:, 6 + c, :CTX], Y[:, i, c * 256 + trig * P:c * 256 + (trig + 1) * P],
                                    dctx[:, i, trig, :], start=(i == 0 and trig == 0), stop=(i == NCT - 1 and trig == 1))
                    mm.then_inc(cdone, 1)

            @block.vector
            def _(dve):
                for i, n in enumerate(tiles):
                    dve.wait_ge(ymm, i + 1)
                    nc.vector.tensor_copy(Y[:, n, :], ps[:, i % 2, :]).then_inc(yev, 1)
                dve.wait_ge(dused, SEQ // P)
                for c in range(2):
                    for half in range(2):
                        nc.vector.tensor_copy(Z[:, c, CTX + half * 512:CTX + (half + 1) * 512],
                                              ps[:, 2 + 2 * c + half, :]).then_inc(zev, 1)
                if ctx_out:
                    dve.wait_ge(cdone, 1)
                    nc.vector.tensor_copy(Z[:, :, 0:CTX], ps[:, 6:8, :CTX]).then_inc(zev, 1)


def phase_sgu(nc, io, S, l, TM, ctx_out):
    tiles = list(range(0 if ctx_out else NCT, NT))
    with Phase(nc, f"sgu{l}") as ph:
        ws = ph.sb("ws", [P, NH, P])
        wsT = ph.sb("wsT", [P, NH, P])
        bs = ph.sb("bs", [P, NH])
        stats = ph.sb("stats", [P, NT, 6])
        mv = ph.sb("mv", [P, NT, 2])
        rstd = ph.sb("rstd", [P, NT])
        ld, tr, wev, chain, var, sd, vn, mm_done, done = (
            ph.sem(n) for n in ("loaded", "transposed", "wT_ready", "dve_step", "var_ready", "sd_ready", "vn_ready", "mixed", "gated"))
        ps, ident = S["ps"], S["c"]("ident")
        t0 = tiles[0]
        with nc.Block() as block:

            @block.sync
            def _(sp):
                sp.dma_start(ws[:, :, :], io["sgu_w"][l].rearrange("g a b -> a g b")).then_inc(ld, 16)
                with nc.allow_non_contiguous_dma(reason="bias columns"):
                    sp.dma_start(bs[:, :], io["sgu_b"][l].rearrange("g a -> a g")).then_inc(ld, 16)

            @block.tensor
            def _(pe):
                pe.wait_ge(ld, 32)
                for g in range(NH):
                    t = nc.tensor.transpose(ps[:, 7, g * P:(g + 1) * P], ws[:, g, :], ident)
                t.then_inc(tr, 1)
                pe.wait_ge(wev, 1)
                pe.wait_ge(vn, len(tiles))
                for g in range(NH):
                    v0 = 1280 + g * HD
                    nc.tensor.matmul(ps[:, g, :].rearrange("p (n c) -> p n c", c=HD), wsT[:, g, :], TM[:, NCT:NT, v0:v0 + HD],
                                     start=True, stop=True).then_inc(mm_done, 1)
                if ctx_out:
                    for g in range(NH):
                        v0 = 1280 + g * HD
                        nc.tensor.matmul(ps[:, 4, g * P:(g + 1) * P].rearrange("p (n c) -> p n c", c=HD), wsT[:, g, :],
                                         TM[:, 0:NCT, v0:v0 + HD], start=True, stop=True).then_inc(mm_done, 1)

            @block.scalar
            def _(act):
                act.wait_ge(tr, 1)
                nc.scalar.copy(wsT[:, :, :], ps[:, 7, :].rearrange("p (g t) -> p g t", t=P)).then_inc(wev, 1)
                act.wait_ge(var, 1)
                nc.scalar.activation(rstd[:, t0:], rstd[:, t0:], ACT.Sqrt).then_inc(sd, 1)

            @block.vector
            def _(dve):
                step = Chain(dve, chain)
                for n in tiles:
                    st = nc.vector.bn_stats(stats[:, n, :], TM[:, n, 1280:1536])
                step(st)
                for n in tiles:
                    st = nc.vector.bn_aggr(mv[:, n, :], stats[:, n, :])
                step(st)
                nc.vector.tensor_scalar(rstd[:, t0:], mv[:, t0:, 1], EPS, None, ALU.add).then_inc(var, 1)
                dve.wait_ge(sd, 1)
                step(nc.vector.reciprocal(rstd[:, t0:], rstd[:, t0:]))
                for n in tiles:
                    nc.vector.tensor_scalar(TM[:, n, 1280:1536], TM[:, n, 1280:1536], mv[:, n, 0:1], rstd[:, n:n + 1],
                                            ALU.subtract, ALU.mult).then_inc(vn, 1)
                dve.wait_ge(ld, 32)
                for g in range(NH):
                    dve.wait_ge(mm_done, g + 1)
                    u = TM[:, NCT:NT, 1024 + g * HD:1024 + (g + 1) * HD]
                    nc.vector.scalar_tensor_tensor(out=u, in0=ps[:, g, :].rearrange("p (n c) -> p n c", c=HD),
                                                   scalar=bs[:, g:g + 1], in1=u, op0=ALU.add, op1=ALU.mult).then_inc(done, 1)
                if ctx_out:
                    for g in range(NH):
                        dve.wait_ge(mm_done, 2 * NH)
                        u = TM[:, 0:NCT, 1024 + g * HD:1024 + (g + 1) * HD]
                        nc.vector.scalar_tensor_tensor(out=u, in0=ps[:, 4, g * P:(g + 1) * P].rearrange("p (n c) -> p n c", c=HD),
                                                       scalar=bs[:, g:g + 1], in1=u, op0=ALU.add, op1=ALU.mult).then_inc(done, 1)
                dve.wait_ge(done, 8 if ctx_out else 4)


def order(direction, j):
    if direction == 0:
        return j
    return NCT - 1 - j if j < NCT else NT - 1 - (j - NCT)


def phase_decays(nc, io, S, l, FM, M):
    with Phase(nc, f"dec{l}") as ph:
        wlr = ph.sb("wlr", [P, 2, P])
        blr = ph.sb("blr", [P, 2])
        gb = ph.sb("gb", [P, 1])
        z = ph.sb("z", [P, 2, T])
        e = FM[:, 6:8, :]
        lf = ph.sb("lf", [8, T])
        le = ph.sb("le", [8, T])
        cum8 = ph.sb("cum8", [8, 2, T])
        ones8 = ph.sb("ones8", [8, T])
        stack = ph.sb("stack", [P, T])
        mprev = ph.sb("mprev", [8, 2, NT])
        mlast = ph.sb("mlast", [8, 2, NT])
        dec = ph.sb("dec", [8, 2, NT])
        ld, zer, zmm, ch_d, ch_a, d2a, a2d, st_ready, trd, tev, dmm = (
            ph.sem(n) for n in ("loaded", "zeroed", "z_done", "dve_step", "act_step", "dve_to_act", "act_to_dve", "stack_ready",
                                "stack_transposed", "stack_read", "decay_rows_done"))
        ps, c = S["ps"], S["c"]
        mx, tg, dcol, qd, kd, em = M["mx"], M["tg"], M["dcol"], M["qd"], M["kd"], M["em"]

        def tiles(ap):
            return ap.rearrange("p (n t) -> p n t", t=P)

        with nc.Block() as block:

            @block.sync
            def _(sp):
                sp.wait_ge(zer, 1)
                with nc.allow_non_contiguous_dma(reason="vectors as columns"):
                    for d in range(2):
                        sp.dma_start(wlr[64 + 16 * d:80 + 16 * d, d, :], io["gla_w_lr"][l, d]).then_inc(ld, 16)
                        sp.dma_start(blr[:, d:d + 1], io["gla_b_lr"][l, d].rearrange("(p a) -> p a", a=1)).then_inc(ld, 16)
                        for kind in range(2):
                            sp.dma_start(gb[32 * kind + 4 * d:32 * kind + 4 * d + 4, :],
                                         io["mlstm_gate_b"][l, d, kind].rearrange("(p a) -> p a", a=1)).then_inc(ld, 16)

            @block.gpsimd
            def _(pool):
                nc.gpsimd.memset(wlr[:, :, :], 0.0)
                nc.gpsimd.memset(gb[:, :], 0.0)
                nc.gpsimd.memset(ones8[:, :], 1.0)
                nc.gpsimd.memset(stack[:, :], 0.0).then_inc(zer, 1)

            @block.tensor
            def _(pe):
                pe.wait_ge(ld, 16 * 8)
                for d in range(2):
                    for g, (t0, n) in enumerate(GROUPS):
                        mm = nc.tensor.matmul(ps[:, 3 * d + g, :n], wlr[64:96, d, :], FM[64:96, 8, t0:t0 + n], start=True, stop=True)
                mm.then_inc(zmm, 1)
                for d in range(2):
                    pe.wait_ge(st_ready, d + 1)
                    for n in range(NT):
                        q = d * NT + n
                        if q >= 2:
                            pe.wait_ge(tev, q - 1)
                        nc.tensor.transpose(ps[:, 6 + q % 2, 0:P], stack[:, n * P:(n + 1) * P], c("ident")).then_inc(trd, 1)
                pe.wait_ge(a2d, 6)
                selp = c("selpair").rearrange("p (a t) -> p a t", t=P)
                for j in range(4):
                    mm = nc.tensor.matmul(ps[:, 0, j * NT:(j + 1) * NT], selp[0:8, j, :], dec[:, j // 2, :], start=True, stop=True)
                mm.then_inc(dmm, 1)

            @block.scalar
            def _(act):
                step = Chain(act, ch_a)
                act.wait_ge(d2a, 1)
                step(nc.scalar.activation(e[:, :, :], e[:, :, :], ACT.Exp, scale=-1.0))
                nc.scalar.activation(e[:, :, :], e[:, :, :], ACT.Ln, bias=c("one")).then_inc(a2d, 1)
                act.wait_ge(d2a, 2)
                step(nc.scalar.activation(le[:, :], le[:, :], ACT.Exp, scale=-1.0))
                nc.scalar.activation(le[:, :], le[:, :], ACT.Ln, bias=c("one")[0:8, :]).then_inc(a2d, 1)
                act.wait_ge(d2a, 3)
                nc.scalar.activation(em[:, :, :, :], em[:, :, :, :], ACT.Exp, scale=1.0 / 16).then_inc(a2d, 1)
                for d in range(2):
                    act.wait_ge(d2a, 4 + d)
                    nc.scalar.activation(e[:, 0, :], z[:, d, :], ACT.Exp, scale=1.0 / 16)
                    nc.scalar.activation(e[:, 1, :], z[:, d, :], ACT.Exp, scale=-1.0 / 16).then_inc(a2d, 1)
                for d in range(2):
                    act.wait_ge(d2a, 6 + d)
                    nc.scalar.activation(stack[32:40, :], stack[32:40, :], ACT.Exp)
                    nc.scalar.activation(stack[64:72, :], stack[64:72, :], ACT.Exp, scale=-1.0)
                    nc.scalar.activation(stack[96:104, :], stack[96:104, :], ACT.Exp).then_inc(st_ready, 1)
                nc.scalar.activation(dec[:, :, :], dec[:, :, :], ACT.Exp).then_inc(a2d, 1)

            @block.vector
            def _(dve):
                step = Chain(dve, ch_d)
                dve.wait_ge(ld, 16 * 8)
                dve.wait_ge(zmm, 1)
                for d in range(2):
                    for g, (t0, n) in enumerate(GROUPS):
                        x = nc.vector.tensor_scalar(z[:, d, t0:t0 + n], ps[:, 3 * d + g, :n], blr[:, d:d + 1], None, ALU.add)
                step(x)
                nc.vector.scalar_tensor_tensor(out=e[:, :, :], in0=z[:, :, :], scalar=-1.0, in1=z[:, :, :], op0=ALU.mult, op1=ALU.max).then_inc(d2a, 1)
                nc.vector.tensor_scalar(M["ig"][:, :], FM[0:8, 8, :], gb[0:8, :], None, ALU.add)
                step(nc.vector.tensor_scalar(lf[:, :], FM[32:40, 8, :], gb[32:40, :], None, ALU.add))
                nc.vector.scalar_tensor_tensor(out=le[:, :], in0=lf[:, :], scalar=-1.0, in1=lf[:, :], op0=ALU.mult, op1=ALU.max).then_inc(d2a, 1)
                dve.wait_ge(a2d, 1)
                step(nc.vector.scalar_tensor_tensor(out=z[:, :, :], in0=z[:, :, :], scalar=0.0, in1=e[:, :, :], op0=ALU.min, op1=ALU.subtract))
                for n in range(NT):
                    t = slice(n * P, (n + 1) * P)
                    nc.vector.tensor_tensor_scan(e[:, 0, t], c("ones"), z[:, 0, t], 0.0, ALU.mult, ALU.add)
                    x = nc.vector.tensor_tensor_scan(e[:, 1, t][:, ::-1], c("ones"), z[:, 1, t][:, ::-1], 0.0, ALU.mult, ALU.add)
                step(x)
                for d, (mid, last) in enumerate(((63, 127), (64, 0))):
                    et = tiles(e[:, d, :])
                    nc.vector.tensor_copy(em[:, d, 0, :], et[:, :, mid])
                    nc.vector.tensor_copy(em[:, d, 1, :], et[:, :, last])
                    x = nc.vector.tensor_tensor(em[:, d, 2, :], et[:, :, last], et[:, :, mid], ALU.subtract)
                step(x)
                for d in range(2):
                    x = nc.vector.tensor_tensor(tiles(z[:, d, :]), tiles(e[:, d, :]), bc(em[:, d, 0, :], P), ALU.subtract)
                step(x)
                dve.sem_inc(d2a, 1)
                dve.sem_inc(d2a, 1)
                for d in range(2):
                    dve.wait_ge(a2d, 4 + d)
                    nc.vector.scalar_tensor_tensor(out=qd[:, d, :], in0=FM[:, 0, :], scalar=32.0 ** -0.5, in1=e[:, 0, :], op0=ALU.mult, op1=ALU.mult)
                    step(nc.vector.tensor_tensor(kd[:, d, :], FM[:, 1, :], e[:, 1, :], ALU.mult))
                    if d == 0:
                        dve.sem_inc(d2a, 1)
                step(nc.vector.scalar_tensor_tensor(out=lf[:, :], in0=lf[:, :], scalar=0.0, in1=le[:, :], op0=ALU.min, op1=ALU.subtract))
                step(nc.vector.tensor_tensor_scan(cum8[:, 0, :], ones8[:, :], lf[:, :], 0.0, ALU.mult, ALU.add))
                back = [(0, CTX), (CTX, T)]
                init = 0.0
                for a, b in back:
                    step(nc.vector.tensor_tensor_scan(cum8[:, 1, a:b][:, ::-1], ones8[:, a:b], lf[:, a:b][:, ::-1], init, ALU.mult, ALU.add))
                    init = cum8[:, 1, a:a + 1]
                for d in range(2):
                    if d == 1:
                        dve.wait_ge(trd, NT)
                    step(nc.vector.tensor_tensor(stack[0:8, :], M["ig"][:, :], cum8[:, d, :], ALU.subtract))
                    if d == 0:
                        step(nc.vector.tensor_tensor_scan(mx[:, 0, :], stack[0:8, :], stack[0:8, :], 0.0, ALU.max, ALU.max))
                    else:
                        init = 0.0
                        for a, b in back:
                            r = stack[0:8, a:b][:, ::-1]
                            step(nc.vector.tensor_tensor_scan(mx[:, 1, a:b][:, ::-1], r, r, init, ALU.max, ALU.max))
                            init = mx[:, 1, a:a + 1]
                    m3 = tiles(mx[:, d, :])
                    step(nc.vector.tensor_copy(mlast[:, d, :], m3[:, :, P - 1 if d == 0 else 0]))
                    first = order(d, 0)
                    nc.vector.memset(mprev[:, d, first:first + 1], 0.0)
                    if d == 0:
                        x = nc.vector.tensor_copy(mprev[:, 0, 1:NT], mlast[:, 0, 0:NT - 1])
                    else:
                        nc.vector.tensor_copy(mprev[:, 1, 0:1], mlast[:, 1, 1:2])
                        nc.vector.tensor_copy(mprev[:, 1, NT - 1:NT], mlast[:, 1, 0:1])
                        x = nc.vector.tensor_copy(mprev[:, 1, NCT:NT - 1], mlast[:, 1, NCT + 1:NT])
                    step(x)
                    nc.vector.tensor_tensor(dec[:, d, :], mprev[:, d, :], mlast[:, d, :], ALU.subtract)
                    nc.vector.tensor_tensor(tiles(stack[32:40, :]), bc(mprev[:, d, :], P), m3, ALU.subtract)
                    nc.vector.tensor_tensor(stack[64:72, :], cum8[:, d, :], mx[:, d, :], ALU.add)
                    step(nc.vector.tensor_tensor(tiles(stack[96:104, :]), tiles(stack[0:8, :]), bc(mlast[:, d, :], P), ALU.subtract))
                    dve.sem_inc(d2a, 1)
                    for n in range(NT):
                        q = d * NT + n
                        dve.wait_ge(trd, q + 1)
                        nc.vector.tensor_copy(tg[:, n, d, :, :], ps[:, 6 + q % 2, 0:P].rearrange("p (a r) -> p a r", r=32)[:, :, 0:8]).then_inc(tev, 1)
                dve.wait_ge(dmm, 1)
                step(nc.vector.tensor_copy(dcol[:, :, :], ps[:, 0, 0:4 * NT].rearrange("p (j n) -> p j n", n=NT)))
                dve.wait_ge(tev, 2 * NT)
                dve.wait_ge(a2d, 6)


def phase_conv(nc, io, S, l, FM, TM, M):
    src, dst = [2, 3, 4, 5], [0, 1, 6, 7]
    with Phase(nc, f"conv{l}") as ph:
        w = ph.sb("w", [P, 4, 9])
        ld, ch, cv, done, vx = (ph.sem(n) for n in ("loaded", "dve_step", "convolved", "silu_done", "v_ready"))
        with nc.Block() as block:

            @block.sync
            def _(sp):
                with nc.allow_non_contiguous_dma(reason="taps as columns"):
                    for j in range(4):
                        sp.dma_start(w[:, j, :], io["mlstm_conv"][l].rearrange("a b d -> (a b) d")[:, j * P:(j + 1) * P]
                                     .rearrange("t p -> p t")).then_inc(ld, 16)

            @block.vector
            def _(dve):
                step = Chain(dve, ch)
                dve.wait_ge(ld, 64)
                for j in range(4):
                    x, y = FM[:, src[j], :], FM[:, dst[j], :]
                    x2, y2 = (a[:, CTX:].rearrange("p (r c) -> p r c", c=GRID_W) for a in (x, y))
                    step(nc.vector.tensor_scalar(y, x, w[:, j, 4:5], None, ALU.mult))
                    for dr in (-1, 0, 1):
                        for dc in (-1, 0, 1):
                            if dr == 0 and dc == 0:
                                continue
                            r0, r1 = max(0, -dr), ROWS - max(0, dr)
                            c0, c1 = max(0, -dc), GRID_W - max(0, dc)
                            o = y2[:, r0:r1, c0:c1]
                            tap = w[:, j, 3 * (dr + 1) + dc + 1:3 * (dr + 1) + dc + 2]
                            step(nc.vector.scalar_tensor_tensor(out=o, in0=x2[:, r0 + dr:r1 + dr, c0 + dc:c1 + dc], scalar=tap,
                                                                in1=o, op0=ALU.mult, op1=ALU.add))
                            if dr == 0:
                                a, b = max(0, -dc), CTX - max(0, dc)
                                step(nc.vector.scalar_tensor_tensor(out=y[:, a:b], in0=x[:, a + dc:b + dc], scalar=tap,
                                                                    in1=y[:, a:b], op0=ALU.mult, op1=ALU.add))
                    dve.sem_inc(cv, 1)
                for j in range(2):
                    dve.wait_ge(done, j + 1)
                    step(nc.vector.tensor_scalar(FM[:, dst[j], :], FM[:, dst[j], :], HD ** -0.5, None, ALU.mult))

            @block.scalar
            def _(act):
                for j in range(4):
                    act.wait_ge(cv, j + 1)
                    nc.scalar.activation(FM[:, dst[j], :], FM[:, dst[j], :], ACT.Silu).then_inc(done, 1)
                act.wait_ge(done, 4)

            @block.gpsimd
            def _(pool):
                for n in range(NT):
                    nc.gpsimd.memset(M["vx"][:, n, :, HD:HD + 1], 1.0)
                    x = nc.gpsimd.tensor_copy(M["vx"][:, n, :, 0:HD], TM[:, n, 512:768].rearrange("p (h c) -> p h c", c=HD))
                x.then_inc(vx, 1)
                pool.wait_ge(vx, 1)


def phase_scan(nc, io, S, l, FM, TM, M):
    U = 2 * NT
    with Phase(nc, f"scan{l}") as ph:
        kdt = ph.sb("kdt", [P, 2, P])
        kw = ph.sb("kw", [P, 2, NH, HD])
        sg = ph.sb("sg", [P, 2, NH, P])
        ex = ph.sb("ex", [P, 2, NH, P])
        tmp = ph.sb("tmp", [P, NH, 65])
        num = ph.sb("num", [P, NH, 65])
        den = ph.sb("den", [P, NH])
        dsg = ph.sb("dsg", [P, 2 * P])
        dsm = ph.sb("dsm", [P, 2, 130])
        Sg = ph.sb("Sg", [P, 2, 2 * P])
        Sp = ph.sb("Sp", [P, 2, 2 * P])
        Sm = ph.sb("Sm", [P, 2, 2, 130])
        pe_tr, pe_mb, pe_sg, pe_sm, pe_og, pe_om, pe_u = (ph.sem(n) for n in (
            "transposed", "max_rows_done", "gla_scores_done", "mlstm_scores_done", "gla_out_done", "mlstm_out_done", "updates_done"))
        a_kdt, a_ex = ph.sem("kdt_ready"), ph.sem("ex_ready")
        g_q = ph.sem("masked_q_ready")
        qg = ph.sb("qg", [P, 2, NH, P])
        qm = ph.sb("qm", [P, 2, NH, P])
        v_init, v_kw, v_sg, v_w, v_og, v_om, v_st, ch = (ph.sem(n) for n in (
            "states_zero", "kw_ready", "gla_weights_ready", "mlstm_weights_ready", "gla_out_read", "mlstm_out_read", "states_ready", "dve_step"))
        ps, c = S["ps"], S["c"]
        mx, tg, dcol, qd, kd, em, vx, og, om = (M[k] for k in ("mx", "tg", "dcol", "qd", "kd", "em", "vx", "og", "om"))
        TR, SG, OG, KT, MB, SM, OI, OC = range(8)
        mq, mk = (0, 1), (6, 7)
        sel8 = c("sel8").rearrange("p (a t) -> p a t", t=P)

        def unit(u):
            d = u % 2
            n = order(d, u // 2)
            return d, n, slice(n * P, (n + 1) * P)

        with nc.Block() as block:

            @block.tensor
            def _(pe):
                for u in range(U):
                    d, n, t = unit(u)
                    if u >= 1:
                        pe.wait_ge(a_kdt, u)
                        pe.wait_ge(v_kw, u)
                    nc.tensor.transpose(ps[:, KT, 0:P], kd[:, d, t], c("ident"))
                    for j in range(2):
                        x = nc.tensor.transpose(ps[:, TR, (j + 1) * P:(j + 2) * P], FM[:, mk[j], t], c("ident"))
                    x.then_inc(pe_tr, 1)
                    if u >= 1:
                        pe.wait_ge(a_ex, u)
                    nc.tensor.matmul(ps[:, MB, :], c("ident"), c("negF" if d == 0 else "negB"), start=True, stop=False, skip_group_check=True)
                    for h in range(NH):
                        x = nc.tensor.matmul(ps[:, MB, h * P:(h + 1) * P], sel8[0:8, 4 * d + h, :], mx[:, d, t],
                                             start=False, stop=(h == NH - 1), skip_group_check=True)
                    x.then_inc(pe_mb, 1)
                    if u >= 1:
                        pe.wait_ge(v_w, u)
                    pe.wait_ge(g_q, u + 1)
                    for j in range(2):
                        x = nc.tensor.matmul(ps[:, SM, j * 256:(j + 1) * 256], FM[:, mk[j], t],
                                             qm[:, d, 2 * j:2 * j + 2, :].rearrange("p a b -> p (a b)"), start=True, stop=True)
                    x.then_inc(pe_sm, 1)
                    if u >= 1:
                        pe.wait_ge(v_st, u)
                    else:
                        pe.wait_ge(v_init, 1)
                    nc.tensor.matmul(ps[:, SG, :], kd[:, d, t], qg[:, d, :, :].rearrange("p a b -> p (a b)"),
                                     start=True, stop=True).then_inc(pe_sg, 1)
                    if u >= 1:
                        pe.wait_ge(v_og, u)
                        pe.wait_ge(v_om, u)
                    nc.tensor.matmul(ps[:, OG, 0:256], qd[:, d, t], Sp[:, d, :], start=True, stop=False, skip_group_check=True)
                    for j in range(2):
                        nc.tensor.matmul(ps[:, OC, j * 130:(j + 1) * 130], FM[:, mq[j], t], Sm[:, d, j, :], start=True, stop=True)
                    pe.wait_ge(v_sg, u + 1)
                    for h in range(NH):
                        x = nc.tensor.matmul(ps[:, OG, h * HD:(h + 1) * HD], sg[:, d, h, :], TM[:, n, h * HD:(h + 1) * HD],
                                             start=False, stop=(h == NH - 1), skip_group_check=True)
                    x.then_inc(pe_og, 1)
                    pe.wait_ge(v_w, u + 1)
                    for h in range(NH):
                        x = nc.tensor.matmul(ps[:, OI, h * 65:(h + 1) * 65], ex[:, d, h, :], vx[:, n, h, :], start=True, stop=True)
                    x.then_inc(pe_om, 1)
                    pe.wait_ge(a_kdt, u + 1)
                    pe.wait_ge(v_og, u + 1)
                    nc.tensor.matmul(ps[:, OG, 256:512], kdt[:, d, :], TM[:, n, 0:256], start=True, stop=True)
                    pe.wait_ge(v_kw, u + 1)
                    for j in range(2):
                        x = nc.tensor.matmul(ps[:, SG, j * 130:(j + 1) * 130], kw[:, d, 2 * j:2 * j + 2, :].rearrange("p a b -> p (a b)"),
                                             vx[:, n, 2 * j:2 * j + 2, :].rearrange("p a b -> p (a b)"), start=True, stop=True)
                    x.then_inc(pe_u, 1)

            @block.scalar
            def _(act):
                for u in range(U):
                    d, n, t = unit(u)
                    if u >= 2:
                        act.wait_ge(pe_u, u - 1)
                    act.wait_ge(pe_tr, u + 1)
                    nc.scalar.copy(kdt[:, d, :], ps[:, KT, 0:P]).then_inc(a_kdt, 1)
                    act.wait_ge(pe_mb, u + 1)
                    for h in range(NH):
                        x = nc.scalar.activation(ex[:, d, h, :], ps[:, MB, h * P:(h + 1) * P], ACT.Exp,
                                                 bias=tg[:, n, d, 0, 4 * d + h:4 * d + h + 1], scale=-1.0)
                    x.then_inc(a_ex, 1)

            @block.gpsimd
            def _(pool):
                for u in range(U):
                    d, n, t = unit(u)
                    if u >= 2:
                        pool.wait_ge(pe_sm, u - 1)
                        pool.wait_ge(pe_sg, u - 1)
                    nc.gpsimd.tensor_tensor(qg[:, d, :, :], qd[:, d, t].unsqueeze(1).to_broadcast([P, NH, P]), bc(c("row4"), P), ALU.mult)
                    for j in range(2):
                        x = nc.gpsimd.tensor_tensor(qm[:, d, 2 * j:2 * j + 2, :], FM[:, mq[j], t].unsqueeze(1).to_broadcast([P, 2, P]),
                                                    bc(c("row2"), P), ALU.mult)
                    x.then_inc(g_q, 1)

            @block.vector
            def _(dve):
                step = Chain(dve, ch)
                nc.vector.memset(sg[:, :, :, :], 0.0)
                nc.vector.memset(Sg[:, :, :], 0.0)
                nc.vector.memset(Sp[:, :, :], 0.0)
                nc.vector.memset(Sm[:, :, :, :], 0.0).then_inc(v_init, 1)
                dve.wait_ge(v_init, 1)
                keep = [c("keepF"), c("keepB")]
                written = set()
                for u in range(U):
                    d, n, t = unit(u)
                    h8 = slice(4 * d, 4 * d + 4)
                    if u >= 2:
                        dve.wait_ge(pe_u, u - 1)
                    dve.wait_ge(pe_tr, u + 1)
                    nc.vector.tensor_tensor(kw[:, d, :, :], ps[:, TR, P:3 * P].rearrange("p (h c) -> p h c", c=HD),
                                            bc(tg[:, n, d, 3, h8], HD), ALU.mult).then_inc(v_kw, 1)
                    dve.wait_ge(pe_sg, u + 1)
                    nc.vector.copy_predicated(sg[:, d, :, :], keep[d].bitcast(I32).unsqueeze(1).to_broadcast([P, NH, P]),
                                              ps[:, SG, :].rearrange("p (h t) -> p h t", t=P)).then_inc(v_sg, 1)
                    dve.wait_ge(a_ex, u + 1)
                    dve.wait_ge(pe_sm, u + 1)
                    nc.vector.tensor_tensor(ex[:, d, :, :], ex[:, d, :, :], ps[:, SM, :].rearrange("p (h t) -> p h t", t=P), ALU.mult).then_inc(v_w, 1)
                    dve.wait_ge(pe_og, u + 1)
                    if n in written:
                        nc.vector.tensor_tensor(og[:, n, :], og[:, n, :], ps[:, OG, 0:256], ALU.add).then_inc(v_og, 1)
                    else:
                        nc.vector.tensor_copy(og[:, n, :], ps[:, OG, 0:256]).then_inc(v_og, 1)
                    dve.wait_ge(pe_om, u + 1)
                    step(nc.vector.tensor_tensor(tmp[:, :, :], ps[:, OC, 0:260].rearrange("p (h c) -> p h c", c=65),
                                                 bc(tg[:, n, d, 1, h8], 65), ALU.mult))
                    nc.vector.tensor_tensor(num[:, :, :], tmp[:, :, :], ps[:, OI, 0:260].rearrange("p (h c) -> p h c", c=65),
                                            ALU.add).then_inc(v_om, 1)
                    dve.wait_ge(v_om, u + 1)
                    step(nc.vector.scalar_tensor_tensor(out=den[:, :], in0=num[:, :, 64], scalar=-1.0, in1=num[:, :, 64],
                                                        op0=ALU.mult, op1=ALU.max))
                    step(nc.vector.tensor_tensor(den[:, :], den[:, :], tg[:, n, d, 2, h8], ALU.max))
                    step(nc.vector.reciprocal(den[:, :], den[:, :]))
                    on = om[:, n, :].rearrange("p (h c) -> p h c", c=HD)
                    if n in written:
                        step(nc.vector.tensor_tensor(tmp[:, :, 0:HD], num[:, :, 0:HD], bc(den[:, :], HD), ALU.mult))
                        nc.vector.tensor_tensor(on, on, tmp[:, :, 0:HD], ALU.add)
                    else:
                        nc.vector.tensor_tensor(on, num[:, :, 0:HD], bc(den[:, :], HD), ALU.mult)
                    written.add(n)
                    dve.wait_ge(pe_u, u + 1)
                    nc.vector.scalar_tensor_tensor(out=dsg[:, :], in0=ps[:, OG, 256:512], scalar=em[:, d, 2, n:n + 1], in1=c("blockg"),
                                                   op0=ALU.mult, op1=ALU.mult)
                    nc.vector.tensor_tensor(dsm[:, :, :], ps[:, SG, 0:260].rearrange("p (a b) -> p a b", b=130),
                                            c("blockm").unsqueeze(1).to_broadcast([P, 2, 130]), ALU.mult)
                    step(nc.vector.tensor_tensor(Sm[:, d, :, :], Sm[:, d, :, :], bc(dcol[:, 2 * d:2 * d + 2, n], 130), ALU.mult))
                    step(nc.vector.scalar_tensor_tensor(out=Sg[:, d, :], in0=Sg[:, d, :], scalar=em[:, d, 1, n:n + 1], in1=dsg[:, :],
                                                        op0=ALU.mult, op1=ALU.add))
                    nc.vector.tensor_tensor(Sm[:, d, :, :], Sm[:, d, :, :], dsm[:, :, :], ALU.add)
                    nn = order(d, min(u // 2 + 1, NT - 1))
                    nc.vector.tensor_scalar(Sp[:, d, :], Sg[:, d, :], em[:, d, 0, nn:nn + 1], None, ALU.mult).then_inc(v_st, 1)
                    dve.wait_ge(v_st, u + 1)


def phase_mix_out(nc, io, S, l, TM, M, ctx_out):
    t0 = 0 if ctx_out else NCT
    tiles = list(range(t0, NT))
    with Phase(nc, f"mix{l}") as ph:
        sq = ph.sb("sq", [P, NT, 256])
        ms = ph.sb("ms", [P, NT, NH])
        ng = ph.sb("ng", [P, 256])
        turned = ph.sb("turned", [P, 2, 6, P])
        ld, ch, var, sd, gates, sqd, gd, gm, tr, ev, st = (ph.sem(n) for n in (
            "loaded", "dve_step", "var_ready", "sd_ready", "gates_ready", "squared", "gla_ready", "mlstm_ready", "transposed", "turned_ready", "stored"))
        ps, ident, og, om = S["ps"], S["c"]("ident"), M["og"], M["om"]
        with nc.Block() as block:

            @block.sync
            def _(sp):
                sp.dma_start(ng[:, :], io["gla_norm_g"][l].rearrange("(a n) -> a n", a=1).to_broadcast([P, 256])).then_inc(ld, 16)
                for i, n in enumerate(tiles):
                    sp.wait_ge(ev, i + 1)
                    sp.dma_start(S["mixT_d"][:, 0:6, n * P:(n + 1) * P], turned[:, i % 2, :, :]).then_inc(st, 16)
                    sp.wait_ge(st, 16 * (i + 1))

            @block.scalar
            def _(act):
                nc.scalar.activation(sq[:, t0:, :], og[:, t0:, :], ACT.Square).then_inc(sqd, 1)
                nc.scalar.activation(TM[:, t0:, 768:1024], TM[:, t0:, 768:1024], ACT.Sigmoid).then_inc(gates, 1)
                nc.scalar.activation(TM[:, t0:, 256:512], TM[:, t0:, 256:512], ACT.Silu).then_inc(gates, 1)
                act.wait_ge(var, 1)
                nc.scalar.activation(ms[:, t0:, :], ms[:, t0:, :], ACT.Sqrt).then_inc(sd, 1)

            @block.gpsimd
            def _(pool):
                pool.wait_ge(gates, 1)
                nc.gpsimd.tensor_tensor(om[:, t0:, :], om[:, t0:, :], TM[:, t0:, 768:1024], ALU.mult).then_inc(gm, 1)

            @block.vector
            def _(dve):
                step = Chain(dve, ch)
                dve.wait_ge(sqd, 1)
                step(nc.vector.tensor_reduce(ms[:, t0:, :], sq[:, t0:, :].rearrange("p n (h c) -> p n h c", c=HD), AX.X, ALU.add))
                nc.vector.tensor_scalar(ms[:, t0:, :], ms[:, t0:, :], 1.0 / HD, EPS, ALU.mult, ALU.add).then_inc(var, 1)
                dve.wait_ge(sd, 1)
                step(nc.vector.reciprocal(ms[:, t0:, :], ms[:, t0:, :]))
                dve.wait_ge(ld, 16)
                dve.wait_ge(gates, 2)
                for n in tiles:
                    o = og[:, n, :].rearrange("p (h c) -> p h c", c=HD)
                    step(nc.vector.tensor_tensor(o, o, bc(ms[:, n, :], HD), ALU.mult))
                    step(nc.vector.tensor_tensor(og[:, n, :], og[:, n, :], ng[:, :], ALU.mult))
                    nc.vector.tensor_tensor(og[:, n, :], og[:, n, :], TM[:, n, 256:512], ALU.mult).then_inc(gd, 1)
                for i, n in enumerate(tiles):
                    dve.wait_ge(tr, i + 1)
                    if i >= 2:
                        dve.wait_ge(st, 16 * (i - 1))
                    nc.vector.tensor_copy(turned[:, i % 2, :, :].rearrange("p k t -> p (k t)"),
                                          ps[:, 2 * (i % 2):2 * (i % 2) + 2, :].rearrange("p b t -> p (b t)")[:, 0:6 * P]).then_inc(ev, 1)

            @block.tensor
            def _(pe):
                pe.wait_ge(gm, 1)
                for i, n in enumerate(tiles):
                    pe.wait_ge(gd, i + 1)
                    if i >= 2:
                        pe.wait_ge(ev, i - 1)
                    for k in range(6):
                        src = (og, om)[k // 2][:, n, (k % 2) * P:(k % 2 + 1) * P] if k < 4 else TM[:, n, 1024 + (k - 4) * P:1024 + (k - 3) * P]
                        x = nc.tensor.transpose(ps[:, 2 * (i % 2) + k // 4, (k % 4) * P:(k % 4 + 1) * P], src, ident)
                    x.then_inc(tr, 1)


def phase_out_proj(nc, io, S, l, groups):
    with Phase(nc, f"op{l}") as ph:
        xT = ph.sb("xT", [P, KD, T])
        mT = ph.sb("mT", [P, KD, T])
        w = ph.sb("w", [P, KD, D])
        ld, mm_done, done, st = (ph.sem(n) for n in ("loaded", "mm_done", "added", "stored"))
        ps, mod = S["ps"], S["mod"]
        a = groups[0][0]
        units = [(d, t0, n) for d in range(KD) for t0, n in groups]
        with nc.Block() as block:

            @block.sync
            def _(sp):
                sp.dma_start(w[:, :, :], io["w_out"][l].rearrange("(k p) n -> p k n", p=P)).then_inc(ld, 16)
                sp.dma_start(mT[:, :, a:], S["mixT_d"][:, :, a:]).then_inc(ld, 16)
                sp.dma_start(xT[:, :, a:], S["xT_d"][:, :, a:]).then_inc(ld, 16)
                for d in range(KD):
                    sp.wait_ge(done, (d + 1) * len(groups))
                    sp.dma_start(S["xT_d"][:, d, a:], xT[:, d, a:]).then_inc(st, 16)
                sp.wait_ge(st, 16 * KD)

            @block.tensor
            def _(pe):
                pe.wait_ge(ld, 48)
                for u, (d, t0, n) in enumerate(units):
                    if u >= 8:
                        pe.wait_ge(done, u - 7)
                    for k in range(KD):
                        x = nc.tensor.matmul(ps[:, u % 8, :n], w[:, k, d * P:(d + 1) * P], mT[:, k, t0:t0 + n], start=(k == 0), stop=(k == KD - 1))
                    x.then_inc(mm_done, 1)

            @block.vector
            def _(dve):
                dve.wait_ge(ld, 48)
                for u, (d, t0, n) in enumerate(units):
                    dve.wait_ge(mm_done, u + 1)
                    j = 1 if t0 < CTX else 0
                    nc.vector.scalar_tensor_tensor(out=xT[:, d, t0:t0 + n], in0=ps[:, u % 8, :n], scalar=mod[:, l, 16 + d, j:j + 1],
                                                   in1=xT[:, d, t0:t0 + n], op0=ALU.mult, op1=ALU.add).then_inc(done, 1)


def phase_ffn_up(nc, io, S, hT, aT):
    NC = DFF // P
    with Phase(nc, "up") as ph:
        wg = ph.sb("wg", [P, 2, KD, P])
        wu = ph.sb("wu", [P, 2, KD, P])
        sil = ph.sb("sil", [P, 3, 512])
        wl = [ph.sem(f"w_loaded{s}") for s in range(2)]
        wfree, g_done, u_done, silu_ready, used = (ph.sem(n) for n in ("w_slot_free", "gate_done", "up_done", "silu_ready", "banks_free"))
        ps = S["ps"]
        gsrc, usrc = (io[n][0].rearrange("(k p) n -> p k n", p=P) for n in ("ffn_w_gate", "ffn_w_up"))
        with nc.Block() as block:

            @block.sync
            def _(sp):
                with sp.Fori(0, NC // 2) as i:
                    for s in range(2):
                        sp.wait_ge(wfree, i * 2 + (s + 1))
                        sp.dma_start(wg[:, s, :, :], gsrc[:, :, bass.ds(i * 256 + s * P, P)]).then_inc(wl[s], 16)
                        sp.dma_start(wu[:, s, :, :], usrc[:, :, bass.ds(i * 256 + s * P, P)]).then_inc(wl[s], 16)

            @block.tensor
            def _(pe):
                pe.sem_inc(wfree, 2)
                with pe.Fori(0, NC // 2) as i:
                    for s in range(2):
                        pe.wait_ge(wl[s], i * 32 + 32)
                        for g, (t0, n) in enumerate(GROUPS):
                            pe.wait_ge(used, i * 6 + (3 * s + g + 1))
                            for k in range(KD):
                                x = nc.tensor.matmul(ps[:, 2 * g, :n], wg[:, s, k, :], hT[:, k, t0:t0 + n], start=(k == 0), stop=(k == KD - 1))
                            x.then_inc(g_done, 1)
                            for k in range(KD):
                                x = nc.tensor.matmul(ps[:, 2 * g + 1, :n], wu[:, s, k, :], hT[:, k, t0:t0 + n], start=(k == 0), stop=(k == KD - 1))
                            x.then_inc(u_done, 1)
                        pe.wait_ge(u_done, i * 6 + 3 * (s + 1))
                        pe.sem_inc(wfree, 1)

            @block.scalar
            def _(act):
                with act.Fori(0, NC // 2) as i:
                    for s in range(2):
                        for g, (t0, n) in enumerate(GROUPS):
                            act.wait_ge(g_done, i * 6 + (3 * s + g + 1))
                            act.wait_ge(used, i * 6 + (3 * s + g + 1))
                            nc.scalar.activation(sil[:, g, :n], ps[:, 2 * g, :n], ACT.Silu).then_inc(silu_ready, 1)

            @block.vector
            def _(dve):
                dve.sem_inc(used, 3)
                with dve.Fori(0, NC // 2) as i:
                    for s in range(2):
                        for g, (t0, n) in enumerate(GROUPS):
                            dve.wait_ge(silu_ready, i * 6 + (3 * s + g + 1))
                            dve.wait_ge(u_done, i * 6 + (3 * s + g + 1))
                            nc.vector.tensor_tensor(aT[:, bass.ds(i * (2 * T) + (s * T + t0), n)], sil[:, g, :n], ps[:, 2 * g + 1, :n],
                                                    ALU.mult).then_inc(used, 1)
                dve.wait_ge(used, 3 * NC + 3)


def phase_ffn_down(nc, io, S, aT):
    NC = DFF // P
    with Phase(nc, "down") as ph:
        wd = ph.sb("wd", [P, 2, NC, P])
        xs = ph.sb("xs", [P, 2, T])
        wl = [ph.sem(f"w_loaded{s}") for s in range(2)]
        st = [ph.sem(f"stored{s}") for s in range(2)]
        mm_done, added = ph.sem("mm_done"), ph.sem("added")
        ps, mod = S["ps"], S["mod"]
        src = io["ffn_w_down"][0].rearrange("(f p) n -> p f n", p=P)
        with nc.Block() as block:

            @block.sync
            def _(sp):
                for d in range(KD):
                    s = d % 2
                    if d >= 2:
                        sp.wait_ge(mm_done, 3 * (d - 1))
                        sp.wait_ge(st[s], 16 * (d // 2))
                    sp.dma_start(wd[:, s, :, :], src[:, :, d * P:(d + 1) * P]).then_inc(wl[s], 16)
                    sp.dma_start(xs[:, s, :], S["xT_d"][:, d, :]).then_inc(wl[s], 16)

            @block.tensor
            def _(pe):
                for d in range(KD):
                    s = d % 2
                    pe.wait_ge(wl[s], 32 * (d // 2 + 1))
                    for g, (t0, n) in enumerate(GROUPS):
                        if d >= 2:
                            pe.wait_ge(added, 3 * (d - 2) + g + 1)
                        for f in range(NC):
                            x = nc.tensor.matmul(ps[:, 3 * s + g, :n], wd[:, s, f, :], aT[:, f * T + t0:f * T + t0 + n],
                                                 start=(f == 0), stop=(f == NC - 1))
                        x.then_inc(mm_done, 1)

            @block.vector
            def _(dve):
                for d in range(KD):
                    s = d % 2
                    dve.wait_ge(wl[s], 32 * (d // 2 + 1))
                    for g, (t0, n) in enumerate(GROUPS):
                        dve.wait_ge(mm_done, 3 * d + g + 1)
                        j = 1 if t0 < CTX else 0
                        nc.vector.scalar_tensor_tensor(out=xs[:, s, t0:t0 + n], in0=ps[:, 3 * s + g, :n], scalar=mod[:, 0, 40 + d, j:j + 1],
                                                       in1=xs[:, s, t0:t0 + n], op0=ALU.mult, op1=ALU.add).then_inc(added, 1)

            @block.scalar
            def _(act):
                for d in range(KD):
                    s = d % 2
                    act.wait_ge(added, 3 * (d + 1))
                    act.dma_start(S["xT_d"][:, d, :], xs[:, s, :]).then_inc(st[s], 16)
                for s in range(2):
                    act.wait_ge(st[s], 16 * (KD // 2))


def phase_route(nc, io, S, hT, R):
    NX = SEQ // P
    with Phase(nc, "route") as ph:
        wr = ph.sb("wr", [P, KD, NE])
        L = ph.sb("L", [P, NX, NE])
        sel = ph.sb("sel", [P, 2, NX, NE])
        both = ph.sb("both", [P, NX, NE])
        t = ph.sb("t", [P, NX, NE])
        m = ph.sb("m", [P, 2, NX])
        r = ph.sb("r", [P, NX])
        cnt = ph.sb("cnt", [P, NE])
        ind = ph.sb("ind", [P, NE, NE])
        nb = ph.sb("nb", [P, NE])
        end = ph.sb("end", [P, NE])
        start = ph.sb("start", [P, NE])
        indb = ph.sb("indb", [P, NUNIT, NE])
        indc = ph.sb("indc", [P, NUNIT, NE])
        ebf = ph.sb("ebf", [P, NUNIT])
        slotf = ph.sb("slotf", [P, 2, NX])
        ex = ph.sb("ex", [P, NX])
        rows = ph.sb("rows", [P, 2, D])
        zero = ph.sb("zero", [P, D])
        wl, zr, zf, lg, ch, sel_ready, pre, dif, exr, slots, tr, rv, g2s = (ph.sem(n) for n in (
            "router_loaded", "zero_ready", "slots_zeroed", "logits_done", "dve_step", "choice_ready", "ranks_done", "gap_ready", "exp_ready",
            "slots_ready", "rows_transposed", "rows_ready", "g2_stored"))
        sc = [ph.sem(f"scattered{s}") for s in range(2)]
        ps, c = S["ps"], S["c"]
        with nc.Block() as block:

            @block.sync
            def _(sp):
                sp.dma_start(wr[:, :, :], io["moe_router"][0].rearrange("(k p) e -> p k e", p=P)).then_inc(wl, 16)
                sp.wait_ge(zr, 1)
                sp.dma_start(S["xs_d"].rearrange("(b p) d -> p b d", p=P), zero[:, :].unsqueeze(1).to_broadcast([P, 2 * (NUNIT + 1), D])).then_inc(zf, 16)
                with nc.allow_non_contiguous_dma(reason="a column set as a vector"):
                    sp.dma_start(cols(S["g2_d"]), S["mod"][:, 1, 40:48, 0]).then_inc(g2s, 16)
                sp.wait_ge(g2s, 16)

            @block.tensor
            def _(pe):
                pe.wait_ge(wl, 16)
                for n in range(NX):
                    for k in range(KD):
                        x = nc.tensor.matmul(ps[:, 0, n * NE:(n + 1) * NE], hT[:, k, CTX + n * P:CTX + (n + 1) * P], wr[:, k, :],
                                             start=(k == 0), stop=(k == KD - 1))
                x.then_inc(lg, 1)
                pe.wait_ge(sel_ready, 1)
                for n in range(NX):
                    for i in range(n + 1):
                        nc.tensor.matmul(ps[:, 1, n * NE:(n + 1) * NE], c("tri") if i == n else c("ones"), both[:, i, :], start=(i == 0), stop=(i == n))
                for i in range(NX):
                    x = nc.tensor.matmul(ps[:, 2, 0:NE], c("ones"), both[:, i, :], start=(i == 0), stop=(i == NX - 1))
                x.then_inc(pre, 1)
                for n in range(NX):
                    if n >= 2:
                        pe.wait_ge(rv, n - 1)
                    for k in range(KD):
                        b = 4 + 2 * (n % 2) + k // 4
                        x = nc.tensor.transpose(ps[:, b, (k % 4) * P:(k % 4 + 1) * P], hT[:, k, CTX + n * P:CTX + (n + 1) * P], c("ident"))
                    x.then_inc(tr, 1)

            @block.vector
            def _(dve):
                step = Chain(dve, ch)
                pref = c("pref").unsqueeze(1).to_broadcast([P, NX, NE])
                dve.wait_ge(lg, 1)
                step(nc.vector.tensor_copy(L[:, :, :], ps[:, 0, 0:NX * NE].rearrange("p (n e) -> p n e", e=NE)))
                for i in range(2):
                    step(nc.vector.tensor_reduce(m[:, i, :], L[:, :, :], AX.X, ALU.max))
                    step(nc.vector.tensor_tensor(t[:, :, :], L[:, :, :], bc(m[:, i, :], NE), ALU.is_equal))
                    step(nc.vector.tensor_tensor(t[:, :, :], t[:, :, :], pref, ALU.mult))
                    step(nc.vector.tensor_reduce(r[:, :], t[:, :, :], AX.X, ALU.max))
                    step(nc.vector.tensor_tensor(sel[:, i, :, :], pref, bc(r[:, :], NE), ALU.is_equal))
                    if i == 0:
                        step(nc.vector.scalar_tensor_tensor(out=L[:, :, :], in0=sel[:, 0, :, :], scalar=-BIG, in1=L[:, :, :], op0=ALU.mult, op1=ALU.add))
                nc.vector.tensor_tensor(both[:, :, :], sel[:, 0, :, :], sel[:, 1, :, :], ALU.add).then_inc(sel_ready, 1)
                nc.vector.tensor_tensor(ex[:, :], m[:, 1, :], m[:, 0, :], ALU.subtract).then_inc(dif, 1)
                dve.wait_ge(exr, 1)
                step(nc.vector.tensor_scalar(r[:, :], ex[:, :], 1.0, None, ALU.add))
                step(nc.vector.reciprocal(R["gate"][:, 0, :], r[:, :]))
                step(nc.vector.tensor_tensor(R["gate"][:, 1, :], R["gate"][:, 0, :], ex[:, :], ALU.mult))
                dve.wait_ge(pre, 1)
                step(nc.vector.tensor_copy(cnt[:, :], ps[:, 2, 0:NE]))
                step(nc.vector.tensor_tensor(ind[:, :, :], bc(cnt[:, :], NE), c("koff").unsqueeze(1).to_broadcast([P, NE, NE]), ALU.is_gt))
                step(nc.vector.tensor_reduce(nb[:, :], ind[:, :, :], AX.X, ALU.add))
                step(nc.vector.tensor_tensor_scan(end[:, :], c("ones")[:, 0:NE], nb[:, :], 0.0, ALU.mult, ALU.add))
                step(nc.vector.tensor_tensor(start[:, :], end[:, :], nb[:, :], ALU.subtract))
                step(nc.vector.tensor_scalar(start[:, :], start[:, :], float(UNIT), None, ALU.mult))
                step(nc.vector.tensor_tensor(t[:, :, :], ps[:, 1, 0:NX * NE].rearrange("p (n e) -> p n e", e=NE),
                                             start[:, :].unsqueeze(1).to_broadcast([P, NX, NE]), ALU.add))
                for i in range(2):
                    step(nc.vector.tensor_tensor(sel[:, i, :, :], sel[:, i, :, :], t[:, :, :], ALU.mult))
                    step(nc.vector.tensor_reduce(slotf[:, i, :], sel[:, i, :, :], AX.X, ALU.add))
                step(nc.vector.tensor_tensor(indb[:, :, :], bc(c("blk"), NE), end[:, :].unsqueeze(1).to_broadcast([P, NUNIT, NE]), ALU.is_ge))
                step(nc.vector.tensor_reduce(ebf[:, :], indb[:, :, :], AX.X, ALU.add))
                step(nc.vector.tensor_scalar(ebf[:, :], ebf[:, :], float(NE - 1), None, ALU.min))
                step(nc.vector.tensor_copy(R["expert"][:, :], ebf[:, :]))
                step(nc.vector.tensor_tensor(cnt[:, :], cnt[:, :], start[:, :], ALU.add))
                step(nc.vector.tensor_tensor(indb[:, :, :], bc(c("half"), NE), cnt[:, :].unsqueeze(1).to_broadcast([P, NUNIT, NE]), ALU.is_lt))
                step(nc.vector.tensor_tensor(indc[:, :, :], bc(c("half"), NE), start[:, :].unsqueeze(1).to_broadcast([P, NUNIT, NE]), ALU.is_gt))
                step(nc.vector.tensor_tensor(indb[:, :, :], indb[:, :, :], indc[:, :, :], ALU.mult))
                step(nc.vector.tensor_reduce(ebf[:, :], indb[:, :, :], AX.X, ALU.max))
                step(nc.vector.tensor_copy(R["second"][:, :], ebf[:, :]))
                nc.vector.tensor_copy(R["slot"][:, :, :], slotf[:, :, :]).then_inc(slots, 1)
                for n in range(NX):
                    dve.wait_ge(tr, n + 1)
                    if n >= 2:
                        dve.wait_ge(sc[n % 2], 32 * (n // 2))
                    nc.vector.tensor_copy(rows[:, n % 2, :], ps[:, 4 + 2 * (n % 2):6 + 2 * (n % 2), :].rearrange("p b t -> p (b t)")).then_inc(rv, 1)

            @block.scalar
            def _(act):
                act.wait_ge(dif, 1)
                nc.scalar.activation(ex[:, :], ex[:, :], ACT.Exp).then_inc(exr, 1)

            @block.gpsimd
            def _(pool):
                nc.gpsimd.memset(zero[:, :], 0.0).then_inc(zr, 1)
                pool.wait_ge(zf, 16)
                pool.wait_ge(slots, 1)
                for n in range(NX):
                    pool.wait_ge(rv, n + 1)
                    for i in range(2):
                        nc.gpsimd.indirect_dma_start(
                            out=S["xs_d"][:, :], out_offset=bass.IndirectOffsetOnAxis(ap=R["slot"][:, i, n:n + 1], axis=0),
                            in_=rows[:, n % 2, :], in_offset=None).then_inc(sc[n % 2], 16)
                for s in range(2):
                    pool.wait_ge(sc[s], 32 * (NX // 2))


def phase_experts(nc, io, S, R):
    NF = DFE // P
    PAIRS = NF // 2
    RING = 4
    with Phase(nc, "moe") as ph:
        wst = ph.sb("wst", [P, 2, 3, 2 * KD * P])
        wh = ph.sb("wh", [P, RING, 3, KD * P], F32R)
        wlo = ph.sb("wl", [P, RING, 3, KD * P], F32R)
        rows = ph.sb("rows", [P, 2, D])
        xh = ph.sb("xh", [P, KD, 2 * P], F32R)
        xl = ph.sb("xl", [P, KD, 2 * P], F32R)
        sil = ph.sb("sil", [P, 2 * P])
        a = ph.sb("a", [P, 2, 2 * P])
        ah = ph.sb("ah", [P, 2, 2 * P], F32R)
        al = ph.sb("al", [P, 2, 2 * P], F32R)
        y = ph.sb("y", [P, 2, D])
        wl = [[ph.sem(f"{k}_loaded{s}") for k in ("gate", "up", "down")] for s in range(2)]
        hi, split, gdone, udone, ddone, silu, prod, ahr, alr, rl, xtr, xhr, xlr, yev, yst, yfree = (ph.sem(n) for n in (
            "weights_hi", "weights_split", "gate_done", "up_done", "down_done", "silu_ready", "product_ready", "product_hi", "product_split",
            "rows_loaded", "rows_transposed", "rows_hi", "rows_split", "y_read", "y_stored", "y_free"))
        ps, ident = S["ps"], S["c"]("ident")
        Y0 = 4
        gw, uw, dw = io["moe_w_gate"][0], io["moe_w_up"][0], io["moe_w_down"][0]
        xs_b = S["xs_d"].rearrange("(b i p) d -> b i p d", p=P, i=2)
        ys_b = S["ys_d"].rearrange("(b i p) d -> b i p d", p=P, i=2)

        def chunk(kind, f):
            t = wst[:, (f // 2) % 2, kind, :]
            if kind == 2:
                return t.rearrange("p (c n) -> p c n", c=2)[:, f % 2, :]
            return t.rearrange("p (k n) -> p k n", k=KD)[:, :, (f % 2) * P:(f % 2 + 1) * P]

        def split_ap(w, kind, f):
            t = w[:, f % RING, kind, :]
            return t if kind == 2 else t.rearrange("p (k n) -> p k n", k=KD)

        def turn_bank(s):
            return (0, 2, 1, 3)[s], s // 2, s % 2

        with nc.Block() as block:

            @block.sync
            def _(sp):
                with sp.Fori(0, NUNIT) as b:
                    e = sp.value_load(R["expert"][0:1, bass.ds(b, 1)], min_val=0, max_val=NE - 1)
                    for p in range(PAIRS):
                        sp.wait_ge(split, b * NF + (2 * p + 2))
                        dst = wst[:, p % 2, :, :]
                        for kind, w in ((0, gw), (1, uw)):
                            sp.dma_start(dst[:, kind, :].rearrange("p (k n) -> p k n", k=KD),
                                         w[bass.ds(e, 1), :, 2 * P * p:2 * P * (p + 1)].rearrange("a (k p) n -> p (a k) n", p=P)).then_inc(wl[p % 2][kind], 16)
                        sp.dma_start(dst[:, 2, :].rearrange("p (c n) -> p c n", c=2),
                                     dw[bass.ds(e, 1), 2 * P * p:2 * P * (p + 1), :].rearrange("a (c p) n -> p (a c) n", p=P)).then_inc(wl[p % 2][2], 16)

            @block.gpsimd
            def _(pool):
                pool.sem_inc(yfree, 1)
                pool.dma_start(rows[:, :, :], xs_b[0].rearrange("i p d -> p i d")).then_inc(rl, 16)
                with pool.Fori(0, NUNIT) as b:
                    pool.wait_ge(xtr, b * 4 + 4)
                    pool.dma_start(rows[:, :, :], xs_b[bass.ds(b + 1, 1)].rearrange("a i p d -> p (a i) d")).then_inc(rl, 16)
                    pool.wait_ge(yev, b + 2)
                    pool.dma_start(ys_b[bass.ds(b, 1)].rearrange("a i p d -> p (a i) d"), y[:, :, :]).then_inc(yst, 16)
                    pool.wait_ge(yst, b * 16 + 16)
                    pool.sem_inc(yfree, 1)
                pool.wait_ge(rl, 16 * (NUNIT + 1))

            @block.tensor
            def _(pe):
                pe.sem_inc(ddone, RING)

                def turn_rows(s):
                    bank, i, kh = turn_bank(s)
                    for k in range(4):
                        x = nc.tensor.transpose(ps[:, bank, k * P:(k + 1) * P], rows[:, i, (4 * kh + k) * P:(4 * kh + k + 1) * P], ident)
                    x.then_inc(xtr, 1)

                pe.wait_ge(rl, 16)
                for s in range(4):
                    turn_rows(s)
                with pe.Fori(0, NUNIT) as b:
                    second = pe.value_load(R["second"][0:1, bass.ds(b, 1)], min_val=0, max_val=1)

                    def up(kind, f, n, done):
                        h, l = split_ap(wh, kind, f), split_ap(wlo, kind, f)
                        for k in range(KD):
                            for i, (w, xx) in enumerate(((h, xh), (h, xl), (l, xh))):
                                x = nc.tensor.matmul(ps[:, 2 * kind + f % 2, 0:n], w[:, k, :], xx[:, k, 0:n],
                                                     start=(k == 0 and i == 0), stop=(k == KD - 1 and i == 2))
                        x.then_inc(done, 1)

                    def down(f, tiles):
                        h, l = split_ap(wh, 2, f), split_ap(wlo, 2, f)
                        for i in range(tiles):
                            t = slice(i * P, (i + 1) * P)
                            for j, (aa, w) in enumerate(((ah, h), (ah, l), (al, h))):
                                for half in range(2):
                                    x = nc.tensor.matmul(ps[:, Y0 + 2 * i + half, :], aa[:, f % 2, t], w[:, half * 512:(half + 1) * 512],
                                                         start=(f == 0 and j == 0), stop=(f == NF - 1 and j == 2))
                        x.then_inc(ddone, 1)

                    def chunk_step(f, tiles):
                        if f < NF:
                            pe.wait_ge(split, b * NF + (f + 5))
                            pe.wait_ge(silu, b * NF + (f + 1))
                            up(0, f, tiles * P, gdone)
                            pe.wait_ge(prod, b * NF + (f + 1))
                            up(1, f, tiles * P, udone)
                        if f == NF:
                            pe.wait_ge(rl, b * 16 + 32)
                            pe.wait_ge(silu, b * NF + (NF + 1))
                            pe.wait_ge(prod, b * NF + (NF + 1))
                            turn_rows(0)
                            turn_rows(1)
                        if f >= 1:
                            pe.wait_ge(alr, b * NF + f)
                            if f == 1:
                                pe.wait_ge(yev, b + 1)
                            down(f - 1, tiles)
                        if f == NF:
                            pe.wait_ge(prod, b * NF + (NF + 2))
                            pe.wait_ge(silu, b * NF + (NF + 2))
                            turn_rows(2)
                            turn_rows(3)

                    pe.wait_ge(xlr, b * 4 + 4)
                    for f in range(NF + 1):
                        with pe.If(second):
                            chunk_step(f, 2)
                        with pe.Else():
                            chunk_step(f, 1)

            @block.scalar
            def _(act):
                act.sem_inc(silu, 2)

                def rows_hi(n0, s):
                    bank, i, kh = turn_bank(s)
                    act.wait_ge(xtr, n0 + (s + 1))
                    nc.scalar.copy(xh[:, 4 * kh:4 * kh + 4, i * P:(i + 1) * P], ps[:, bank, :].rearrange("p (k t) -> p k t", t=P)).then_inc(xhr, 1)

                for s in range(4):
                    rows_hi(0, s)
                with act.Fori(0, NUNIT) as b:

                    def weights_hi(f, kind):
                        act.wait_ge(wl[(f // 2) % 2][kind], b * (16 * (PAIRS // 2)) + 16 * (f // 4 + 1))
                        act.wait_ge(ddone, b * NF + (f + 1))
                        nc.scalar.copy(split_ap(wh, kind, f), chunk(kind, f)).then_inc(hi, 1)

                    for f in range(RING - 1):
                        for kind in range(3):
                            weights_hi(f, kind)
                    for f in range(NF):
                        act.wait_ge(gdone, b * NF + (f + 1))
                        act.wait_ge(prod, b * NF + (f + 2))
                        nc.scalar.activation(sil[:, :], ps[:, f % 2, 0:2 * P], ACT.Silu).then_inc(silu, 1)
                        g = f + RING - 1
                        if g < NF:
                            weights_hi(g, 0)
                        act.wait_ge(prod, b * NF + (f + 3))
                        nc.scalar.copy(ah[:, f % 2, :], a[:, f % 2, :]).then_inc(ahr, 1)
                        if g < NF:
                            weights_hi(g, 1)
                            weights_hi(g, 2)
                    for s in range(4):
                        rows_hi(b * 4 + 4, s)

            @block.vector
            def _(dve):
                dve.sem_inc(prod, 2)
                dve.sem_inc(yev, 1)
                dve.sem_inc(split, 4)

                def rows_lo(n0, s):
                    bank, i, kh = turn_bank(s)
                    dve.wait_ge(xhr, n0 + (s + 1))
                    o = (slice(None), slice(4 * kh, 4 * kh + 4), slice(i * P, (i + 1) * P))
                    nc.vector.tensor_tensor(xl[o], ps[:, bank, :].rearrange("p (k t) -> p k t", t=P), xh[o].bitcast(F32), ALU.subtract).then_inc(xlr, 1)

                for s in range(4):
                    rows_lo(0, s)
                with dve.Fori(0, NUNIT) as b:

                    def weights_lo(f, kind):
                        dve.wait_ge(hi, b * (3 * NF) + (3 * f + kind + 1))
                        x = nc.vector.tensor_tensor(split_ap(wlo, kind, f), chunk(kind, f), split_ap(wh, kind, f).bitcast(F32), ALU.subtract)
                        if kind == 2:
                            x.then_inc(split, 1)

                    for f in range(RING - 1):
                        for kind in range(3):
                            weights_lo(f, kind)
                    for f in range(NF):
                        g = f + RING - 1
                        dve.wait_ge(silu, b * NF + (f + 3))
                        dve.wait_ge(udone, b * NF + (f + 1))
                        nc.vector.tensor_tensor(a[:, f % 2, :], sil[:, :], ps[:, 2 + f % 2, 0:2 * P], ALU.mult).then_inc(prod, 1)
                        if g < NF:
                            weights_lo(g, 0)
                        dve.wait_ge(ahr, b * NF + (f + 1))
                        nc.vector.tensor_tensor(al[:, f % 2, :], a[:, f % 2, :], ah[:, f % 2, :].bitcast(F32), ALU.subtract).then_inc(alr, 1)
                        if g < NF:
                            weights_lo(g, 1)
                            weights_lo(g, 2)
                    for s in range(4):
                        rows_lo(b * 4 + 4, s)
                    dve.wait_ge(ddone, b * NF + (NF + RING))
                    dve.wait_ge(yfree, b + 1)
                    for i in range(2):
                        x = nc.vector.tensor_copy(y[:, i, :], ps[:, Y0 + 2 * i:Y0 + 2 * i + 2, :].rearrange("p b t -> p (b t)"))
                    x.then_inc(yev, 1)


def phase_final(nc, io, S, R):
    NX = SEQ // P
    with Phase(nc, "fin") as ph:
        xT = ph.sb("xT", [P, KD, SEQ])
        g2 = ph.sb("g2", [P, D])
        fg = ph.sb("fg", [P, D])
        y = ph.sb("y", [P, 2, 2, D])
        x = ph.sb("x", [P, 2, D])
        sq = ph.sb("sq", [P, D])
        ss = ph.sb("ss", [P, NX])
        ld, tr, ch, xr, va, sr, od = (ph.sem(n) for n in ("loaded", "transposed", "dve_step", "x_ready", "var_ready", "sd_ready", "out_ready"))
        gl = [ph.sem(f"gathered{s}") for s in range(2)]
        st = [ph.sem(f"stored{s}") for s in range(2)]
        ps, ident = S["ps"], S["c"]("ident")
        with nc.Block() as block:

            @block.sync
            def _(sp):
                sp.dma_start(xT[:, :, :], S["xT_d"][:, :, CTX:]).then_inc(ld, 16)
                sp.dma_start(g2[:, :], S["g2_d"].rearrange("(a n) -> a n", a=1).to_broadcast([P, D])).then_inc(ld, 16)
                sp.dma_start(fg[:, :], io["final_norm_g"].rearrange("(a n) -> a n", a=1).to_broadcast([P, D])).then_inc(ld, 16)
                for n in range(NX):
                    sp.wait_ge(od, n + 1)
                    sp.dma_start(io["out"][0, n * P:(n + 1) * P, :], x[:, n % 2, :]).then_inc(st[n % 2], 16)
                for s in range(2):
                    sp.wait_ge(st[s], 16 * (NX // 2))

            @block.gpsimd
            def _(pool):
                for n in range(NX):
                    if n >= 2:
                        pool.wait_ge(xr, n - 1)
                    for i in range(2):
                        nc.gpsimd.indirect_dma_start(
                            out=y[:, n % 2, i, :], out_offset=None, in_=S["ys_d"][:, :],
                            in_offset=bass.IndirectOffsetOnAxis(ap=R["slot"][:, i, n:n + 1], axis=0)).then_inc(gl[n % 2], 16)

            @block.tensor
            def _(pe):
                pe.wait_ge(ld, 48)
                for n in range(NX):
                    if n >= 2:
                        pe.wait_ge(xr, n - 1)
                    for k in range(KD):
                        t = nc.tensor.transpose(ps[:, 2 * (n % 2) + k // 4, (k % 4) * P:(k % 4 + 1) * P], xT[:, k, n * P:(n + 1) * P], ident)
                    t.then_inc(tr, 1)

            @block.scalar
            def _(act):
                for n in range(NX):
                    act.wait_ge(xr, n + 1)
                    if n >= 1:
                        act.wait_ge(va, n)
                    nc.scalar.activation(sq[:, :], x[:, n % 2, :], ACT.Square, accum_out=ss[:, n:n + 1]).then_inc(sr, 1)
                    act.wait_ge(va, n + 1)
                    nc.scalar.activation(ss[:, n:n + 1], ss[:, n:n + 1], ACT.Sqrt).then_inc(sr, 1)

            @block.vector
            def _(dve):
                step = Chain(dve, ch)
                dve.wait_ge(ld, 48)
                for n in range(NX):
                    s = n % 2
                    dve.wait_ge(gl[s], 32 * (n // 2 + 1))
                    if n >= 2:
                        dve.wait_ge(st[s], 16 * (n // 2))
                    step(nc.vector.tensor_scalar(y[:, s, 0, :], y[:, s, 0, :], R["gate"][:, 0, n:n + 1], None, ALU.mult))
                    step(nc.vector.scalar_tensor_tensor(out=y[:, s, 0, :], in0=y[:, s, 1, :], scalar=R["gate"][:, 1, n:n + 1],
                                                        in1=y[:, s, 0, :], op0=ALU.mult, op1=ALU.add))
                    step(nc.vector.tensor_tensor(y[:, s, 0, :], y[:, s, 0, :], g2[:, :], ALU.mult))
                    dve.wait_ge(tr, n + 1)
                    nc.vector.tensor_tensor(x[:, s, :], y[:, s, 0, :], ps[:, 2 * s:2 * s + 2, :].rearrange("p b t -> p (b t)"), ALU.add).then_inc(xr, 1)
                    dve.wait_ge(sr, 2 * n + 1)
                    nc.vector.tensor_scalar(ss[:, n:n + 1], ss[:, n:n + 1], 1.0 / D, EPS, ALU.mult, ALU.add).then_inc(va, 1)
                    dve.wait_ge(sr, 2 * n + 2)
                    step(nc.vector.reciprocal(ss[:, n:n + 1], ss[:, n:n + 1]))
                    nc.vector.scalar_tensor_tensor(out=x[:, s, :], in0=x[:, s, :], scalar=ss[:, n:n + 1], in1=fg[:, :],
                                                   op0=ALU.mult, op1=ALU.mult).then_inc(od, 1)


INPUTS = ["x", "c", "ctx", "c_ctx", "w_ada", "b_ada", "norm_mix_g", "norm_ffn_g", "w_in", "w_out", "gla_w_lr", "gla_b_lr",
          "gla_norm_g", "mlstm_conv", "mlstm_gate_b", "sgu_w", "sgu_b", "ffn_w_gate", "ffn_w_up", "ffn_w_down", "moe_router",
          "moe_w_gate", "moe_w_up", "moe_w_down", "final_norm_g", "cst", "dft_seq", "dft_ctx"]


def build(nc, io):
    S = {name: nc.dram_tensor(name, shape, F32, kind="Internal").ap() for name, shape in
         (("xT_d", (P, KD, T)), ("mixT_d", (P, KD, T)), ("xs_d", ((NUNIT + 1) * UNIT, D)), ("ys_d", (NUNIT * UNIT, D)), ("g2_d", (D,)))}
    with ExitStack() as top:
        def sb(stack, name, shape, dt=F32):
            return stack.enter_context(nc.sbuf_tensor(name, shape, dt))

        S["ps"] = top.enter_context(nc.psum_tensor("ps", [P, 8, 512], F32))
        S["cst"] = sb(top, "cst", [P, NCST])
        S["c"] = lambda name: S["cst"][:, CST[name][0]:CST[name][0] + CST[name][1]]
        S["mod"] = sb(top, "mod", [P, 2, 48, 2])
        S["gmod"] = sb(top, "gmod", [P, 2, 2, 2, KD])
        R = {"slot": sb(top, "slot", [P, 2, SEQ // P], I32), "gate": sb(top, "gate", [P, 2, SEQ // P]),
             "expert": sb(top, "expert", [P, NUNIT], I32), "second": sb(top, "second", [P, NUNIT], I32)}
        phase_modulation(nc, io, S)
        phase_to_features(nc, io, S)
        for l in range(2):
            ctx_out = l == 0
            groups = GROUPS if ctx_out else GROUPS[1:]
            with ExitStack() as lay:
                FM = sb(lay, f"FM{l}", [P, 9, T])
                TM = sb(lay, f"TM{l}", [P, NT, 1536])
                with ExitStack() as st:
                    hT = sb(st, f"hT{l}", [P, KD, T])
                    xT = TM[:, 0:7, :].rearrange("p a b -> p (a b)")[:, 0:KD * T].rearrange("p (k t) -> p k t", t=T)
                    phase_norm(nc, S, f"nm{l}", xT, hT, l, 0, GROUPS)
                    phase_project(nc, io, S, l, hT, FM, TM, ctx_out)
                phase_fourier(nc, io, S, l, FM, ctx_out)
                phase_sgu(nc, io, S, l, TM, ctx_out)
                M = {}
                M["qd"] = sb(lay, f"qd{l}", [P, 2, T])
                M["kd"] = sb(lay, f"kd{l}", [P, 2, T])
                M["em"] = sb(lay, f"em{l}", [P, 2, 3, NT])
                M["mx"] = sb(lay, f"mx{l}", [8, 2, T])
                M["ig"] = sb(lay, f"ig{l}", [8, T])
                M["tg"] = sb(lay, f"tg{l}", [P, NT, 2, 4, 8])
                M["dcol"] = sb(lay, f"dcol{l}", [P, 4, NT])
                phase_decays(nc, io, S, l, FM, M)
                M["vx"] = sb(lay, f"vx{l}", [P, NT, NH, 65])
                for name, ch in (("og", 2), ("om", 4)):
                    M[name] = FM[:, ch:ch + 2, :].rearrange("p a b -> p (a b)").rearrange("p (n c) -> p n c", c=256)
                phase_conv(nc, io, S, l, FM, TM, M)
                phase_scan(nc, io, S, l, FM, TM, M)
                phase_mix_out(nc, io, S, l, TM, M, ctx_out)
            phase_out_proj(nc, io, S, l, groups)
            with ExitStack() as lay:
                hT = sb(lay, f"hF{l}", [P, KD, T])
                with ExitStack() as st:
                    xT = sb(st, f"xF{l}", [P, KD, T])
                    phase_norm(nc, S, f"nf{l}", xT, hT, l, 1, groups)
                if l == 0:
                    aT = sb(lay, "aT", [P, (DFF // P) * T])
                    phase_ffn_up(nc, io, S, hT, aT)
                    phase_ffn_down(nc, io, S, aT)
                else:
                    phase_route(nc, io, S, hT, R)
        phase_experts(nc, io, S, R)
        phase_final(nc, io, S, R)


def kernel(**inputs):
    import concourse.bacc as bacc
    from concourse.bass_utils import run_bass_kernel_spmd

    nc = bacc.Bacc("TRN2", target_bir_lowering=False, num_devices=1)
    shapes = {"cst": constants(), "dft_seq": dft(SEQ), "dft_ctx": dft(CTX)}
    arrays, io = {}, {}
    for name in INPUTS:
        a = shapes[name] if name in shapes else np.ascontiguousarray(inputs[name])
        arrays["in_" + name] = a
        io[name] = nc.dram_tensor("in_" + name, a.shape, mybir.dt.from_np(a.dtype), kind="ExternalInput").ap()
    io["out"] = nc.dram_tensor("out", (1, SEQ, D), F32, kind="ExternalOutput").ap()
    build(nc, io)
    r = run_bass_kernel_spmd(nc, [arrays], core_ids=[0])
    return r.results[0]["out"]
```

```python
from contextlib import ExitStack

import concourse.bass as bass
import numpy as np
from concourse import mybir

F32 = mybir.dt.float32
F32R = mybir.dt.float32r
I32 = mybir.dt.int32
U32 = mybir.dt.uint32
ACT = mybir.ActivationFunctionType
ALU = mybir.AluOpType
AX = mybir.AxisListType

P = 128
D = 1024
KD = D // P
CTX, SEQ = 256, 1024
T = CTX + SEQ
NT = T // P
NCT = CTX // P
GRID_W = 64
ROWS = SEQ // GRID_W
GROUPS = [(0, CTX), (CTX, 512), (CTX + 512, 512)]
NH, HD = 4, 64
GW = NH * HD
DFF = 2816
DFE = 3584
NE = 8
EPS = 1e-6
BIG = 1e30
UNIT = 2 * P
NUNIT = (2 * SEQ + NE * (UNIT - 1)) // UNIT

CST = {}


def _layout():
    at = 0
    for name, n in [("ident", P), ("ones", P), ("negF", 4 * P), ("negB", 4 * P), ("keepF", P), ("keepB", P),
                    ("sel8", 8 * P), ("selpair", 4 * P), ("blockg", 2 * P), ("blockm", 130), ("tri", P),
                    ("pref", NE), ("koff", NE), ("blk", NUNIT), ("half", NUNIT), ("one", 1), ("eps", 1), ("chan", 2 * P), ("row4", 4), ("row2", 2)]:
        CST[name] = (at, n)
        at += n
    return at


NCST = _layout()


def constants():
    c = np.zeros((P, NCST), np.float32)

    def put(name, a):
        o, n = CST[name]
        c[:a.shape[0], o:o + n] = a.reshape(a.shape[0], n)

    s, l = np.arange(P)[:, None], np.arange(P)[None, :]
    put("ident", np.eye(P))
    put("ones", np.ones((P, P)))
    put("negF", np.tile(np.where(s > l, BIG, 0.0), (1, 4)))
    put("negB", np.tile(np.where(s < l, BIG, 0.0), (1, 4)))
    put("keepF", (s <= l) * 1.0)
    put("keepB", (s >= l) * 1.0)
    sel = np.zeros((8, 8, P))
    for r in range(8):
        sel[r, r] = 1
    put("sel8", sel)
    selp = np.zeros((8, 4, P))
    for j in range(4):
        for p in range(P):
            selp[4 * (j // 2) + 2 * (j % 2) + p // HD, j, p] = 1
    put("selpair", selp)
    put("blockg", (np.arange(P)[:, None] // 32 == np.arange(2 * P)[None, :] // HD) * 1.0)
    put("blockm", (np.arange(P)[:, None] // HD == np.arange(130)[None, :] // 65) * 1.0)
    put("tri", (s < l) * 1.0)
    put("pref", np.tile(np.arange(NE, 0, -1.0), (P, 1)))
    put("koff", np.tile(UNIT * np.arange(NE * 1.0), (P, 1)))
    put("blk", np.tile(np.arange(NUNIT * 1.0), (P, 1)))
    put("half", np.tile(UNIT * np.arange(NUNIT * 1.0) + P, (P, 1)))
    put("row4", (np.arange(P)[:, None] // 32 == np.arange(4)[None, :]) * 1.0)
    put("row2", (np.arange(P)[:, None] // HD == np.arange(2)[None, :]) * 1.0)
    put("one", np.ones((P, 1)))
    put("eps", np.full((P, 1), EPS))
    ang = 2 * np.pi * (np.outer(np.arange(HD), np.arange(HD)) % HD) / HD
    ch = np.zeros((P, 2, P))
    for h in range(2):
        i = slice(h * HD, (h + 1) * HD)
        ch[i, 0, i] = np.cos(ang)
        ch[i, 1, i] = -np.sin(ang)
    put("chan", ch)
    return c


def dft(n):
    ang = 2 * np.pi * (np.outer(np.arange(n), np.arange(n)) % n) / n
    m = np.stack([np.cos(ang), np.sin(ang)], 1) / np.sqrt(n * HD)
    return np.ascontiguousarray(m.reshape(n // P, P, 2, n).transpose(1, 0, 2, 3)).astype(np.float32)


class Phase:

    def __init__(self, nc, name):
        self.nc, self.name, self.sems = nc, name, []

    def __enter__(self):
        self.stack = ExitStack()
        return self

    def sb(self, name, shape, dt=F32):
        return self.stack.enter_context(self.nc.sbuf_tensor(f"{self.name}_{name}", shape, dt))

    def sem(self, name):
        s = self.stack.enter_context(self.nc.semaphore(f"{self.name}_{name}"))
        self.sems.append(s)
        return s

    def __exit__(self, kind, value, trace):
        if kind is None:
            for s in self.sems:
                self.nc.gpsimd.sem_clear(s)
            self.nc.all_engine_barrier()
        self.stack.close()
        return False


class Chain:

    def __init__(self, eng, sem):
        self.eng, self.sem, self.n = eng, sem, 0

    def __call__(self, ins):
        self.n += 1
        ins.then_inc(self.sem, 1)
        self.eng.wait_ge(self.sem, self.n)


def cols(ap1d):
    return ap1d.rearrange("(k p) -> p k", p=P)


def bc(ap, n):
    return ap.unsqueeze(2).to_broadcast([ap.shape[0], ap.shape[1], n])


def phase_modulation(nc, io, S):
    with Phase(nc, "ada") as ph:
        wring = ph.sb("w", [P, 6, KD, 512])
        cond = ph.sb("cond", [P, 2, KD])
        act = ph.sb("act", [P, KD, 2])
        bias = ph.sb("bias", [P, 2, 48])
        ng = ph.sb("ng", [P, 2, 2, KD])
        small = ph.sem("small_loaded")
        wl = [ph.sem(f"w_loaded{s}") for s in range(6)]
        silu_ready, mm_done, evac, mod_done = (ph.sem(n) for n in ("silu_ready", "mm_done", "evacuated", "mod_done"))
        wfree = ph.sem("w_slot_free")
        mod, gmod, ps = S["mod"], S["gmod"], S["ps"]
        with nc.Block() as block:

            @block.sync
            def _(sp):
                with nc.allow_non_contiguous_dma(reason="vectors as columns"):
                    sp.dma_start(S["cst"][:, :], io["cst"]).then_inc(small, 16)
                    sp.dma_start(cond[:, 0, :], cols(io["c"].rearrange("a d -> (a d)"))).then_inc(small, 16)
                    sp.dma_start(cond[:, 1, :], cols(io["c_ctx"])).then_inc(small, 16)
                    for l in range(2):
                        sp.dma_start(bias[:, l, :], cols(io["b_ada"][l])).then_inc(small, 16)
                        sp.dma_start(ng[:, l, 0, :], cols(io["norm_mix_g"][l])).then_inc(small, 16)
                        sp.dma_start(ng[:, l, 1, :], cols(io["norm_ffn_g"][l])).then_inc(small, 16)
                for l in range(2):
                    w = io["w_ada"][l].rearrange("(k p) n -> p k n", p=P)
                    with sp.Fori(0, 2) as i:
                        for s in range(6):
                            sp.wait_ge(wfree, i * 6 + (12 * l + s + 1))
                            sp.dma_start(wring[:, s, :, :], w[:, :, bass.ds(i * 3072 + 512 * s, 512)]).then_inc(wl[s], 16)

            @block.scalar
            def _(act_e):
                act_e.wait_ge(small, 16 * 9)
                for j in range(2):
                    a = nc.scalar.activation(act[:, :, j], cond[:, j, :], ACT.Silu)
                a.then_inc(silu_ready, 1)

            @block.tensor
            def _(pe):
                pe.sem_inc(wfree, 6)
                pe.wait_ge(silu_ready, 1)
                for l in range(2):
                    with pe.Fori(0, 2) as i:
                        for s in range(6):
                            pe.wait_ge(wl[s], i * 16 + 16 * (2 * l + 1))
                            pe.wait_ge(evac, i * 6 + (12 * l + s + 1))
                            for m in range(4):
                                for k in range(KD):
                                    mm = nc.tensor.matmul(ps[:, s % 2, 2 * m:2 * m + 2], wring[:, s, k, m * P:(m + 1) * P],
                                                          act[:, k, :], start=(k == 0), stop=(k == KD - 1))
                            mm.then_inc(mm_done, 1)
                            pe.wait_ge(mm_done, i * 6 + (12 * l + s + 1))
                            pe.sem_inc(wfree, 1)

            @block.vector
            def _(dve):
                dve.sem_inc(evac, 2)
                dve.wait_ge(small, 16 * 9)
                for l in range(2):
                    with dve.Fori(0, 2) as i:
                        for s in range(6):
                            dve.wait_ge(mm_done, i * 6 + (12 * l + s + 1))
                            nc.vector.tensor_tensor(
                                mod[:, l, bass.ds(i * 24 + 4 * s, 4), :], ps[:, s % 2, 0:8].rearrange("p (m j) -> p m j", j=2),
                                bc(bias[:, l, bass.ds(i * 24 + 4 * s, 4)], 2), ALU.add).then_inc(evac, 1)
                dve.wait_ge(evac, 26)
                for l in range(2):
                    for w in range(2):
                        for j in range(2):
                            a = nc.vector.scalar_tensor_tensor(
                                out=gmod[:, l, w, j, :], in0=mod[:, l, 24 * w + 8:24 * w + 16, j], scalar=1.0,
                                in1=ng[:, l, w, :], op0=ALU.add, op1=ALU.mult)
                a.then_inc(mod_done, 1)
                dve.wait_ge(mod_done, 1)


def phase_to_features(nc, io, S):
    with Phase(nc, "x0") as ph:
        rows = ph.sb("rows", [P, 2, D])
        turned = ph.sb("turned", [P, 2, KD, P])
        loaded = [ph.sem(f"loaded{s}") for s in range(2)]
        stored = [ph.sem(f"stored{s}") for s in range(2)]
        tr, ev = ph.sem("transposed"), ph.sem("evacuated")
        ps, ident = S["ps"], S["c"]("ident")
        with nc.Block() as block:

            @block.sync
            def _(sp):
                for n in range(NT):
                    src = io["ctx"][0, n * P:(n + 1) * P, :] if n < NCT else io["x"][0, (n - NCT) * P:(n - NCT + 1) * P, :]
                    if n >= 2:
                        sp.wait_ge(tr, n - 1)
                    sp.dma_start(rows[:, n % 2, :], src).then_inc(loaded[n % 2], 16)

            @block.tensor
            def _(pe):
                for n in range(NT):
                    pe.wait_ge(loaded[n % 2], 16 * (n // 2 + 1))
                    if n >= 2:
                        pe.wait_ge(ev, n - 1)
                    for k in range(KD):
                        b = 2 * (n % 2) + k // 4
                        t = nc.tensor.transpose(ps[:, b, (k % 4) * P:(k % 4 + 1) * P], rows[:, n % 2, k * P:(k + 1) * P], ident)
                    t.then_inc(tr, 1)

            @block.vector
            def _(dve):
                for n in range(NT):
                    dve.wait_ge(tr, n + 1)
                    if n >= 2:
                        dve.wait_ge(stored[n % 2], 16 * (n // 2))
                    nc.vector.tensor_copy(turned[:, n % 2, :, :], ps[:, 2 * (n % 2):2 * (n % 2) + 2, :].rearrange(
                        "p b (k t) -> p (b k) t", t=P)).then_inc(ev, 1)

            @block.scalar
            def _(act):
                for n in range(NT):
                    act.wait_ge(ev, n + 1)
                    act.dma_start(S["xT_d"][:, :, n * P:(n + 1) * P], turned[:, n % 2, :, :]).then_inc(stored[n % 2], 16)
                for s in range(2):
                    act.wait_ge(stored[s], 16 * (NT // 2))


def phase_norm(nc, S, name, xT, hT, l, which, groups):
    with Phase(nc, name) as ph:
        sq = ph.sb("sq", [P, 4, 512])
        rstd = ph.sb("rstd", [P, 2, 512])
        xl, sq_ready, sq_used, ss_ready, var_ready, sd_ready, scaled, shifted, rst = (
            ph.sem(n) for n in ("x_loaded", "sq_ready", "sq_used", "ss_ready", "var_ready", "sd_ready", "scaled", "shifted", "rstd_ready"))
        ps, ones = S["ps"], S["c"]("ones")
        gmod, mod = S["gmod"], S["mod"]
        first = groups[0][0]
        with nc.Block() as block:

            @block.sync
            def _(sp):
                for t0, n in groups:
                    sp.dma_start(xT[:, :, t0:t0 + n], S["xT_d"][:, :, t0:t0 + n]).then_inc(xl, 16)

            @block.scalar
            def _(act):
                act.wait_ge(xl, 16 * len(groups))

                def squares(g, t0, n):
                    for k in range(KD):
                        q = g * KD + k
                        if q >= 4:
                            act.wait_ge(sq_used, q - 3)
                        nc.scalar.activation(sq[:, q % 4, :n], xT[:, k, t0:t0 + n], ACT.Square).then_inc(sq_ready, 1)

                def root(g, t0, n):
                    act.wait_ge(var_ready, g + 1)
                    nc.scalar.activation(rstd[:, g % 2, :n], rstd[:, g % 2, :n], ACT.Sqrt).then_inc(sd_ready, 1)

                for g, (t0, n) in enumerate(groups):
                    squares(g, t0, n)
                    root(g, t0, n)

            @block.tensor
            def _(pe):
                for g, (t0, n) in enumerate(groups):
                    for k in range(KD):
                        q = g * KD + k
                        pe.wait_ge(sq_ready, q + 1)
                        mm = nc.tensor.matmul(ps[:, g, :n], ones, sq[:, q % 4, :n], start=(k == 0), stop=(k == KD - 1))
                        mm.then_inc(sq_used, 1)

            @block.vector
            def _(dve):
                for g, (t0, n) in enumerate(groups):
                    dve.wait_ge(sq_used, (g + 1) * KD)
                    if g >= 2:
                        dve.wait_ge(scaled, KD * (g - 1))
                    nc.vector.tensor_scalar(rstd[:, g % 2, :n], ps[:, g, :n], 1.0 / D, EPS, ALU.mult, ALU.add).then_inc(var_ready, 1)
                    dve.wait_ge(sd_ready, g + 1)
                    nc.vector.reciprocal(rstd[:, g % 2, :n], rstd[:, g % 2, :n]).then_inc(rst, 1)
                    dve.wait_ge(rst, g + 1)
                    j = 1 if t0 < CTX else 0
                    for k in range(KD):
                        nc.vector.scalar_tensor_tensor(
                            out=hT[:, k, t0:t0 + n], in0=xT[:, k, t0:t0 + n], scalar=gmod[:, l, which, j, k:k + 1],
                            in1=rstd[:, g % 2, :n], op0=ALU.mult, op1=ALU.mult).then_inc(scaled, 1)

            @block.gpsimd
            def _(pool):
                for g, (t0, n) in enumerate(groups):
                    j = 1 if t0 < CTX else 0
                    for k in range(KD):
                        pool.wait_ge(scaled, g * KD + k + 1)
                        nc.gpsimd.tensor_scalar(hT[:, k, t0:t0 + n], hT[:, k, t0:t0 + n],
                                                mod[:, l, 24 * which + k, j:j + 1], None, ALU.add).then_inc(shifted, 1)
                pool.wait_ge(shifted, KD * len(groups))


def phase_project(nc, io, S, l, hT, FM, TM, ctx_out):
    loads = [((0, 256), [0, 1]), ((800, 512), [2, 3, 4, 5]), ((2352, 256), [6, 7]), (None, [8])]
    tok = [(256, 0), (1312, 512), (1840, 1024)]
    w_in = io["w_in"][l].rearrange("(k p) n -> p k n", p=P)
    units = []
    for i, (_, chunks) in enumerate(loads):
        for j, ch in enumerate(chunks):
            for t0, n in GROUPS:
                if ch in (6, 7) and not ctx_out and t0 < CTX:
                    continue
                units.append((i, "fm", j, ch, t0, n))
    for i, (_, dst) in enumerate(tok):
        for n in range(NT):
            if dst == 1024 and not ctx_out and n < NCT:
                continue
            units.append((len(loads) + i, "tm", 0, dst, n, 0))
    last_of = {}
    for u, un in enumerate(units):
        last_of[un[0]] = u
    NB = 8
    with Phase(nc, f"proj{l}") as ph:
        wring = ph.sb("w", [P, 2, KD, 512])
        wl = [ph.sem(f"w_loaded{s}") for s in range(2)]
        mm_done, ev = ph.sem("mm_done"), [ph.sem("evacuated_act"), ph.sem("evacuated_dve")]
        zeroed = ph.sem("gate_slot_zeroed")
        ps = S["ps"]
        nl = len(loads) + len(tok)
        cnt = {}
        need = []
        for i in range(nl):
            s = i % 2
            cnt[s] = cnt.setdefault(s, 0) + (5 if i == 3 else 1)
            need.append(16 * cnt[s])

        with nc.Block() as block:

            @block.sync
            def _(sp):
                for i in range(nl):
                    s = i % 2
                    if i >= 2:
                        sp.wait_ge(mm_done, last_of[i - 2] + 1)
                    if i == 3:
                        sp.wait_ge(zeroed, 1)
                        with nc.allow_non_contiguous_dma(reason="gate columns"):
                            for dst, src, n in ((0, 1824, 4), (4, 1832, 4), (32, 1828, 4), (36, 1836, 4), (64, 768, 32)):
                                sp.dma_start(wring[:, s, :, dst:dst + n], w_in[:, :, src:src + n]).then_inc(wl[s], 16)
                    else:
                        c0, n = loads[i][0] if i < len(loads) else (tok[i - len(loads)][0], 512)
                        sp.dma_start(wring[:, s, :, 0:n], w_in[:, :, c0:c0 + n]).then_inc(wl[s], 16)

            @block.gpsimd
            def _(pool):
                pool.wait_ge(mm_done, last_of[1] + 1)
                nc.gpsimd.memset(wring[:, 1, :, 0:P], 0.0).then_inc(zeroed, 1)

            @block.tensor
            def _(pe):
                seen = -1
                for u, (i, kind, j, dst, a, n) in enumerate(units):
                    if i != seen:
                        pe.wait_ge(wl[i % 2], need[i])
                        seen = i
                    if u >= NB:
                        v = u - NB
                        pe.wait_ge(ev[v % 2], v // 2 + 1)
                    for k in range(KD):
                        if kind == "fm":
                            mm = nc.tensor.matmul(ps[:, u % NB, :n], wring[:, i % 2, k, j * P:(j + 1) * P], hT[:, k, a:a + n],
                                                  start=(k == 0), stop=(k == KD - 1))
                        else:
                            mm = nc.tensor.matmul(ps[:, u % NB, :], hT[:, k, a * P:(a + 1) * P], wring[:, i % 2, k, :],
                                                  start=(k == 0), stop=(k == KD - 1))
                    mm.then_inc(mm_done, 1)

            def evacuate(eng, copy, par):
                for u, (i, kind, j, dst, a, n) in enumerate(units):
                    if u % 2 != par:
                        continue
                    eng.wait_ge(mm_done, u + 1)
                    out = FM[:, dst, a:a + n] if kind == "fm" else TM[:, a, dst:dst + 512]
                    src = ps[:, u % NB, :n] if kind == "fm" else ps[:, u % NB, :]
                    copy(out, src).then_inc(ev[par], 1)
                eng.wait_ge(ev[par], (len(units) + 1 - par) // 2)

            @block.scalar
            def _(act):
                evacuate(act, nc.scalar.copy, 0)

            @block.vector
            def _(dve):
                evacuate(dve, nc.vector.tensor_copy, 1)


def phase_fourier(nc, io, S, l, FM, ctx_out):
    tiles = list(range(0 if ctx_out else NCT, NT))
    with Phase(nc, f"four{l}") as ph:
        Y = ph.sb("y", [P, NT, 512])
        dring = ph.sb("dft", [P, 3, 2, SEQ])
        dctx = ph.sb("dftc", [P, NCT, 2, CTX])
        Z = ph.sb("z", [P, 2, T])
        dl = [ph.sem(f"dft_loaded{s}") for s in range(3)]
        cl, ymm, yev, dused, zdone, cdone, zev, st = (
            ph.sem(n) for n in ("ctx_dft_loaded", "y_done", "y_ready", "dft_used", "z_done", "ctx_z_done", "z_ready", "stored"))
        ps, chan = S["ps"], S["c"]("chan")
        with nc.Block() as block:

            @block.sync
            def _(sp):
                if ctx_out:
                    sp.dma_start(dctx[:, :, :, :], io["dft_ctx"]).then_inc(cl, 16)
                for i in range(SEQ // P):
                    if i >= 3:
                        sp.wait_ge(dused, i - 2)
                    sp.dma_start(dring[:, i % 3, :, :], io["dft_seq"][:, i, :, :]).then_inc(dl[i % 3], 16)
                sp.wait_ge(zev, 5 if ctx_out else 4)
                a = 0 if ctx_out else CTX
                sp.dma_start(S["mixT_d"][:, 6:8, a:], Z[:, :, a:]).then_inc(st, 16)
                sp.wait_ge(st, 16)

            @block.tensor
            def _(pe):
                for i, n in enumerate(tiles):
                    if i >= 2:
                        pe.wait_ge(yev, i - 1)
                    for c in range(2):
                        mm = nc.tensor.matmul(ps[:, i % 2, c * 256:(c + 1) * 256], FM[:, 6 + c, n * P:(n + 1) * P], chan,
                                              start=True, stop=True)
                    mm.then_inc(ymm, 1)
                pe.wait_ge(yev, len(tiles))
                for i in range(SEQ // P):
                    pe.wait_ge(dl[i % 3], 16 * (i // 3 + 1))
                    for c in range(2):
                        for trig in range(2):
                            for half in range(2):
                                mm = nc.tensor.matmul(
                                    ps[:, 2 + 2 * c + half, :], Y[:, NCT + i, c * 256 + trig * P:c * 256 + (trig + 1) * P],
                                    dring[:, i % 3, trig, half * 512:(half + 1) * 512],
                                    start=(i == 0 and trig == 0), stop=(i == SEQ // P - 1 and trig == 1))
                    mm.then_inc(dused, 1)
                if ctx_out:
                    pe.wait_ge(cl, 16)
                    for c in range(2):
                        for i in range(NCT):
                            for trig in range(2):
                                mm = nc.tensor.matmul(
                                    ps[:, 6 + c, :CTX], Y[:, i, c * 256 + trig * P:c * 256 + (trig + 1) * P],
                                    dctx[:, i, trig, :], start=(i == 0 and trig == 0), stop=(i == NCT - 1 and trig == 1))
                    mm.then_inc(cdone, 1)

            @block.vector
            def _(dve):
                for i, n in enumerate(tiles):
                    dve.wait_ge(ymm, i + 1)
                    nc.vector.tensor_copy(Y[:, n, :], ps[:, i % 2, :]).then_inc(yev, 1)
                dve.wait_ge(dused, SEQ // P)
                for c in range(2):
                    for half in range(2):
                        nc.vector.tensor_copy(Z[:, c, CTX + half * 512:CTX + (half + 1) * 512],
                                              ps[:, 2 + 2 * c + half, :]).then_inc(zev, 1)
                if ctx_out:
                    dve.wait_ge(cdone, 1)
                    nc.vector.tensor_copy(Z[:, :, 0:CTX], ps[:, 6:8, :CTX]).then_inc(zev, 1)


def phase_sgu(nc, io, S, l, TM, ctx_out):
    tiles = list(range(0 if ctx_out else NCT, NT))
    with Phase(nc, f"sgu{l}") as ph:
        ws = ph.sb("ws", [P, NH, P])
        wsT = ph.sb("wsT", [P, NH, P])
        bs = ph.sb("bs", [P, NH])
        stats = ph.sb("stats", [P, NT, 6])
        mv = ph.sb("mv", [P, NT, 2])
        rstd = ph.sb("rstd", [P, NT])
        ld, tr, wev, chain, var, sd, vn, mm_done, done = (
            ph.sem(n) for n in ("loaded", "transposed", "wT_ready", "dve_step", "var_ready", "sd_ready", "vn_ready", "mixed", "gated"))
        ps, ident = S["ps"], S["c"]("ident")
        t0 = tiles[0]
        with nc.Block() as block:

            @block.sync
            def _(sp):
                sp.dma_start(ws[:, :, :], io["sgu_w"][l].rearrange("g a b -> a g b")).then_inc(ld, 16)
                with nc.allow_non_contiguous_dma(reason="bias columns"):
                    sp.dma_start(bs[:, :], io["sgu_b"][l].rearrange("g a -> a g")).then_inc(ld, 16)

            @block.tensor
            def _(pe):
                pe.wait_ge(ld, 32)
                for g in range(NH):
                    t = nc.tensor.transpose(ps[:, 7, g * P:(g + 1) * P], ws[:, g, :], ident)
                t.then_inc(tr, 1)
                pe.wait_ge(wev, 1)
                pe.wait_ge(vn, len(tiles))
                for g in range(NH):
                    v0 = 1280 + g * HD
                    nc.tensor.matmul(ps[:, g, :].rearrange("p (n c) -> p n c", c=HD), wsT[:, g, :], TM[:, NCT:NT, v0:v0 + HD],
                                     start=True, stop=True).then_inc(mm_done, 1)
                if ctx_out:
                    for g in range(NH):
                        v0 = 1280 + g * HD
                        nc.tensor.matmul(ps[:, 4, g * P:(g + 1) * P].rearrange("p (n c) -> p n c", c=HD), wsT[:, g, :],
                                         TM[:, 0:NCT, v0:v0 + HD], start=True, stop=True).then_inc(mm_done, 1)

            @block.scalar
            def _(act):
                act.wait_ge(tr, 1)
                nc.scalar.copy(wsT[:, :, :], ps[:, 7, :].rearrange("p (g t) -> p g t", t=P)).then_inc(wev, 1)
                act.wait_ge(var, 1)
                nc.scalar.activation(rstd[:, t0:], rstd[:, t0:], ACT.Sqrt).then_inc(sd, 1)

            @block.vector
            def _(dve):
                step = Chain(dve, chain)
                for n in tiles:
                    st = nc.vector.bn_stats(stats[:, n, :], TM[:, n, 1280:1536])
                step(st)
                for n in tiles:
                    st = nc.vector.bn_aggr(mv[:, n, :], stats[:, n, :])
                step(st)
                nc.vector.tensor_scalar(rstd[:, t0:], mv[:, t0:, 1], EPS, None, ALU.add).then_inc(var, 1)
                dve.wait_ge(sd, 1)
                step(nc.vector.reciprocal(rstd[:, t0:], rstd[:, t0:]))
                for n in tiles:
                    nc.vector.tensor_scalar(TM[:, n, 1280:1536], TM[:, n, 1280:1536], mv[:, n, 0:1], rstd[:, n:n + 1],
                                            ALU.subtract, ALU.mult).then_inc(vn, 1)
                dve.wait_ge(ld, 32)
                for g in range(NH):
                    dve.wait_ge(mm_done, g + 1)
                    u = TM[:, NCT:NT, 1024 + g * HD:1024 + (g + 1) * HD]
                    nc.vector.scalar_tensor_tensor(out=u, in0=ps[:, g, :].rearrange("p (n c) -> p n c", c=HD),
                                                   scalar=bs[:, g:g + 1], in1=u, op0=ALU.add, op1=ALU.mult).then_inc(done, 1)
                if ctx_out:
                    for g in range(NH):
                        dve.wait_ge(mm_done, 2 * NH)
                        u = TM[:, 0:NCT, 1024 + g * HD:1024 + (g + 1) * HD]
                        nc.vector.scalar_tensor_tensor(out=u, in0=ps[:, 4, g * P:(g + 1) * P].rearrange("p (n c) -> p n c", c=HD),
                                                       scalar=bs[:, g:g + 1], in1=u, op0=ALU.add, op1=ALU.mult).then_inc(done, 1)
                dve.wait_ge(done, 8 if ctx_out else 4)


def order(direction, j):
    if direction == 0:
        return j
    return NCT - 1 - j if j < NCT else NT - 1 - (j - NCT)


def phase_decays(nc, io, S, l, FM, M):
    with Phase(nc, f"dec{l}") as ph:
        wlr = ph.sb("wlr", [P, 2, P])
        blr = ph.sb("blr", [P, 2])
        gb = ph.sb("gb", [P, 1])
        z = ph.sb("z", [P, 2, T])
        e = FM[:, 6:8, :]
        lf = ph.sb("lf", [8, T])
        le = ph.sb("le", [8, T])
        cum8 = ph.sb("cum8", [8, 2, T])
        ones8 = ph.sb("ones8", [8, T])
        stack = ph.sb("stack", [P, T])
        mprev = ph.sb("mprev", [8, 2, NT])
        mlast = ph.sb("mlast", [8, 2, NT])
        dec = ph.sb("dec", [8, 2, NT])
        ld, zer, zmm, ch_d, ch_a, d2a, a2d, st_ready, trd, tev, dmm = (
            ph.sem(n) for n in ("loaded", "zeroed", "z_done", "dve_step", "act_step", "dve_to_act", "act_to_dve", "stack_ready",
                                "stack_transposed", "stack_read", "decay_rows_done"))
        ps, c = S["ps"], S["c"]
        mx, tg, dcol, qd, kd, em = M["mx"], M["tg"], M["dcol"], M["qd"], M["kd"], M["em"]

        def tiles(ap):
            return ap.rearrange("p (n t) -> p n t", t=P)

        with nc.Block() as block:

            @block.sync
            def _(sp):
                sp.wait_ge(zer, 1)
                with nc.allow_non_contiguous_dma(reason="vectors as columns"):
                    for d in range(2):
                        sp.dma_start(wlr[64 + 16 * d:80 + 16 * d, d, :], io["gla_w_lr"][l, d]).then_inc(ld, 16)
                        sp.dma_start(blr[:, d:d + 1], io["gla_b_lr"][l, d].rearrange("(p a) -> p a", a=1)).then_inc(ld, 16)
                        for kind in range(2):
                            sp.dma_start(gb[32 * kind + 4 * d:32 * kind + 4 * d + 4, :],
                                         io["mlstm_gate_b"][l, d, kind].rearrange("(p a) -> p a", a=1)).then_inc(ld, 16)

            @block.gpsimd
            def _(pool):
                nc.gpsimd.memset(wlr[:, :, :], 0.0)
                nc.gpsimd.memset(gb[:, :], 0.0)
                nc.gpsimd.memset(ones8[:, :], 1.0)
                nc.gpsimd.memset(stack[:, :], 0.0).then_inc(zer, 1)

            @block.tensor
            def _(pe):
                pe.wait_ge(ld, 16 * 8)
                for d in range(2):
                    for g, (t0, n) in enumerate(GROUPS):
                        mm = nc.tensor.matmul(ps[:, 3 * d + g, :n], wlr[64:96, d, :], FM[64:96, 8, t0:t0 + n], start=True, stop=True)
                mm.then_inc(zmm, 1)
                for d in range(2):
                    pe.wait_ge(st_ready, d + 1)
                    for n in range(NT):
                        q = d * NT + n
                        if q >= 2:
                            pe.wait_ge(tev, q - 1)
                        nc.tensor.transpose(ps[:, 6 + q % 2, 0:P], stack[:, n * P:(n + 1) * P], c("ident")).then_inc(trd, 1)
                pe.wait_ge(a2d, 6)
                selp = c("selpair").rearrange("p (a t) -> p a t", t=P)
                for j in range(4):
                    mm = nc.tensor.matmul(ps[:, 0, j * NT:(j + 1) * NT], selp[0:8, j, :], dec[:, j // 2, :], start=True, stop=True)
                mm.then_inc(dmm, 1)

            @block.scalar
            def _(act):
                step = Chain(act, ch_a)
                act.wait_ge(d2a, 1)
                step(nc.scalar.activation(e[:, :, :], e[:, :, :], ACT.Exp, scale=-1.0))
                nc.scalar.activation(e[:, :, :], e[:, :, :], ACT.Ln, bias=c("one")).then_inc(a2d, 1)
                act.wait_ge(d2a, 2)
                step(nc.scalar.activation(le[:, :], le[:, :], ACT.Exp, scale=-1.0))
                nc.scalar.activation(le[:, :], le[:, :], ACT.Ln, bias=c("one")[0:8, :]).then_inc(a2d, 1)
                act.wait_ge(d2a, 3)
                nc.scalar.activation(em[:, :, :, :], em[:, :, :, :], ACT.Exp, scale=1.0 / 16).then_inc(a2d, 1)
                for d in range(2):
                    act.wait_ge(d2a, 4 + d)
                    nc.scalar.activation(e[:, 0, :], z[:, d, :], ACT.Exp, scale=1.0 / 16)
                    nc.scalar.activation(e[:, 1, :], z[:, d, :], ACT.Exp, scale=-1.0 / 16).then_inc(a2d, 1)
                for d in range(2):
                    act.wait_ge(d2a, 6 + d)
                    nc.scalar.activation(stack[32:40, :], stack[32:40, :], ACT.Exp)
                    nc.scalar.activation(stack[64:72, :], stack[64:72, :], ACT.Exp, scale=-1.0)
                    nc.scalar.activation(stack[96:104, :], stack[96:104, :], ACT.Exp).then_inc(st_ready, 1)
                nc.scalar.activation(dec[:, :, :], dec[:, :, :], ACT.Exp).then_inc(a2d, 1)

            @block.vector
            def _(dve):
                step = Chain(dve, ch_d)
                dve.wait_ge(ld, 16 * 8)
                dve.wait_ge(zmm, 1)
                for d in range(2):
                    for g, (t0, n) in enumerate(GROUPS):
                        x = nc.vector.tensor_scalar(z[:, d, t0:t0 + n], ps[:, 3 * d + g, :n], blr[:, d:d + 1], None, ALU.add)
                step(x)
                nc.vector.scalar_tensor_tensor(out=e[:, :, :], in0=z[:, :, :], scalar=-1.0, in1=z[:, :, :], op0=ALU.mult, op1=ALU.max).then_inc(d2a, 1)
                nc.vector.tensor_scalar(M["ig"][:, :], FM[0:8, 8, :], gb[0:8, :], None, ALU.add)
                step(nc.vector.tensor_scalar(lf[:, :], FM[32:40, 8, :], gb[32:40, :], None, ALU.add))
                nc.vector.scalar_tensor_tensor(out=le[:, :], in0=lf[:, :], scalar=-1.0, in1=lf[:, :], op0=ALU.mult, op1=ALU.max).then_inc(d2a, 1)
                dve.wait_ge(a2d, 1)
                step(nc.vector.scalar_tensor_tensor(out=z[:, :, :], in0=z[:, :, :], scalar=0.0, in1=e[:, :, :], op0=ALU.min, op1=ALU.subtract))
                for n in range(NT):
                    t = slice(n * P, (n + 1) * P)
                    nc.vector.tensor_tensor_scan(e[:, 0, t], c("ones"), z[:, 0, t], 0.0, ALU.mult, ALU.add)
                    x = nc.vector.tensor_tensor_scan(e[:, 1, t][:, ::-1], c("ones"), z[:, 1, t][:, ::-1], 0.0, ALU.mult, ALU.add)
                step(x)
                for d, (mid, last) in enumerate(((63, 127), (64, 0))):
                    et = tiles(e[:, d, :])
                    nc.vector.tensor_copy(em[:, d, 0, :], et[:, :, mid])
                    nc.vector.tensor_copy(em[:, d, 1, :], et[:, :, last])
                    x = nc.vector.tensor_tensor(em[:, d, 2, :], et[:, :, last], et[:, :, mid], ALU.subtract)
                step(x)
                for d in range(2):
                    x = nc.vector.tensor_tensor(tiles(z[:, d, :]), tiles(e[:, d, :]), bc(em[:, d, 0, :], P), ALU.subtract)
                step(x)
                dve.sem_inc(d2a, 1)
                dve.sem_inc(d2a, 1)
                for d in range(2):
                    dve.wait_ge(a2d, 4 + d)
                    nc.vector.scalar_tensor_tensor(out=qd[:, d, :], in0=FM[:, 0, :], scalar=32.0 ** -0.5, in1=e[:, 0, :], op0=ALU.mult, op1=ALU.mult)
                    step(nc.vector.tensor_tensor(kd[:, d, :], FM[:, 1, :], e[:, 1, :], ALU.mult))
                    if d == 0:
                        dve.sem_inc(d2a, 1)
                step(nc.vector.scalar_tensor_tensor(out=lf[:, :], in0=lf[:, :], scalar=0.0, in1=le[:, :], op0=ALU.min, op1=ALU.subtract))
                step(nc.vector.tensor_tensor_scan(cum8[:, 0, :], ones8[:, :], lf[:, :], 0.0, ALU.mult, ALU.add))
                back = [(0, CTX), (CTX, T)]
                init = 0.0
                for a, b in back:
                    step(nc.vector.tensor_tensor_scan(cum8[:, 1, a:b][:, ::-1], ones8[:, a:b], lf[:, a:b][:, ::-1], init, ALU.mult, ALU.add))
                    init = cum8[:, 1, a:a + 1]
                for d in range(2):
                    if d == 1:
                        dve.wait_ge(trd, NT)
                    step(nc.vector.tensor_tensor(stack[0:8, :], M["ig"][:, :], cum8[:, d, :], ALU.subtract))
                    if d == 0:
                        step(nc.vector.tensor_tensor_scan(mx[:, 0, :], stack[0:8, :], stack[0:8, :], 0.0, ALU.max, ALU.max))
                    else:
                        init = 0.0
                        for a, b in back:
                            r = stack[0:8, a:b][:, ::-1]
                            step(nc.vector.tensor_tensor_scan(mx[:, 1, a:b][:, ::-1], r, r, init, ALU.max, ALU.max))
                            init = mx[:, 1, a:a + 1]
                    m3 = tiles(mx[:, d, :])
                    step(nc.vector.tensor_copy(mlast[:, d, :], m3[:, :, P - 1 if d == 0 else 0]))
                    first = order(d, 0)
                    nc.vector.memset(mprev[:, d, first:first + 1], 0.0)
                    if d == 0:
                        x = nc.vector.tensor_copy(mprev[:, 0, 1:NT], mlast[:, 0, 0:NT - 1])
                    else:
                        nc.vector.tensor_copy(mprev[:, 1, 0:1], mlast[:, 1, 1:2])
                        nc.vector.tensor_copy(mprev[:, 1, NT - 1:NT], mlast[:, 1, 0:1])
                        x = nc.vector.tensor_copy(mprev[:, 1, NCT:NT - 1], mlast[:, 1, NCT + 1:NT])
                    step(x)
                    nc.vector.tensor_tensor(dec[:, d, :], mprev[:, d, :], mlast[:, d, :], ALU.subtract)
                    nc.vector.tensor_tensor(tiles(stack[32:40, :]), bc(mprev[:, d, :], P), m3, ALU.subtract)
                    nc.vector.tensor_tensor(stack[64:72, :], cum8[:, d, :], mx[:, d, :], ALU.add)
                    step(nc.vector.tensor_tensor(tiles(stack[96:104, :]), tiles(stack[0:8, :]), bc(mlast[:, d, :], P), ALU.subtract))
                    dve.sem_inc(d2a, 1)
                    for n in range(NT):
                        q = d * NT + n
                        dve.wait_ge(trd, q + 1)
                        nc.vector.tensor_copy(tg[:, n, d, :, :], ps[:, 6 + q % 2, 0:P].rearrange("p (a r) -> p a r", r=32)[:, :, 0:8]).then_inc(tev, 1)
                dve.wait_ge(dmm, 1)
                step(nc.vector.tensor_copy(dcol[:, :, :], ps[:, 0, 0:4 * NT].rearrange("p (j n) -> p j n", n=NT)))
                dve.wait_ge(tev, 2 * NT)
                dve.wait_ge(a2d, 6)


def phase_conv(nc, io, S, l, FM, TM, M):
    src, dst = [2, 3, 4, 5], [0, 1, 6, 7]
    with Phase(nc, f"conv{l}") as ph:
        w = ph.sb("w", [P, 4, 9])
        ld, ch, cv, done, vx = (ph.sem(n) for n in ("loaded", "dve_step", "convolved", "silu_done", "v_ready"))
        with nc.Block() as block:

            @block.sync
            def _(sp):
                with nc.allow_non_contiguous_dma(reason="taps as columns"):
                    for j in range(4):
                        sp.dma_start(w[:, j, :], io["mlstm_conv"][l].rearrange("a b d -> (a b) d")[:, j * P:(j + 1) * P]
                                     .rearrange("t p -> p t")).then_inc(ld, 16)

            @block.vector
            def _(dve):
                step = Chain(dve, ch)
                dve.wait_ge(ld, 64)
                for j in range(4):
                    x, y = FM[:, src[j], :], FM[:, dst[j], :]
                    x2, y2 = (a[:, CTX:].rearrange("p (r c) -> p r c", c=GRID_W) for a in (x, y))
                    step(nc.vector.tensor_scalar(y, x, w[:, j, 4:5], None, ALU.mult))
                    for dr in (-1, 0, 1):
                        for dc in (-1, 0, 1):
                            if dr == 0 and dc == 0:
                                continue
                            r0, r1 = max(0, -dr), ROWS - max(0, dr)
                            c0, c1 = max(0, -dc), GRID_W - max(0, dc)
                            o = y2[:, r0:r1, c0:c1]
                            tap = w[:, j, 3 * (dr + 1) + dc + 1:3 * (dr + 1) + dc + 2]
                            step(nc.vector.scalar_tensor_tensor(out=o, in0=x2[:, r0 + dr:r1 + dr, c0 + dc:c1 + dc], scalar=tap,
                                                                in1=o, op0=ALU.mult, op1=ALU.add))
                            if dr == 0:
                                a, b = max(0, -dc), CTX - max(0, dc)
                                step(nc.vector.scalar_tensor_tensor(out=y[:, a:b], in0=x[:, a + dc:b + dc], scalar=tap,
                                                                    in1=y[:, a:b], op0=ALU.mult, op1=ALU.add))
                    dve.sem_inc(cv, 1)
                for j in range(2):
                    dve.wait_ge(done, j + 1)
                    step(nc.vector.tensor_scalar(FM[:, dst[j], :], FM[:, dst[j], :], HD ** -0.5, None, ALU.mult))

            @block.scalar
            def _(act):
                for j in range(4):
                    act.wait_ge(cv, j + 1)
                    nc.scalar.activation(FM[:, dst[j], :], FM[:, dst[j], :], ACT.Silu).then_inc(done, 1)
                act.wait_ge(done, 4)

            @block.gpsimd
            def _(pool):
                for n in range(NT):
                    nc.gpsimd.memset(M["vx"][:, n, :, HD:HD + 1], 1.0)
                    x = nc.gpsimd.tensor_copy(M["vx"][:, n, :, 0:HD], TM[:, n, 512:768].rearrange("p (h c) -> p h c", c=HD))
                x.then_inc(vx, 1)
                pool.wait_ge(vx, 1)


def phase_scan(nc, io, S, l, FM, TM, M):
    U = 2 * NT
    with Phase(nc, f"scan{l}") as ph:
        kdt = ph.sb("kdt", [P, 2, P])
        kw = ph.sb("kw", [P, 2, NH, HD])
        sg = ph.sb("sg", [P, 2, NH, P])
        ex = ph.sb("ex", [P, 2, NH, P])
        tmp = ph.sb("tmp", [P, NH, 65])
        num = ph.sb("num", [P, NH, 65])
        den = ph.sb("den", [P, NH])
        dsg = ph.sb("dsg", [P, 2 * P])
        dsm = ph.sb("dsm", [P, 2, 130])
        Sg = ph.sb("Sg", [P, 2, 2 * P])
        Sp = ph.sb("Sp", [P, 2, 2 * P])
        Sm = ph.sb("Sm", [P, 2, 2, 130])
        pe_tr, pe_mb, pe_sg, pe_sm, pe_og, pe_om, pe_u = (ph.sem(n) for n in (
            "transposed", "max_rows_done", "gla_scores_done", "mlstm_scores_done", "gla_out_done", "mlstm_out_done", "updates_done"))
        a_kdt, a_ex = ph.sem("kdt_ready"), ph.sem("ex_ready")
        g_q = ph.sem("masked_q_ready")
        qg = ph.sb("qg", [P, 2, NH, P])
        qm = ph.sb("qm", [P, 2, NH, P])
        v_init, v_kw, v_sg, v_w, v_og, v_om, v_st, ch = (ph.sem(n) for n in (
            "states_zero", "kw_ready", "gla_weights_ready", "mlstm_weights_ready", "gla_out_read", "mlstm_out_read", "states_ready", "dve_step"))
        ps, c = S["ps"], S["c"]
        mx, tg, dcol, qd, kd, em, vx, og, om = (M[k] for k in ("mx", "tg", "dcol", "qd", "kd", "em", "vx", "og", "om"))
        TR, SG, OG, KT, MB, SM, OI, OC = range(8)
        mq, mk = (0, 1), (6, 7)
        sel8 = c("sel8").rearrange("p (a t) -> p a t", t=P)

        def unit(u):
            d = u % 2
            n = order(d, u // 2)
            return d, n, slice(n * P, (n + 1) * P)

        with nc.Block() as block:

            @block.tensor
            def _(pe):
                for u in range(U):
                    d, n, t = unit(u)
                    if u >= 1:
                        pe.wait_ge(a_kdt, u)
                        pe.wait_ge(v_kw, u)
                    nc.tensor.transpose(ps[:, KT, 0:P], kd[:, d, t], c("ident"))
                    for j in range(2):
                        x = nc.tensor.transpose(ps[:, TR, (j + 1) * P:(j + 2) * P], FM[:, mk[j], t], c("ident"))
                    x.then_inc(pe_tr, 1)
                    if u >= 1:
                        pe.wait_ge(a_ex, u)
                    nc.tensor.matmul(ps[:, MB, :], c("ident"), c("negF" if d == 0 else "negB"), start=True, stop=False, skip_group_check=True)
                    for h in range(NH):
                        x = nc.tensor.matmul(ps[:, MB, h * P:(h + 1) * P], sel8[0:8, 4 * d + h, :], mx[:, d, t],
                                             start=False, stop=(h == NH - 1), skip_group_check=True)
                    x.then_inc(pe_mb, 1)
                    if u >= 1:
                        pe.wait_ge(v_w, u)
                    pe.wait_ge(g_q, u + 1)
                    for j in range(2):
                        x = nc.tensor.matmul(ps[:, SM, j * 256:(j + 1) * 256], FM[:, mk[j], t],
                                             qm[:, d, 2 * j:2 * j + 2, :].rearrange("p a b -> p (a b)"), start=True, stop=True)
                    x.then_inc(pe_sm, 1)
                    if u >= 1:
                        pe.wait_ge(v_st, u)
                    else:
                        pe.wait_ge(v_init, 1)
                    nc.tensor.matmul(ps[:, SG, :], kd[:, d, t], qg[:, d, :, :].rearrange("p a b -> p (a b)"),
                                     start=True, stop=True).then_inc(pe_sg, 1)
                    if u >= 1:
                        pe.wait_ge(v_og, u)
                        pe.wait_ge(v_om, u)
                    nc.tensor.matmul(ps[:, OG, 0:256], qd[:, d, t], Sp[:, d, :], start=True, stop=False, skip_group_check=True)
                    for j in range(2):
                        nc.tensor.matmul(ps[:, OC, j * 130:(j + 1) * 130], FM[:, mq[j], t], Sm[:, d, j, :], start=True, stop=True)
                    pe.wait_ge(v_sg, u + 1)
                    for h in range(NH):
                        x = nc.tensor.matmul(ps[:, OG, h * HD:(h + 1) * HD], sg[:, d, h, :], TM[:, n, h * HD:(h + 1) * HD],
                                             start=False, stop=(h == NH - 1), skip_group_check=True)
                    x.then_inc(pe_og, 1)
                    pe.wait_ge(v_w, u + 1)
                    for h in range(NH):
                        x = nc.tensor.matmul(ps[:, OI, h * 65:(h + 1) * 65], ex[:, d, h, :], vx[:, n, h, :], start=True, stop=True)
                    x.then_inc(pe_om, 1)
                    pe.wait_ge(a_kdt, u + 1)
                    pe.wait_ge(v_og, u + 1)
                    nc.tensor.matmul(ps[:, OG, 256:512], kdt[:, d, :], TM[:, n, 0:256], start=True, stop=True)
                    pe.wait_ge(v_kw, u + 1)
                    for j in range(2):
                        x = nc.tensor.matmul(ps[:, SG, j * 130:(j + 1) * 130], kw[:, d, 2 * j:2 * j + 2, :].rearrange("p a b -> p (a b)"),
                                             vx[:, n, 2 * j:2 * j + 2, :].rearrange("p a b -> p (a b)"), start=True, stop=True)
                    x.then_inc(pe_u, 1)

            @block.scalar
            def _(act):
                for u in range(U):
                    d, n, t = unit(u)
                    if u >= 2:
                        act.wait_ge(pe_u, u - 1)
                    act.wait_ge(pe_tr, u + 1)
                    nc.scalar.copy(kdt[:, d, :], ps[:, KT, 0:P]).then_inc(a_kdt, 1)
                    act.wait_ge(pe_mb, u + 1)
                    for h in range(NH):
                        x = nc.scalar.activation(ex[:, d, h, :], ps[:, MB, h * P:(h + 1) * P], ACT.Exp,
                                                 bias=tg[:, n, d, 0, 4 * d + h:4 * d + h + 1], scale=-1.0)
                    x.then_inc(a_ex, 1)

            @block.gpsimd
            def _(pool):
                for u in range(U):
                    d, n, t = unit(u)
                    if u >= 2:
                        pool.wait_ge(pe_sm, u - 1)
                        pool.wait_ge(pe_sg, u - 1)
                    nc.gpsimd.tensor_tensor(qg[:, d, :, :], qd[:, d, t].unsqueeze(1).to_broadcast([P, NH, P]), bc(c("row4"), P), ALU.mult)
                    for j in range(2):
                        x = nc.gpsimd.tensor_tensor(qm[:, d, 2 * j:2 * j + 2, :], FM[:, mq[j], t].unsqueeze(1).to_broadcast([P, 2, P]),
                                                    bc(c("row2"), P), ALU.mult)
                    x.then_inc(g_q, 1)

            @block.vector
            def _(dve):
                step = Chain(dve, ch)
                nc.vector.memset(sg[:, :, :, :], 0.0)
                nc.vector.memset(Sg[:, :, :], 0.0)
                nc.vector.memset(Sp[:, :, :], 0.0)
                nc.vector.memset(Sm[:, :, :, :], 0.0).then_inc(v_init, 1)
                dve.wait_ge(v_init, 1)
                keep = [c("keepF"), c("keepB")]
                written = set()
                for u in range(U):
                    d, n, t = unit(u)
                    h8 = slice(4 * d, 4 * d + 4)
                    if u >= 2:
                        dve.wait_ge(pe_u, u - 1)
                    dve.wait_ge(pe_tr, u + 1)
                    nc.vector.tensor_tensor(kw[:, d, :, :], ps[:, TR, P:3 * P].rearrange("p (h c) -> p h c", c=HD),
                                            bc(tg[:, n, d, 3, h8], HD), ALU.mult).then_inc(v_kw, 1)
                    dve.wait_ge(pe_sg, u + 1)
                    nc.vector.copy_predicated(sg[:, d, :, :], keep[d].bitcast(I32).unsqueeze(1).to_broadcast([P, NH, P]),
                                              ps[:, SG, :].rearrange("p (h t) -> p h t", t=P)).then_inc(v_sg, 1)
                    dve.wait_ge(a_ex, u + 1)
                    dve.wait_ge(pe_sm, u + 1)
                    nc.vector.tensor_tensor(ex[:, d, :, :], ex[:, d, :, :], ps[:, SM, :].rearrange("p (h t) -> p h t", t=P), ALU.mult).then_inc(v_w, 1)
                    dve.wait_ge(pe_og, u + 1)
                    if n in written:
                        nc.vector.tensor_tensor(og[:, n, :], og[:, n, :], ps[:, OG, 0:256], ALU.add).then_inc(v_og, 1)
                    else:
                        nc.vector.tensor_copy(og[:, n, :], ps[:, OG, 0:256]).then_inc(v_og, 1)
                    dve.wait_ge(pe_om, u + 1)
                    step(nc.vector.tensor_tensor(tmp[:, :, :], ps[:, OC, 0:260].rearrange("p (h c) -> p h c", c=65),
                                                 bc(tg[:, n, d, 1, h8], 65), ALU.mult))
                    nc.vector.tensor_tensor(num[:, :, :], tmp[:, :, :], ps[:, OI, 0:260].rearrange("p (h c) -> p h c", c=65),
                                            ALU.add).then_inc(v_om, 1)
                    dve.wait_ge(v_om, u + 1)
                    step(nc.vector.scalar_tensor_tensor(out=den[:, :], in0=num[:, :, 64], scalar=-1.0, in1=num[:, :, 64],
                                                        op0=ALU.mult, op1=ALU.max))
                    step(nc.vector.tensor_tensor(den[:, :], den[:, :], tg[:, n, d, 2, h8], ALU.max))
                    step(nc.vector.reciprocal(den[:, :], den[:, :]))
                    on = om[:, n, :].rearrange("p (h c) -> p h c", c=HD)
                    if n in written:
                        step(nc.vector.tensor_tensor(tmp[:, :, 0:HD], num[:, :, 0:HD], bc(den[:, :], HD), ALU.mult))
                        nc.vector.tensor_tensor(on, on, tmp[:, :, 0:HD], ALU.add)
                    else:
                        nc.vector.tensor_tensor(on, num[:, :, 0:HD], bc(den[:, :], HD), ALU.mult)
                    written.add(n)
                    dve.wait_ge(pe_u, u + 1)
                    nc.vector.scalar_tensor_tensor(out=dsg[:, :], in0=ps[:, OG, 256:512], scalar=em[:, d, 2, n:n + 1], in1=c("blockg"),
                                                   op0=ALU.mult, op1=ALU.mult)
                    nc.vector.tensor_tensor(dsm[:, :, :], ps[:, SG, 0:260].rearrange("p (a b) -> p a b", b=130),
                                            c("blockm").unsqueeze(1).to_broadcast([P, 2, 130]), ALU.mult)
                    step(nc.vector.tensor_tensor(Sm[:, d, :, :], Sm[:, d, :, :], bc(dcol[:, 2 * d:2 * d + 2, n], 130), ALU.mult))
                    step(nc.vector.scalar_tensor_tensor(out=Sg[:, d, :], in0=Sg[:, d, :], scalar=em[:, d, 1, n:n + 1], in1=dsg[:, :],
                                                        op0=ALU.mult, op1=ALU.add))
                    nc.vector.tensor_tensor(Sm[:, d, :, :], Sm[:, d, :, :], dsm[:, :, :], ALU.add)
                    nn = order(d, min(u // 2 + 1, NT - 1))
                    nc.vector.tensor_scalar(Sp[:, d, :], Sg[:, d, :], em[:, d, 0, nn:nn + 1], None, ALU.mult).then_inc(v_st, 1)
                    dve.wait_ge(v_st, u + 1)


def phase_mix_out(nc, io, S, l, TM, M, ctx_out):
    t0 = 0 if ctx_out else NCT
    tiles = list(range(t0, NT))
    with Phase(nc, f"mix{l}") as ph:
        sq = ph.sb("sq", [P, NT, 256])
        ms = ph.sb("ms", [P, NT, NH])
        ng = ph.sb("ng", [P, 256])
        turned = ph.sb("turned", [P, 2, 6, P])
        ld, ch, var, sd, gates, sqd, gd, gm, tr, ev, st = (ph.sem(n) for n in (
            "loaded", "dve_step", "var_ready", "sd_ready", "gates_ready", "squared", "gla_ready", "mlstm_ready", "transposed", "turned_ready", "stored"))
        ps, ident, og, om = S["ps"], S["c"]("ident"), M["og"], M["om"]
        with nc.Block() as block:

            @block.sync
            def _(sp):
                sp.dma_start(ng[:, :], io["gla_norm_g"][l].rearrange("(a n) -> a n", a=1).to_broadcast([P, 256])).then_inc(ld, 16)
                for i, n in enumerate(tiles):
                    sp.wait_ge(ev, i + 1)
                    sp.dma_start(S["mixT_d"][:, 0:6, n * P:(n + 1) * P], turned[:, i % 2, :, :]).then_inc(st, 16)
                    sp.wait_ge(st, 16 * (i + 1))

            @block.scalar
            def _(act):
                nc.scalar.activation(sq[:, t0:, :], og[:, t0:, :], ACT.Square).then_inc(sqd, 1)
                nc.scalar.activation(TM[:, t0:, 768:1024], TM[:, t0:, 768:1024], ACT.Sigmoid).then_inc(gates, 1)
                nc.scalar.activation(TM[:, t0:, 256:512], TM[:, t0:, 256:512], ACT.Silu).then_inc(gates, 1)
                act.wait_ge(var, 1)
                nc.scalar.activation(ms[:, t0:, :], ms[:, t0:, :], ACT.Sqrt).then_inc(sd, 1)

            @block.gpsimd
            def _(pool):
                pool.wait_ge(gates, 1)
                nc.gpsimd.tensor_tensor(om[:, t0:, :], om[:, t0:, :], TM[:, t0:, 768:1024], ALU.mult).then_inc(gm, 1)

            @block.vector
            def _(dve):
                step = Chain(dve, ch)
                dve.wait_ge(sqd, 1)
                step(nc.vector.tensor_reduce(ms[:, t0:, :], sq[:, t0:, :].rearrange("p n (h c) -> p n h c", c=HD), AX.X, ALU.add))
                nc.vector.tensor_scalar(ms[:, t0:, :], ms[:, t0:, :], 1.0 / HD, EPS, ALU.mult, ALU.add).then_inc(var, 1)
                dve.wait_ge(sd, 1)
                step(nc.vector.reciprocal(ms[:, t0:, :], ms[:, t0:, :]))
                dve.wait_ge(ld, 16)
                dve.wait_ge(gates, 2)
                for n in tiles:
                    o = og[:, n, :].rearrange("p (h c) -> p h c", c=HD)
                    step(nc.vector.tensor_tensor(o, o, bc(ms[:, n, :], HD), ALU.mult))
                    step(nc.vector.tensor_tensor(og[:, n, :], og[:, n, :], ng[:, :], ALU.mult))
                    nc.vector.tensor_tensor(og[:, n, :], og[:, n, :], TM[:, n, 256:512], ALU.mult).then_inc(gd, 1)
                for i, n in enumerate(tiles):
                    dve.wait_ge(tr, i + 1)
                    if i >= 2:
                        dve.wait_ge(st, 16 * (i - 1))
                    nc.vector.tensor_copy(turned[:, i % 2, :, :].rearrange("p k t -> p (k t)"),
                                          ps[:, 2 * (i % 2):2 * (i % 2) + 2, :].rearrange("p b t -> p (b t)")[:, 0:6 * P]).then_inc(ev, 1)

            @block.tensor
            def _(pe):
                pe.wait_ge(gm, 1)
                for i, n in enumerate(tiles):
                    pe.wait_ge(gd, i + 1)
                    if i >= 2:
                        pe.wait_ge(ev, i - 1)
                    for k in range(6):
                        src = (og, om)[k // 2][:, n, (k % 2) * P:(k % 2 + 1) * P] if k < 4 else TM[:, n, 1024 + (k - 4) * P:1024 + (k - 3) * P]
                        x = nc.tensor.transpose(ps[:, 2 * (i % 2) + k // 4, (k % 4) * P:(k % 4 + 1) * P], src, ident)
                    x.then_inc(tr, 1)


def phase_out_proj(nc, io, S, l, groups):
    with Phase(nc, f"op{l}") as ph:
        xT = ph.sb("xT", [P, KD, T])
        mh = ph.sb("mix_hi", [P, KD, T], F32R)
        mT = ph.sb("mix", [P, KD, T])
        ml = mT[:, :, :].bitcast(F32R)
        w = ph.sb("w", [P, KD, D])
        wp = ph.sb("w_parts", [P, 2, 2, KD, P], F32R)
        w_ld, x_ld = ph.sem("w_loaded"), ph.sem("x_loaded")
        m_ld = [ph.sem(f"mix_loaded{g}") for g in range(len(groups))]
        mh_ready, ml_ready, wh_ready, wlo_ready, mm_done, done, st = (
            ph.sem(n) for n in ("mix_hi_ready", "mix_lo_ready", "w_hi_ready", "w_lo_ready", "mm_done", "added", "stored"))
        ps, mod = S["ps"], S["mod"]
        a, G = groups[0][0], len(groups)
        with nc.Block() as block:

            @block.sync
            def _(sp):
                sp.dma_start(w[:, :, :], io["w_out"][l].rearrange("(k p) n -> p k n", p=P)).then_inc(w_ld, 16)
                for g, (t0, n) in enumerate(groups):
                    sp.dma_start(mT[:, :, t0:t0 + n], S["mixT_d"][:, :, t0:t0 + n]).then_inc(m_ld[g], 16)
                sp.dma_start(xT[:, :, a:], S["xT_d"][:, :, a:]).then_inc(x_ld, 16)
                for d in range(KD):
                    sp.wait_ge(done, (d + 1) * G)
                    sp.dma_start(S["xT_d"][:, d, a:], xT[:, d, a:]).then_inc(st, 16)
                sp.wait_ge(st, 16 * KD)

            @block.tensor
            def _(pe):
                for d in range(KD):
                    pe.wait_ge(wlo_ready, d + 1)
                    for g, (t0, n) in enumerate(groups):
                        u = d * G + g
                        if d == 0:
                            pe.wait_ge(ml_ready, g + 1)
                        if u >= 8:
                            pe.wait_ge(done, u - 7)
                        for k in range(KD):
                            for q, (i, m) in enumerate(((0, mh), (1, mh), (0, ml))):
                                x = nc.tensor.matmul(ps[:, u % 8, :n], wp[:, d % 2, i, k, :], m[:, k, t0:t0 + n],
                                                     start=(k == 0 and q == 0), stop=(k == KD - 1 and q == 2))
                        x.then_inc(mm_done, 1)

            @block.scalar
            def _(act):
                def weights_hi(d):
                    if d >= 2:
                        act.wait_ge(mm_done, G * (d - 1))
                    nc.scalar.copy(wp[:, d % 2, 0, :, :], w[:, :, d * P:(d + 1) * P]).then_inc(wh_ready, 1)

                act.wait_ge(w_ld, 16)
                weights_hi(0)
                weights_hi(1)
                for g, (t0, n) in enumerate(groups):
                    act.wait_ge(m_ld[g], 16)
                    nc.scalar.copy(mh[:, :, t0:t0 + n], mT[:, :, t0:t0 + n]).then_inc(mh_ready, 1)
                for d in range(2, KD):
                    weights_hi(d)

            @block.vector
            def _(dve):
                def weights_lo(d):
                    dve.wait_ge(wh_ready, d + 1)
                    nc.vector.tensor_tensor(wp[:, d % 2, 1, :, :], w[:, :, d * P:(d + 1) * P],
                                            wp[:, d % 2, 0, :, :].bitcast(F32), ALU.subtract).then_inc(wlo_ready, 1)

                weights_lo(0)
                weights_lo(1)
                for g, (t0, n) in enumerate(groups):
                    dve.wait_ge(mh_ready, g + 1)
                    nc.vector.tensor_tensor(ml[:, :, t0:t0 + n], mT[:, :, t0:t0 + n], mh[:, :, t0:t0 + n].bitcast(F32),
                                            ALU.subtract).then_inc(ml_ready, 1)
                dve.wait_ge(x_ld, 16)
                for d in range(KD):
                    if 1 <= d < KD - 1:
                        weights_lo(d + 1)
                    for g, (t0, n) in enumerate(groups):
                        dve.wait_ge(mm_done, d * G + g + 1)
                        j = 1 if t0 < CTX else 0
                        nc.vector.scalar_tensor_tensor(out=xT[:, d, t0:t0 + n], in0=ps[:, (d * G + g) % 8, :n], scalar=mod[:, l, 16 + d, j:j + 1],
                                                       in1=xT[:, d, t0:t0 + n], op0=ALU.mult, op1=ALU.add).then_inc(done, 1)


def phase_norm_split(nc, S, name, xT, hh, hl, l, which, groups):
    with Phase(nc, name) as ph:
        sq = ph.sb("sq", [P, 4, 512])
        rstd = ph.sb("rstd", [P, 2, 512])
        xl = [ph.sem(f"x_loaded{g}") for g in range(len(groups))]
        sq_ready, sq_used, var_ready, sd_ready, scaled, hi_ready, lo_ready, rst = (
            ph.sem(n) for n in ("sq_ready", "sq_used", "var_ready", "sd_ready", "scaled", "hi_ready", "lo_ready", "rstd_ready"))
        ps, ones = S["ps"], S["c"]("ones")
        gmod, mod = S["gmod"], S["mod"]
        with nc.Block() as block:

            @block.sync
            def _(sp):
                for g, (t0, n) in enumerate(groups):
                    sp.dma_start(xT[:, :, t0:t0 + n], S["xT_d"][:, :, t0:t0 + n]).then_inc(xl[g], 16)

            @block.scalar
            def _(act):
                def squares(g, t0, n):
                    act.wait_ge(xl[g], 16)
                    for k in range(KD):
                        q = g * KD + k
                        if q >= 4:
                            act.wait_ge(sq_used, q - 3)
                        nc.scalar.activation(sq[:, q % 4, :n], xT[:, k, t0:t0 + n], ACT.Square).then_inc(sq_ready, 1)

                squares(0, *groups[0])
                for g, (t0, n) in enumerate(groups):
                    if g + 1 < len(groups):
                        squares(g + 1, *groups[g + 1])
                    act.wait_ge(var_ready, g + 1)
                    nc.scalar.activation(rstd[:, g % 2, :n], rstd[:, g % 2, :n], ACT.Sqrt).then_inc(sd_ready, 1)
                    j = 1 if t0 < CTX else 0
                    for k in range(KD):
                        act.wait_ge(scaled, g * KD + k + 1)
                        nc.scalar.activation(hh[:, k, t0:t0 + n], xT[:, k, t0:t0 + n], ACT.Identity,
                                             bias=mod[:, l, 24 * which + k, j:j + 1]).then_inc(hi_ready, 1)

            @block.tensor
            def _(pe):
                for g, (t0, n) in enumerate(groups):
                    for k in range(KD):
                        q = g * KD + k
                        pe.wait_ge(sq_ready, q + 1)
                        nc.tensor.matmul(ps[:, g, :n], ones, sq[:, q % 4, :n], start=(k == 0), stop=(k == KD - 1)).then_inc(sq_used, 1)

            @block.vector
            def _(dve):
                for g, (t0, n) in enumerate(groups):
                    j = 1 if t0 < CTX else 0
                    dve.wait_ge(sq_used, (g + 1) * KD)
                    if g >= 2:
                        dve.wait_ge(scaled, KD * (g - 1))
                    nc.vector.tensor_scalar(rstd[:, g % 2, :n], ps[:, g, :n], 1.0 / D, EPS, ALU.mult, ALU.add).then_inc(var_ready, 1)
                    dve.wait_ge(sd_ready, g + 1)
                    nc.vector.reciprocal(rstd[:, g % 2, :n], rstd[:, g % 2, :n]).then_inc(rst, 1)
                    dve.wait_ge(rst, g + 1)
                    for k in range(KD):
                        nc.vector.scalar_tensor_tensor(
                            out=xT[:, k, t0:t0 + n], in0=xT[:, k, t0:t0 + n], scalar=gmod[:, l, which, j, k:k + 1],
                            in1=rstd[:, g % 2, :n], op0=ALU.mult, op1=ALU.mult).then_inc(scaled, 1)
                    for k in range(KD):
                        dve.wait_ge(hi_ready, g * KD + k + 1)
                        dve.wait_ge(scaled, g * KD + k + 1)
                        nc.vector.scalar_tensor_tensor(
                            out=hl[:, k, t0:t0 + n], in0=xT[:, k, t0:t0 + n], scalar=mod[:, l, 24 * which + k, j:j + 1],
                            in1=hh[:, k, t0:t0 + n].bitcast(F32), op0=ALU.add, op1=ALU.subtract).then_inc(lo_ready, 1)
                dve.wait_ge(lo_ready, KD * len(groups))


def phase_ffn_up(nc, io, S, hh, hl):
    NC = DFF // P
    with Phase(nc, "up") as ph:
        wst = ph.sb("wst", [P, 2, 2, KD, P])
        wh = ph.sb("wh", [P, 2, 2, KD, P], F32R)
        wlo = ph.sb("wl", [P, 2, 2, KD, P], F32R)
        sil = ph.sb("sil", [P, 3, 512])
        a = ph.sb("a", [P, 2, T])
        wl = [ph.sem(f"w_loaded{s}") for s in range(2)]
        st = [ph.sem(f"a_stored{s}") for s in range(2)]
        hi, split, wused, g_done, u_done, silu_ready, used = (ph.sem(n) for n in (
            "w_hi", "w_split", "w_used", "gate_done", "up_done", "silu_ready", "banks_free"))
        ps = S["ps"]
        srcs = [io[n][0].rearrange("(k p) n -> p k n", p=P) for n in ("ffn_w_gate", "ffn_w_up")]
        with nc.Block() as block:

            @block.sync
            def _(sp):
                with sp.Fori(0, NC // 2) as i:
                    for s in range(2):
                        sp.wait_ge(split, i * 2 + (s + 1))
                        for kind in range(2):
                            sp.dma_start(wst[:, s, kind, :, :], srcs[kind][:, :, bass.ds(i * 256 + s * P, P)]).then_inc(wl[s], 16)

            @block.tensor
            def _(pe):
                pe.sem_inc(wused, 2)
                with pe.Fori(0, NC // 2) as i:
                    for s in range(2):
                        pe.wait_ge(split, i * 2 + (s + 3))
                        for g, (t0, n) in enumerate(GROUPS):
                            pe.wait_ge(used, i * 6 + (3 * s + g + 1))
                            for kind, done in ((0, g_done), (1, u_done)):
                                for k in range(KD):
                                    for j, (w, h) in enumerate(((wh, hh), (wh, hl), (wlo, hh))):
                                        x = nc.tensor.matmul(ps[:, 2 * g + kind, :n], w[:, s, kind, k, :], h[:, k, t0:t0 + n],
                                                             start=(k == 0 and j == 0), stop=(k == KD - 1 and j == 2))
                                x.then_inc(done, 1)
                        pe.wait_ge(u_done, i * 6 + 3 * (s + 1))
                        pe.sem_inc(wused, 1)

            @block.scalar
            def _(act):
                for s in range(2):
                    act.sem_inc(st[s], 16)

                def weights_hi(i, s):
                    act.wait_ge(wl[s], i * 32 + 32)
                    act.wait_ge(wused, i * 2 + (s + 1))
                    nc.scalar.copy(wh[:, s, :, :, :], wst[:, s, :, :, :]).then_inc(hi, 1)

                def store(i, s):
                    act.wait_ge(used, i * 6 + (3 * s + 6))
                    act.dma_start(S["a_d"][:, bass.ds(i * 2 + s, 1), :].rearrange("p a t -> p (a t)"), a[:, s, :]).then_inc(st[s], 16)

                def chunks(i, last):
                    for s in range(2):
                        if not (last and s == 1):
                            weights_hi(i + s, 1 - s)
                        for g, (t0, n) in enumerate(GROUPS):
                            act.wait_ge(g_done, i * 6 + (3 * s + g + 1))
                            act.wait_ge(used, i * 6 + (3 * s + g + 1))
                            nc.scalar.activation(sil[:, g, :n], ps[:, 2 * g, :n], ACT.Silu).then_inc(silu_ready, 1)
                        store(i, s)

                weights_hi(0, 0)
                with act.Fori(0, NC // 2 - 1) as i:
                    chunks(i, False)
                chunks(NC // 2 - 1, True)
                for s in range(2):
                    act.wait_ge(st[s], 16 * (NC // 2 + 1))

            @block.vector
            def _(dve):
                dve.sem_inc(used, 3)
                dve.sem_inc(split, 2)

                def weights_lo(i, s):
                    dve.wait_ge(hi, i * 2 + (s + 1))
                    nc.vector.tensor_tensor(wlo[:, s, :, :, :].rearrange("p a k n -> p (a k n)"), wst[:, s, :, :, :].rearrange("p a k n -> p (a k n)"),
                                            wh[:, s, :, :, :].rearrange("p a k n -> p (a k n)").bitcast(F32), ALU.subtract).then_inc(split, 1)

                def chunks(i, last):
                    for s in range(2):
                        if not (last and s == 1):
                            weights_lo(i + s, 1 - s)
                        dve.wait_ge(st[s], i * 16 + 16)
                        for g, (t0, n) in enumerate(GROUPS):
                            dve.wait_ge(silu_ready, i * 6 + (3 * s + g + 1))
                            dve.wait_ge(u_done, i * 6 + (3 * s + g + 1))
                            nc.vector.tensor_tensor(a[:, s, t0:t0 + n], sil[:, g, :n], ps[:, 2 * g + 1, :n], ALU.mult).then_inc(used, 1)

                weights_lo(0, 0)
                with dve.Fori(0, NC // 2 - 1) as i:
                    chunks(i, False)
                chunks(NC // 2 - 1, True)


def phase_ffn_down(nc, io, S):
    NC = DFF // P
    with Phase(nc, "down") as ph:
        wst = ph.sb("wst", [P, 2, D])
        wh = ph.sb("wh", [P, 2, D], F32R)
        wlo = ph.sb("wl", [P, 2, D], F32R)
        ast = ph.sb("ast", [P, 2, 512])
        ah = ph.sb("ah", [P, 2, 512], F32R)
        alo = ph.sb("al", [P, 2, 512], F32R)
        x = ph.sb("x", [P, KD, T])
        wl = [ph.sem(f"loaded{s}") for s in range(2)]
        hi, split, used, added, xl, st = (ph.sem(n) for n in ("hi_ready", "split", "used", "added", "x_loaded", "stored"))
        ps, mod = S["ps"], S["mod"]

        def over_chunks(eng, chunk, g):
            for s in range(2):
                chunk(0, s, g, s == 0, False)
            with eng.Fori(1, NC // 2 - 1) as i:
                for s in range(2):
                    chunk(i, s, g, False, False)
            for s in range(2):
                chunk(NC // 2 - 1, s, g, False, s == 1)

        with nc.Block() as block:

            @block.sync
            def _(sp):
                sp.dma_start(x[:, :, :], S["xT_d"]).then_inc(xl, 16)

                def load(i, s, g, first, last):
                    t0, n = GROUPS[g]
                    sp.wait_ge(split, i * 2 + (g * NC + s + 1))
                    sp.dma_start(wst[:, s, :], io["ffn_w_down"][0][bass.ds(i * 256 + s * P, P), :]).then_inc(wl[s], 16)
                    sp.dma_start(ast[:, s, :n], S["a_d"][:, bass.ds(i * 2 + s, 1), t0:t0 + n].rearrange("p a t -> p (a t)")).then_inc(wl[s], 16)

                for g in range(3):
                    over_chunks(sp, load, g)

            @block.tensor
            def _(pe):
                pe.sem_inc(used, 2)

                def products(i, s, g, first, last):
                    n = GROUPS[g][1]
                    pe.wait_ge(split, i * 2 + (g * NC + s + 3))
                    for d in range(KD):
                        if first and g:
                            pe.wait_ge(added, KD * (g - 1) + d + 1)
                        for j, (w, aa) in enumerate(((wh, ah), (wh, alo), (wlo, ah))):
                            mm = nc.tensor.matmul(ps[:, d, :n], w[:, s, d * P:(d + 1) * P], aa[:, s, :n],
                                                  start=(first and j == 0), stop=(last and j == 2))
                    mm.then_inc(used, 1)

                for g in range(3):
                    over_chunks(pe, products, g)

            @block.scalar
            def _(act):

                def parts_hi(i, s, g, first, last):
                    n = GROUPS[g][1]
                    act.wait_ge(wl[s], i * 32 + (16 * g * NC + 32))
                    act.wait_ge(used, i * 2 + (g * NC + s + 1))
                    nc.scalar.copy(wh[:, s, :], wst[:, s, :])
                    nc.scalar.copy(ah[:, s, :n], ast[:, s, :n]).then_inc(hi, 1)

                for g in range(3):
                    over_chunks(act, parts_hi, g)
                for g, (t0, n) in enumerate(GROUPS):
                    act.wait_ge(added, KD * (g + 1))
                    act.dma_start(S["xT_d"][:, :, t0:t0 + n], x[:, :, t0:t0 + n]).then_inc(st, 16)
                act.wait_ge(st, 48)

            @block.vector
            def _(dve):
                dve.sem_inc(split, 2)

                def parts_lo(i, s, g, first, last):
                    n = GROUPS[g][1]
                    dve.wait_ge(hi, i * 2 + (g * NC + s + 1))
                    nc.vector.tensor_tensor(wlo[:, s, :], wst[:, s, :], wh[:, s, :].bitcast(F32), ALU.subtract)
                    nc.vector.tensor_tensor(alo[:, s, :n], ast[:, s, :n], ah[:, s, :n].bitcast(F32), ALU.subtract).then_inc(split, 1)

                for g, (t0, n) in enumerate(GROUPS):
                    over_chunks(dve, parts_lo, g)
                    dve.wait_ge(used, NC * (g + 1) + 2)
                    dve.wait_ge(xl, 16)
                    j = 1 if t0 < CTX else 0
                    for d in range(KD):
                        nc.vector.scalar_tensor_tensor(out=x[:, d, t0:t0 + n], in0=ps[:, d, :n], scalar=mod[:, 0, 40 + d, j:j + 1],
                                                       in1=x[:, d, t0:t0 + n], op0=ALU.mult, op1=ALU.add).then_inc(added, 1)


def phase_route(nc, io, S, hT, R):
    NX = SEQ // P
    with Phase(nc, "route") as ph:
        wr = ph.sb("wr", [P, KD, NE])
        L = ph.sb("L", [P, NX, NE])
        sel = ph.sb("sel", [P, 2, NX, NE])
        both = ph.sb("both", [P, NX, NE])
        t = ph.sb("t", [P, NX, NE])
        m = ph.sb("m", [P, 2, NX])
        r = ph.sb("r", [P, NX])
        cnt = ph.sb("cnt", [P, NE])
        ind = ph.sb("ind", [P, NE, NE])
        nb = ph.sb("nb", [P, NE])
        end = ph.sb("end", [P, NE])
        start = ph.sb("start", [P, NE])
        indb = ph.sb("indb", [P, NUNIT, NE])
        indc = ph.sb("indc", [P, NUNIT, NE])
        ebf = ph.sb("ebf", [P, NUNIT])
        slotf = ph.sb("slotf", [P, 2, NX])
        ex = ph.sb("ex", [P, NX])
        rows = ph.sb("rows", [P, 2, D])
        zero = ph.sb("zero", [P, D])
        wl, zr, zf, lg, ch, sel_ready, pre, dif, exr, slots, tr, rv, g2s = (ph.sem(n) for n in (
            "router_loaded", "zero_ready", "slots_zeroed", "logits_done", "dve_step", "choice_ready", "ranks_done", "gap_ready", "exp_ready",
            "slots_ready", "rows_transposed", "rows_ready", "g2_stored"))
        sc = [ph.sem(f"scattered{s}") for s in range(2)]
        ps, c = S["ps"], S["c"]
        with nc.Block() as block:

            @block.sync
            def _(sp):
                sp.dma_start(wr[:, :, :], io["moe_router"][0].rearrange("(k p) e -> p k e", p=P)).then_inc(wl, 16)
                sp.wait_ge(zr, 1)
                sp.dma_start(S["xs_d"].rearrange("(b p) d -> p b d", p=P), zero[:, :].unsqueeze(1).to_broadcast([P, 2 * (NUNIT + 1), D])).then_inc(zf, 16)
                with nc.allow_non_contiguous_dma(reason="a column set as a vector"):
                    sp.dma_start(cols(S["g2_d"]), S["mod"][:, 1, 40:48, 0]).then_inc(g2s, 16)
                sp.wait_ge(g2s, 16)

            @block.tensor
            def _(pe):
                pe.wait_ge(wl, 16)
                for n in range(NX):
                    for k in range(KD):
                        x = nc.tensor.matmul(ps[:, 0, n * NE:(n + 1) * NE], hT[:, k, CTX + n * P:CTX + (n + 1) * P], wr[:, k, :],
                                             start=(k == 0), stop=(k == KD - 1))
                x.then_inc(lg, 1)
                pe.wait_ge(sel_ready, 1)
                for n in range(NX):
                    for i in range(n + 1):
                        nc.tensor.matmul(ps[:, 1, n * NE:(n + 1) * NE], c("tri") if i == n else c("ones"), both[:, i, :], start=(i == 0), stop=(i == n))
                for i in range(NX):
                    x = nc.tensor.matmul(ps[:, 2, 0:NE], c("ones"), both[:, i, :], start=(i == 0), stop=(i == NX - 1))
                x.then_inc(pre, 1)
                for n in range(NX):
                    if n >= 2:
                        pe.wait_ge(rv, n - 1)
                    for k in range(KD):
                        b = 4 + 2 * (n % 2) + k // 4
                        x = nc.tensor.transpose(ps[:, b, (k % 4) * P:(k % 4 + 1) * P], hT[:, k, CTX + n * P:CTX + (n + 1) * P], c("ident"))
                    x.then_inc(tr, 1)

            @block.vector
            def _(dve):
                step = Chain(dve, ch)
                pref = c("pref").unsqueeze(1).to_broadcast([P, NX, NE])
                dve.wait_ge(lg, 1)
                step(nc.vector.tensor_copy(L[:, :, :], ps[:, 0, 0:NX * NE].rearrange("p (n e) -> p n e", e=NE)))
                for i in range(2):
                    step(nc.vector.tensor_reduce(m[:, i, :], L[:, :, :], AX.X, ALU.max))
                    step(nc.vector.tensor_tensor(t[:, :, :], L[:, :, :], bc(m[:, i, :], NE), ALU.is_equal))
                    step(nc.vector.tensor_tensor(t[:, :, :], t[:, :, :], pref, ALU.mult))
                    step(nc.vector.tensor_reduce(r[:, :], t[:, :, :], AX.X, ALU.max))
                    step(nc.vector.tensor_tensor(sel[:, i, :, :], pref, bc(r[:, :], NE), ALU.is_equal))
                    if i == 0:
                        step(nc.vector.scalar_tensor_tensor(out=L[:, :, :], in0=sel[:, 0, :, :], scalar=-BIG, in1=L[:, :, :], op0=ALU.mult, op1=ALU.add))
                nc.vector.tensor_tensor(both[:, :, :], sel[:, 0, :, :], sel[:, 1, :, :], ALU.add).then_inc(sel_ready, 1)
                nc.vector.tensor_tensor(ex[:, :], m[:, 1, :], m[:, 0, :], ALU.subtract).then_inc(dif, 1)
                dve.wait_ge(exr, 1)
                step(nc.vector.tensor_scalar(r[:, :], ex[:, :], 1.0, None, ALU.add))
                step(nc.vector.reciprocal(R["gate"][:, 0, :], r[:, :]))
                step(nc.vector.tensor_tensor(R["gate"][:, 1, :], R["gate"][:, 0, :], ex[:, :], ALU.mult))
                dve.wait_ge(pre, 1)
                step(nc.vector.tensor_copy(cnt[:, :], ps[:, 2, 0:NE]))
                step(nc.vector.tensor_tensor(ind[:, :, :], bc(cnt[:, :], NE), c("koff").unsqueeze(1).to_broadcast([P, NE, NE]), ALU.is_gt))
                step(nc.vector.tensor_reduce(nb[:, :], ind[:, :, :], AX.X, ALU.add))
                step(nc.vector.tensor_tensor_scan(end[:, :], c("ones")[:, 0:NE], nb[:, :], 0.0, ALU.mult, ALU.add))
                step(nc.vector.tensor_tensor(start[:, :], end[:, :], nb[:, :], ALU.subtract))
                step(nc.vector.tensor_scalar(start[:, :], start[:, :], float(UNIT), None, ALU.mult))
                step(nc.vector.tensor_tensor(t[:, :, :], ps[:, 1, 0:NX * NE].rearrange("p (n e) -> p n e", e=NE),
                                             start[:, :].unsqueeze(1).to_broadcast([P, NX, NE]), ALU.add))
                for i in range(2):
                    step(nc.vector.tensor_tensor(sel[:, i, :, :], sel[:, i, :, :], t[:, :, :], ALU.mult))
                    step(nc.vector.tensor_reduce(slotf[:, i, :], sel[:, i, :, :], AX.X, ALU.add))
                step(nc.vector.tensor_tensor(indb[:, :, :], bc(c("blk"), NE), end[:, :].unsqueeze(1).to_broadcast([P, NUNIT, NE]), ALU.is_ge))
                step(nc.vector.tensor_reduce(ebf[:, :], indb[:, :, :], AX.X, ALU.add))
                step(nc.vector.tensor_scalar(ebf[:, :], ebf[:, :], float(NE - 1), None, ALU.min))
                step(nc.vector.tensor_copy(R["expert"][:, :], ebf[:, :]))
                step(nc.vector.tensor_tensor(cnt[:, :], cnt[:, :], start[:, :], ALU.add))
                step(nc.vector.tensor_tensor(indb[:, :, :], bc(c("half"), NE), cnt[:, :].unsqueeze(1).to_broadcast([P, NUNIT, NE]), ALU.is_lt))
                step(nc.vector.tensor_tensor(indc[:, :, :], bc(c("half"), NE), start[:, :].unsqueeze(1).to_broadcast([P, NUNIT, NE]), ALU.is_gt))
                step(nc.vector.tensor_tensor(indb[:, :, :], indb[:, :, :], indc[:, :, :], ALU.mult))
                step(nc.vector.tensor_reduce(ebf[:, :], indb[:, :, :], AX.X, ALU.max))
                step(nc.vector.tensor_copy(R["second"][:, :], ebf[:, :]))
                nc.vector.tensor_copy(R["slot"][:, :, :], slotf[:, :, :]).then_inc(slots, 1)
                for n in range(NX):
                    dve.wait_ge(tr, n + 1)
                    if n >= 2:
                        dve.wait_ge(sc[n % 2], 32 * (n // 2))
                    nc.vector.tensor_copy(rows[:, n % 2, :], ps[:, 4 + 2 * (n % 2):6 + 2 * (n % 2), :].rearrange("p b t -> p (b t)")).then_inc(rv, 1)

            @block.scalar
            def _(act):
                act.wait_ge(dif, 1)
                nc.scalar.activation(ex[:, :], ex[:, :], ACT.Exp).then_inc(exr, 1)

            @block.gpsimd
            def _(pool):
                nc.gpsimd.memset(zero[:, :], 0.0).then_inc(zr, 1)
                pool.wait_ge(zf, 16)
                pool.wait_ge(slots, 1)
                for n in range(NX):
                    pool.wait_ge(rv, n + 1)
                    for i in range(2):
                        nc.gpsimd.indirect_dma_start(
                            out=S["xs_d"][:, :], out_offset=bass.IndirectOffsetOnAxis(ap=R["slot"][:, i, n:n + 1], axis=0),
                            in_=rows[:, n % 2, :], in_offset=None).then_inc(sc[n % 2], 16)
                for s in range(2):
                    pool.wait_ge(sc[s], 32 * (NX // 2))


def phase_experts(nc, io, S, R):
    W = 2 * P
    NP = DFE // W
    with Phase(nc, "moe") as ph:
        wst = ph.sb("wst", [P, 2, 3, KD * W])
        wh = ph.sb("wh", [P, 2, 3, KD * W], F32R)
        wlo = ph.sb("wl", [P, 2, 3, KD * W], F32R)
        rows = ph.sb("rows", [P, 2, D])
        xh = ph.sb("xh", [P, KD, 2 * P], F32R)
        xl = ph.sb("xl", [P, KD, 2 * P], F32R)
        sil = ph.sb("sil", [P, 2 * W])
        a = ph.sb("a", [P, 2, 2, P])
        ah = ph.sb("ah", [P, 2, 2, P], F32R)
        al = ph.sb("al", [P, 2, 2, P], F32R)
        y = ph.sb("y", [P, 2, D])
        KINDS = ("gate", "up", "down")
        wl = [[ph.sem(f"{k}_loaded{s}") for k in KINDS] for s in range(2)]
        hi = [ph.sem(f"{k}_hi") for k in KINDS]
        split = [ph.sem(f"{k}_split") for k in KINDS]
        done = [ph.sem(f"{k}_done") for k in KINDS]
        silu, prod, tr, ahr, alr, rl, xtr, xhr, xlr, yev, yst, yfree = (ph.sem(n) for n in (
            "silu_ready", "product_ready", "product_turned", "product_hi", "product_split",
            "rows_loaded", "rows_turned", "rows_hi", "rows_split", "y_read", "y_stored", "y_free"))
        ps, ident = S["ps"], S["c"]("ident")
        Y0 = 4
        src = (io["moe_w_gate"][0], io["moe_w_up"][0], io["moe_w_down"][0])
        xs_b = S["xs_d"].rearrange("(b i p) d -> b i p d", p=P, i=2)
        ys_b = S["ys_d"].rearrange("(b i p) d -> b i p d", p=P, i=2)

        def weights(w, kind, p):
            return w[:, p % 2, kind, :].rearrange("p (k n) -> p k n", k=2 if kind == 2 else KD)

        def turn_bank(s):
            return (0, 2, 1, 3)[s], s // 2, s % 2

        with nc.Block() as block:

            @block.sync
            def _(sp):
                with sp.Fori(0, NUNIT) as b:
                    e = sp.value_load(R["expert"][0:1, bass.ds(b, 1)], min_val=0, max_val=NE - 1)
                    for p in range(NP):
                        for kind in range(3):
                            sp.wait_ge(split[kind], b * NP + (p + 1))
                            if kind == 2:
                                w = src[2][bass.ds(e, 1), W * p:W * (p + 1), :].rearrange("a (c p) n -> p (a c) n", p=P)
                            else:
                                w = src[kind][bass.ds(e, 1), :, W * p:W * (p + 1)].rearrange("a (k p) n -> p (a k) n", p=P)
                            sp.dma_start(weights(wst, kind, p), w).then_inc(wl[p % 2][kind], 16)

            @block.gpsimd
            def _(pool):
                pool.sem_inc(yfree, 1)
                pool.dma_start(rows[:, :, :], xs_b[0].rearrange("i p d -> p i d")).then_inc(rl, 16)
                with pool.Fori(0, NUNIT) as b:
                    pool.wait_ge(xtr, b * 4 + 4)
                    pool.dma_start(rows[:, :, :], xs_b[bass.ds(b + 1, 1)].rearrange("a i p d -> p (a i) d")).then_inc(rl, 16)
                    pool.wait_ge(yev, b + 2)
                    pool.dma_start(ys_b[bass.ds(b, 1)].rearrange("a i p d -> p (a i) d"), y[:, :, :]).then_inc(yst, 16)
                    pool.wait_ge(yst, b * 16 + 16)
                    pool.sem_inc(yfree, 1)
                pool.wait_ge(rl, 16 * (NUNIT + 1))

            @block.tensor
            def _(pe):
                for kind in range(3):
                    pe.sem_inc(done[kind], 2)

                def turn_rows(s):
                    bank, i, kh = turn_bank(s)
                    for k in range(4):
                        x = nc.tensor.transpose(ps[:, bank, k * P:(k + 1) * P], rows[:, i, (4 * kh + k) * P:(4 * kh + k + 1) * P], ident)
                    x.then_inc(xtr, 1)

                pe.wait_ge(rl, 16)
                for s in range(4):
                    turn_rows(s)
                with pe.Fori(0, NUNIT) as b:
                    second = pe.value_load(R["second"][0:1, bass.ds(b, 1)], min_val=0, max_val=1)

                    def up(kind, p, tiles):
                        pe.wait_ge(split[kind], b * NP + (p + 3))
                        h, l = weights(wh, kind, p), weights(wlo, kind, p)
                        for i in range(tiles):
                            t = slice(i * P, (i + 1) * P)
                            for k in range(KD):
                                for j, (xx, w) in enumerate(((xh, h), (xh, l), (xl, h))):
                                    x = nc.tensor.matmul(ps[:, 2 * kind + p % 2, i * W:(i + 1) * W], xx[:, k, t], w[:, k, :],
                                                         start=(k == 0 and j == 0), stop=(k == KD - 1 and j == 2))
                        x.then_inc(done[kind], 1)

                    def turn_product(p, tiles):
                        pe.wait_ge(prod, b * NP + (p + 3))
                        for i in range(tiles):
                            for c in range(2):
                                x = nc.tensor.transpose(ps[:, 2 + p % 2, (2 * i + c) * P:(2 * i + c + 1) * P], a[:, i, c, :], ident)
                        x.then_inc(tr, 1)

                    def down(p, tiles):
                        pe.wait_ge(alr, b * NP + (p + 3))
                        pe.wait_ge(split[2], b * NP + (p + 3))
                        if p == 0:
                            pe.wait_ge(yev, b + 1)
                        h, l = weights(wh, 2, p), weights(wlo, 2, p)
                        for i in range(tiles):
                            for c in range(2):
                                for j, (aa, w) in enumerate(((ah, h), (ah, l), (al, h))):
                                    for half in range(2):
                                        x = nc.tensor.matmul(ps[:, Y0 + 2 * i + half, :], aa[:, i, c, :], w[:, c, half * 512:(half + 1) * 512],
                                                             start=(p == 0 and c == 0 and j == 0), stop=(p == NP - 1 and c == 1 and j == 2))
                        x.then_inc(done[2], 1)

                    def step(p, tiles):
                        if p < NP:
                            pe.wait_ge(silu, b * NP + (p + 1))
                            up(0, p, tiles)
                        if p >= 1:
                            turn_product(p - 1, tiles)
                        if p < NP:
                            pe.wait_ge(alr, b * NP + (p + 1))
                            up(1, p, tiles)
                        else:
                            pe.wait_ge(rl, b * 16 + 32)
                            pe.wait_ge(silu, b * NP + (NP + 1))
                            turn_rows(0)
                            pe.wait_ge(alr, b * NP + (NP + 1))
                            turn_rows(1)
                        if p >= 1:
                            down(p - 1, tiles)
                        if p == NP:
                            pe.wait_ge(silu, b * NP + (NP + 2))
                            turn_rows(2)
                            turn_rows(3)

                    pe.wait_ge(xlr, b * 4 + 4)
                    for p in range(NP + 1):
                        with pe.If(second):
                            step(p, 2)
                        with pe.Else():
                            step(p, 1)

            @block.scalar
            def _(act):
                act.sem_inc(silu, 2)

                def rows_hi(n0, s):
                    bank, i, kh = turn_bank(s)
                    act.wait_ge(xtr, n0 + (s + 1))
                    nc.scalar.copy(xh[:, 4 * kh:4 * kh + 4, i * P:(i + 1) * P], ps[:, bank, :].rearrange("p (k t) -> p k t", t=P)).then_inc(xhr, 1)

                for s in range(4):
                    rows_hi(0, s)
                with act.Fori(0, NUNIT) as b:

                    def weights_hi(kind, p):
                        if p < NP:
                            act.wait_ge(wl[p % 2][kind], b * (16 * (NP // 2)) + 16 * (p // 2 + 1))
                            act.wait_ge(done[kind], b * NP + (p + 1))
                            nc.scalar.copy(weights(wh, kind, p), weights(wst, kind, p)).then_inc(hi[kind], 1)

                    def product_hi(p):
                        act.wait_ge(tr, b * NP + (p + 1))
                        nc.scalar.copy(ah[:, :, :, :], ps[:, 2 + p % 2, :].rearrange("p (i c t) -> p i c t", i=2, c=2)).then_inc(ahr, 1)

                    for kind, p in ((0, 0), (1, 0), (0, 1), (2, 0), (1, 1)):
                        weights_hi(kind, p)
                    for p in range(NP):
                        act.wait_ge(done[0], b * NP + (p + 3))
                        act.wait_ge(prod, b * NP + (p + 2))
                        nc.scalar.activation(sil[:, :], ps[:, p % 2, :], ACT.Silu).then_inc(silu, 1)
                        weights_hi(0, p + 2)
                        if p >= 1:
                            product_hi(p - 1)
                        weights_hi(2, p + 1)
                        weights_hi(1, p + 2)
                    product_hi(NP - 1)
                    for s in range(4):
                        rows_hi(b * 4 + 4, s)

            @block.vector
            def _(dve):
                dve.sem_inc(prod, 2)
                dve.sem_inc(alr, 2)
                dve.sem_inc(yev, 1)
                for kind in range(3):
                    dve.sem_inc(split[kind], 2)

                def rows_lo(n0, s):
                    bank, i, kh = turn_bank(s)
                    dve.wait_ge(xhr, n0 + (s + 1))
                    o = (slice(None), slice(4 * kh, 4 * kh + 4), slice(i * P, (i + 1) * P))
                    nc.vector.tensor_tensor(xl[o], ps[:, bank, :].rearrange("p (k t) -> p k t", t=P), xh[o].bitcast(F32), ALU.subtract).then_inc(xlr, 1)

                for s in range(4):
                    rows_lo(0, s)
                with dve.Fori(0, NUNIT) as b:

                    def weights_lo(kind, p):
                        if p < NP:
                            dve.wait_ge(hi[kind], b * NP + (p + 1))
                            nc.vector.tensor_tensor(weights(wlo, kind, p), weights(wst, kind, p), weights(wh, kind, p).bitcast(F32),
                                                    ALU.subtract).then_inc(split[kind], 1)

                    def product_lo(p):
                        dve.wait_ge(ahr, b * NP + (p + 1))
                        nc.vector.tensor_tensor(al[:, :, :, :], ps[:, 2 + p % 2, :].rearrange("p (i c t) -> p i c t", i=2, c=2),
                                                ah[:, :, :, :].bitcast(F32), ALU.subtract).then_inc(alr, 1)

                    for kind, p in ((0, 0), (1, 0), (0, 1), (2, 0), (1, 1)):
                        weights_lo(kind, p)
                    for p in range(NP):
                        if p >= 1:
                            product_lo(p - 1)
                        dve.wait_ge(silu, b * NP + (p + 3))
                        dve.wait_ge(done[1], b * NP + (p + 3))
                        nc.vector.tensor_tensor(a[:, :, :, :].rearrange("p i c f -> p (i c f)"), sil[:, :], ps[:, 2 + p % 2, :], ALU.mult).then_inc(prod, 1)
                        weights_lo(0, p + 2)
                        weights_lo(2, p + 1)
                        weights_lo(1, p + 2)
                    product_lo(NP - 1)
                    for s in range(4):
                        rows_lo(b * 4 + 4, s)
                    dve.wait_ge(done[2], b * NP + (NP + 2))
                    dve.wait_ge(yfree, b + 1)
                    for i in range(2):
                        x = nc.vector.tensor_copy(y[:, i, :], ps[:, Y0 + 2 * i:Y0 + 2 * i + 2, :].rearrange("p b t -> p (b t)"))
                    x.then_inc(yev, 1)


def phase_final(nc, io, S, R):
    NX = SEQ // P
    with Phase(nc, "fin") as ph:
        xT = ph.sb("xT", [P, KD, SEQ])
        g2 = ph.sb("g2", [P, D])
        fg = ph.sb("fg", [P, D])
        y = ph.sb("y", [P, 2, 2, D])
        x = ph.sb("x", [P, 2, D])
        sq = ph.sb("sq", [P, D])
        ss = ph.sb("ss", [P, NX])
        ld, tr, ch, xr, va, sr, od = (ph.sem(n) for n in ("loaded", "transposed", "dve_step", "x_ready", "var_ready", "sd_ready", "out_ready"))
        gl = [ph.sem(f"gathered{s}") for s in range(2)]
        st = [ph.sem(f"stored{s}") for s in range(2)]
        ps, ident = S["ps"], S["c"]("ident")
        with nc.Block() as block:

            @block.sync
            def _(sp):
                sp.dma_start(xT[:, :, :], S["xT_d"][:, :, CTX:]).then_inc(ld, 16)
                sp.dma_start(g2[:, :], S["g2_d"].rearrange("(a n) -> a n", a=1).to_broadcast([P, D])).then_inc(ld, 16)
                sp.dma_start(fg[:, :], io["final_norm_g"].rearrange("(a n) -> a n", a=1).to_broadcast([P, D])).then_inc(ld, 16)
                for n in range(NX):
                    sp.wait_ge(od, n + 1)
                    sp.dma_start(io["out"][0, n * P:(n + 1) * P, :], x[:, n % 2, :]).then_inc(st[n % 2], 16)
                for s in range(2):
                    sp.wait_ge(st[s], 16 * (NX // 2))

            @block.gpsimd
            def _(pool):
                for n in range(NX):
                    if n >= 2:
                        pool.wait_ge(xr, n - 1)
                    for i in range(2):
                        nc.gpsimd.indirect_dma_start(
                            out=y[:, n % 2, i, :], out_offset=None, in_=S["ys_d"][:, :],
                            in_offset=bass.IndirectOffsetOnAxis(ap=R["slot"][:, i, n:n + 1], axis=0)).then_inc(gl[n % 2], 16)

            @block.tensor
            def _(pe):
                pe.wait_ge(ld, 48)
                for n in range(NX):
                    if n >= 2:
                        pe.wait_ge(xr, n - 1)
                    for k in range(KD):
                        t = nc.tensor.transpose(ps[:, 2 * (n % 2) + k // 4, (k % 4) * P:(k % 4 + 1) * P], xT[:, k, n * P:(n + 1) * P], ident)
                    t.then_inc(tr, 1)

            @block.scalar
            def _(act):
                for n in range(NX):
                    act.wait_ge(xr, n + 1)
                    if n >= 1:
                        act.wait_ge(va, n)
                    nc.scalar.activation(sq[:, :], x[:, n % 2, :], ACT.Square, accum_out=ss[:, n:n + 1]).then_inc(sr, 1)
                    act.wait_ge(va, n + 1)
                    nc.scalar.activation(ss[:, n:n + 1], ss[:, n:n + 1], ACT.Sqrt).then_inc(sr, 1)

            @block.vector
            def _(dve):
                step = Chain(dve, ch)
                dve.wait_ge(ld, 48)
                for n in range(NX):
                    s = n % 2
                    dve.wait_ge(gl[s], 32 * (n // 2 + 1))
                    if n >= 2:
                        dve.wait_ge(st[s], 16 * (n // 2))
                    step(nc.vector.tensor_scalar(y[:, s, 0, :], y[:, s, 0, :], R["gate"][:, 0, n:n + 1], None, ALU.mult))
                    step(nc.vector.scalar_tensor_tensor(out=y[:, s, 0, :], in0=y[:, s, 1, :], scalar=R["gate"][:, 1, n:n + 1],
                                                        in1=y[:, s, 0, :], op0=ALU.mult, op1=ALU.add))
                    step(nc.vector.tensor_tensor(y[:, s, 0, :], y[:, s, 0, :], g2[:, :], ALU.mult))
                    dve.wait_ge(tr, n + 1)
                    nc.vector.tensor_tensor(x[:, s, :], y[:, s, 0, :], ps[:, 2 * s:2 * s + 2, :].rearrange("p b t -> p (b t)"), ALU.add).then_inc(xr, 1)
                    dve.wait_ge(sr, 2 * n + 1)
                    nc.vector.tensor_scalar(ss[:, n:n + 1], ss[:, n:n + 1], 1.0 / D, EPS, ALU.mult, ALU.add).then_inc(va, 1)
                    dve.wait_ge(sr, 2 * n + 2)
                    step(nc.vector.reciprocal(ss[:, n:n + 1], ss[:, n:n + 1]))
                    nc.vector.scalar_tensor_tensor(out=x[:, s, :], in0=x[:, s, :], scalar=ss[:, n:n + 1], in1=fg[:, :],
                                                   op0=ALU.mult, op1=ALU.mult).then_inc(od, 1)


INPUTS = ["x", "c", "ctx", "c_ctx", "w_ada", "b_ada", "norm_mix_g", "norm_ffn_g", "w_in", "w_out", "gla_w_lr", "gla_b_lr",
          "gla_norm_g", "mlstm_conv", "mlstm_gate_b", "sgu_w", "sgu_b", "ffn_w_gate", "ffn_w_up", "ffn_w_down", "moe_router",
          "moe_w_gate", "moe_w_up", "moe_w_down", "final_norm_g", "cst", "dft_seq", "dft_ctx"]


def build(nc, io):
    S = {name: nc.dram_tensor(name, shape, F32, kind="Internal").ap() for name, shape in
         (("xT_d", (P, KD, T)), ("mixT_d", (P, KD, T)), ("xs_d", ((NUNIT + 1) * UNIT, D)), ("ys_d", (NUNIT * UNIT, D)), ("g2_d", (D,)), ("a_d", (P, DFF // P, T)))}
    with ExitStack() as top:
        def sb(stack, name, shape, dt=F32):
            return stack.enter_context(nc.sbuf_tensor(name, shape, dt))

        S["ps"] = top.enter_context(nc.psum_tensor("ps", [P, 8, 512], F32))
        S["cst"] = sb(top, "cst", [P, NCST])
        S["c"] = lambda name: S["cst"][:, CST[name][0]:CST[name][0] + CST[name][1]]
        S["mod"] = sb(top, "mod", [P, 2, 48, 2])
        S["gmod"] = sb(top, "gmod", [P, 2, 2, 2, KD])
        R = {"slot": sb(top, "slot", [P, 2, SEQ // P], I32), "gate": sb(top, "gate", [P, 2, SEQ // P]),
             "expert": sb(top, "expert", [P, NUNIT], I32), "second": sb(top, "second", [P, NUNIT], I32)}
        phase_modulation(nc, io, S)
        phase_to_features(nc, io, S)
        for l in range(2):
            ctx_out = l == 0
            groups = GROUPS if ctx_out else GROUPS[1:]
            with ExitStack() as lay:
                FM = sb(lay, f"FM{l}", [P, 9, T])
                TM = sb(lay, f"TM{l}", [P, NT, 1536])
                with ExitStack() as st:
                    hT = sb(st, f"hT{l}", [P, KD, T])
                    xT = TM[:, 0:7, :].rearrange("p a b -> p (a b)")[:, 0:KD * T].rearrange("p (k t) -> p k t", t=T)
                    phase_norm(nc, S, f"nm{l}", xT, hT, l, 0, GROUPS)
                    phase_project(nc, io, S, l, hT, FM, TM, ctx_out)
                phase_fourier(nc, io, S, l, FM, ctx_out)
                phase_sgu(nc, io, S, l, TM, ctx_out)
                M = {}
                M["qd"] = sb(lay, f"qd{l}", [P, 2, T])
                M["kd"] = sb(lay, f"kd{l}", [P, 2, T])
                M["em"] = sb(lay, f"em{l}", [P, 2, 3, NT])
                M["mx"] = sb(lay, f"mx{l}", [8, 2, T])
                M["ig"] = sb(lay, f"ig{l}", [8, T])
                M["tg"] = sb(lay, f"tg{l}", [P, NT, 2, 4, 8])
                M["dcol"] = sb(lay, f"dcol{l}", [P, 4, NT])
                phase_decays(nc, io, S, l, FM, M)
                M["vx"] = sb(lay, f"vx{l}", [P, NT, NH, 65])
                for name, ch in (("og", 2), ("om", 4)):
                    M[name] = FM[:, ch:ch + 2, :].rearrange("p a b -> p (a b)").rearrange("p (n c) -> p n c", c=256)
                phase_conv(nc, io, S, l, FM, TM, M)
                phase_scan(nc, io, S, l, FM, TM, M)
                phase_mix_out(nc, io, S, l, TM, M, ctx_out)
            phase_out_proj(nc, io, S, l, groups)
            with ExitStack() as lay:
                if l == 0:
                    hh = sb(lay, "hh", [P, KD, T], F32R)
                    hl = sb(lay, "hl", [P, KD, T], F32R)
                    with ExitStack() as st:
                        xT = sb(st, "xF0", [P, KD, T])
                        phase_norm_split(nc, S, "nf0", xT, hh, hl, l, 1, groups)
                    phase_ffn_up(nc, io, S, hh, hl)
                else:
                    hT = sb(lay, "hF1", [P, KD, T])
                    with ExitStack() as st:
                        xT = sb(st, "xF1", [P, KD, T])
                        phase_norm(nc, S, "nf1", xT, hT, l, 1, groups)
                    phase_route(nc, io, S, hT, R)
            if l == 0:
                phase_ffn_down(nc, io, S)
        phase_experts(nc, io, S, R)
        phase_final(nc, io, S, R)


def kernel(**inputs):
    import concourse.bacc as bacc
    from concourse.bass_utils import run_bass_kernel_spmd

    nc = bacc.Bacc("TRN2", target_bir_lowering=False, num_devices=1)
    shapes = {"cst": constants(), "dft_seq": dft(SEQ), "dft_ctx": dft(CTX)}
    arrays, io = {}, {}
    for name in INPUTS:
        a = shapes[name] if name in shapes else np.ascontiguousarray(inputs[name])
        arrays["in_" + name] = a
        io[name] = nc.dram_tensor("in_" + name, a.shape, mybir.dt.from_np(a.dtype), kind="ExternalInput").ap()
    io["out"] = nc.dram_tensor("out", (1, SEQ, D), F32, kind="ExternalOutput").ap()
    build(nc, io)
    r = run_bass_kernel_spmd(nc, [arrays], core_ids=[0])
    return r.results[0]["out"]
```
